# Optimizing a Trainium2 kernel written in Bass

```python
import math
import jax
import jax.numpy as jnp
from jax import lax
import numpy as np
import jax, jax.numpy as jnp

D_MODEL = 1024
BATCH = 1
SEQ = 256
DEPTH = 2

MIX_W = D_MODEL // 4
N_BRANCH = 4
CHUNK = 64
EPS = 1e-6
ROPE_BASE = 10000.0
CONV_K = 4

RET_HEADS = 4
RET_DK = MIX_W // RET_HEADS
RET_DV = MIX_W // RET_HEADS

SSD_HEADS = 4
SSD_P = MIX_W // SSD_HEADS
SSD_N = 128
SSD_GROUPS = 2
SSD_CONV_CH = MIX_W + 2 * SSD_GROUPS * SSD_N

GLA_HEADS = 4
GLA_DK = MIX_W // (2 * GLA_HEADS)
GLA_DV = MIX_W // GLA_HEADS
GLA_RANK = 16
GLA_TAU = 16.0

ML_HEADS = 4
ML_DK = MIX_W // ML_HEADS
ML_DV = MIX_W // ML_HEADS

D_FF = 2816
N_EXPERTS = 8
TOP_K = 2
EXPERT_FF = 2816

IN_SIZES = (
    MIX_W, MIX_W, MIX_W, MIX_W,
    MIX_W, SSD_CONV_CH, SSD_HEADS,
    GLA_HEADS * GLA_DK, GLA_HEADS * GLA_DK, MIX_W, MIX_W, GLA_RANK,
    2 * MIX_W, MIX_W, MIX_W, ML_HEADS, ML_HEADS,
    N_BRANCH * D_MODEL,
)
IN_COLS = sum(IN_SIZES)


def rmsnorm(x, g):
    xf = x.astype(jnp.float32)
    y = xf * lax.rsqrt(jnp.mean(xf * xf, axis=-1, keepdims=True) + EPS)
    return (y * g.astype(jnp.float32)).astype(x.dtype)

def head_rmsnorm(t, g):
    nh, d = t.shape[-2], t.shape[-1]
    return rmsnorm(t, g.reshape(nh, d))

def rotary(t, pos):
    half = t.shape[-1] // 2
    inv = ROPE_BASE ** (-jnp.arange(half, dtype=jnp.float32) / half)
    ang = pos.astype(jnp.float32)[:, None] * inv[None, :]
    cos = jnp.cos(ang)[None, :, None, :]
    sin = jnp.sin(ang)[None, :, None, :]
    t1 = t[..., :half].astype(jnp.float32)
    t2 = t[..., half:].astype(jnp.float32)
    return jnp.concatenate([t1 * cos - t2 * sin, t1 * sin + t2 * cos], axis=-1)

def causal_dwconv(u, w, b):
    ch = u.shape[-1]
    y = lax.conv_general_dilated(u, w[:, None, :].astype(u.dtype), window_strides=(1,),
                                 padding=[(CONV_K - 1, 0)],
                                 dimension_numbers=('NWC', 'WIO', 'NWC'),
                                 feature_group_count=ch)
    return y + b

def _chunk(t):
    t = t.astype(jnp.float32)
    bsz, seq, nh = t.shape[:3]
    t = t.reshape((bsz, seq // CHUNK, CHUNK, nh) + t.shape[3:])
    return jnp.moveaxis(t, (1, 3), (0, 2))

def _unchunk(t):
    t = jnp.moveaxis(t, (0, 2), (1, 3))
    return t.reshape((t.shape[0], t.shape[1] * t.shape[2]) + t.shape[3:])

def _tri():
    return jnp.tril(jnp.ones((CHUNK, CHUNK), dtype=bool))

def retention_scan(q, k, v, log_gamma):
    bsz, _, nh, dk = q.shape
    dv = v.shape[-1]
    idx = jnp.arange(CHUNK, dtype=jnp.float32)
    rel = idx[:, None] - idx[None, :]
    tri = rel >= 0
    decay = jnp.where(tri[None], jnp.exp(jnp.where(tri, rel, 0.0)[None] * log_gamma[:, None, None]), 0.0)
    q_decay = jnp.exp((idx + 1.0)[None, :] * log_gamma[:, None])
    k_decay = jnp.exp((CHUNK - 1.0 - idx)[None, :] * log_gamma[:, None])
    chunk_decay = jnp.exp(CHUNK * log_gamma)

    def step(state, inp):
        qc, kc, vc = inp
        s = jnp.einsum('bhid,bhjd->bhij', qc, kc) * decay
        o = (jnp.einsum('bhij,bhjv->bhiv', s, vc)
             + jnp.einsum('bhid,bhdv->bhiv', qc, state) * q_decay[:, :, None])
        state = (state * chunk_decay[:, None, None]
                 + jnp.einsum('bhjd,bhjv->bhdv', kc * k_decay[:, :, None], vc))
        return state, o

    s0 = jnp.zeros((bsz, nh, dk, dv), jnp.float32)
    _, o = lax.scan(step, s0, (_chunk(q), _chunk(k), _chunk(v)))
    return _unchunk(o)

def ssd_scan(x, dt, bmat, cmat, a):
    bsz, _, nh, p = x.shape
    n = bmat.shape[-1]
    tri = _tri()

    def step(state, inp):
        xc, dtc, bc, cc = inp
        acs = jnp.cumsum(dtc * a[None, :, None], axis=-1)
        seg = jnp.exp(jnp.where(tri, acs[..., :, None] - acs[..., None, :], -jnp.inf))
        scores = jnp.einsum('bhin,bhjn->bhij', cc, bc) * seg
        xdt = xc * dtc[..., None]
        y = (jnp.einsum('bhij,bhjp->bhip', scores, xdt)
             + jnp.einsum('bhin,bhpn->bhip', cc, state) * jnp.exp(acs)[..., None])
        w_end = jnp.exp(acs[..., -1:] - acs)
        state = (state * jnp.exp(acs[..., -1])[..., None, None]
                 + jnp.einsum('bhjp,bhjn->bhpn', xdt * w_end[..., None], bc))
        return state, y

    s0 = jnp.zeros((bsz, nh, p, n), jnp.float32)
    _, y = lax.scan(step, s0, (_chunk(x), _chunk(dt), _chunk(bmat), _chunk(cmat)))
    return _unchunk(y)

def gla_scan(q, k, v, log_alpha):
    bsz, _, nh, dk = q.shape
    dv = v.shape[-1]
    tri = _tri()

    def step(state, inp):
        qc, kc, vc, gc = inp
        g = jnp.cumsum(gc, axis=2)
        seg = jnp.exp(jnp.where(tri[:, :, None], g[:, :, :, None, :] - g[:, :, None, :, :], -jnp.inf))
        att = jnp.sum(qc[:, :, :, None, :] * kc[:, :, None, :, :] * seg, axis=-1)
        o = (jnp.einsum('bhij,bhjv->bhiv', att, vc)
             + jnp.einsum('bhid,bhdv->bhiv', qc * jnp.exp(g), state))
        g_end = g[:, :, -1:, :]
        state = (state * jnp.exp(g_end[:, :, 0, :])[..., None]
                 + jnp.einsum('bhjd,bhjv->bhdv', kc * jnp.exp(g_end - g), vc))
        return state, o

    s0 = jnp.zeros((bsz, nh, dk, dv), jnp.float32)
    _, o = lax.scan(step, s0, (_chunk(q), _chunk(k), _chunk(v), _chunk(log_alpha)))
    return _unchunk(o)

def mlstm_scan(q, k, v, i_pre, log_f):
    bsz, _, nh, dk = q.shape
    dv = v.shape[-1]
    tri = _tri()

    def step(carry, inp):
        c_st, n_st, m = carry
        qc, kc, vc, ic, fc = inp
        b = jnp.cumsum(fc, axis=-1)
        dlog = jnp.where(tri, b[..., :, None] - b[..., None, :] + ic[..., None, :], -jnp.inf)
        inter = b + m[..., None]
        m_t = jnp.maximum(inter, jnp.max(dlog, axis=-1))
        s = jnp.einsum('bhid,bhjd->bhij', qc, kc) * jnp.exp(dlog - m_t[..., None])
        inter_w = jnp.exp(inter - m_t)
        num = (jnp.einsum('bhij,bhjv->bhiv', s, vc)
               + jnp.einsum('bhid,bhdv->bhiv', qc, c_st) * inter_w[..., None])
        den = jnp.sum(s, axis=-1) + jnp.einsum('bhid,bhd->bhi', qc, n_st) * inter_w
        h = num / jnp.maximum(jnp.abs(den), jnp.exp(-m_t))[..., None]
        b_end = b[..., -1]
        w_log = b_end[..., None] - b + ic
        m_new = jnp.maximum(b_end + m, jnp.max(w_log, axis=-1))
        w = jnp.exp(w_log - m_new[..., None])
        carry_decay = jnp.exp(b_end + m - m_new)
        kw = kc * w[..., None]
        c_st = c_st * carry_decay[..., None, None] + jnp.einsum('bhjd,bhjv->bhdv', kw, vc)
        n_st = n_st * carry_decay[..., None] + jnp.sum(kw, axis=2)
        return (c_st, n_st, m_new), h

    init = (jnp.zeros((bsz, nh, dk, dv), jnp.float32),
            jnp.zeros((bsz, nh, dk), jnp.float32),
            jnp.zeros((bsz, nh), jnp.float32))
    _, h = lax.scan(step, init, (_chunk(q), _chunk(k), _chunk(v), _chunk(i_pre), _chunk(log_f)))
    return _unchunk(h)

def _split_cols(u):
    outs, start = [], 0
    for width in IN_SIZES:
        outs.append(u[..., start:start + width])
        start += width
    return outs

def token_mixers(h, pos, w_in, ret_norm_g, ssd_conv_w, ssd_conv_b, ssd_dt_bias, ssd_a_log, ssd_d,
                 ssd_norm_g, gla_w_alpha, gla_b_alpha, gla_norm_g, ml_conv_w, ml_conv_b, ml_b_i,
                 ml_b_f, ml_norm_g, w_branch, w_out):
    bsz, seq, _ = h.shape
    u = h @ w_in
    (rq, rk, rv, rg, sz, sxbc, sdt, gq, gk, gv, gr, ga,
     mqk, mv, mo, mi, mf, mgate) = _split_cols(u)

    def heads(t, nh):
        return t.reshape(bsz, seq, nh, -1)

    log_gamma = jnp.log1p(-jnp.exp2(-5.0 - jnp.arange(RET_HEADS, dtype=jnp.float32)))
    q = rotary(heads(rq, RET_HEADS), pos)
    k = rotary(heads(rk, RET_HEADS), pos) * (RET_DK ** -0.5)
    o = retention_scan(q, k, heads(rv, RET_HEADS), log_gamma)
    y_ret = (head_rmsnorm(o, ret_norm_g).reshape(bsz, seq, MIX_W) * jax.nn.silu(rg)).astype(h.dtype)

    xbc = jax.nn.silu(causal_dwconv(sxbc, ssd_conv_w, ssd_conv_b))
    sx = xbc[..., :MIX_W]
    sb = xbc[..., MIX_W:MIX_W + SSD_GROUPS * SSD_N].reshape(bsz, seq, SSD_GROUPS, SSD_N)
    sc = xbc[..., MIX_W + SSD_GROUPS * SSD_N:].reshape(bsz, seq, SSD_GROUPS, SSD_N)
    rep = SSD_HEADS // SSD_GROUPS
    bh = jnp.repeat(sb, rep, axis=2)
    ch = jnp.repeat(sc, rep, axis=2)
    dt = jax.nn.softplus(sdt.astype(jnp.float32) + ssd_dt_bias.astype(jnp.float32))
    a = -jnp.exp(ssd_a_log.astype(jnp.float32))
    xs = heads(sx, SSD_HEADS).astype(jnp.float32)
    y = ssd_scan(xs, dt, bh, ch, a) + ssd_d.astype(jnp.float32)[:, None] * xs
    y_ssd = rmsnorm(y.reshape(bsz, seq, MIX_W) * jax.nn.silu(sz), ssd_norm_g).astype(h.dtype)

    alpha_pre = (ga @ gla_w_alpha + gla_b_alpha).astype(jnp.float32)
    log_alpha = heads(jax.nn.log_sigmoid(alpha_pre) / GLA_TAU, GLA_HEADS)
    q = heads(gq, GLA_HEADS) * (GLA_DK ** -0.5)
    o = gla_scan(q, heads(gk, GLA_HEADS), heads(gv, GLA_HEADS), log_alpha)
    y_gla = (head_rmsnorm(o, gla_norm_g).reshape(bsz, seq, MIX_W) * jax.nn.silu(gr)).astype(h.dtype)

    qk = jax.nn.silu(causal_dwconv(mqk, ml_conv_w, ml_conv_b))
    q = heads(qk[..., :MIX_W], ML_HEADS)
    k = heads(qk[..., MIX_W:], ML_HEADS) * (ML_DK ** -0.5)
    i_pre = mi.astype(jnp.float32) + ml_b_i.astype(jnp.float32)
    log_f = jax.nn.log_sigmoid(mf.astype(jnp.float32) + ml_b_f.astype(jnp.float32))
    o = mlstm_scan(q, k, heads(mv, ML_HEADS), i_pre, log_f)
    y_ml = (head_rmsnorm(o, ml_norm_g).reshape(bsz, seq, MIX_W) * jax.nn.sigmoid(mo)).astype(h.dtype)

    ybr = jnp.stack([y_ret, y_ssd, y_gla, y_ml], axis=2)
    gates = jax.nn.sigmoid(mgate.reshape(bsz, seq, N_BRANCH, D_MODEL))
    merged = jnp.sum(gates * jnp.einsum('bsnv,nvd->bsnd', ybr, w_branch), axis=2)
    return merged @ w_out

def swiglu(h, w1, w3, w2):
    return (jax.nn.silu(h @ w1) * (h @ w3)) @ w2

def moe_ffn(h, router_w, w1, w3, w2):
    logits = (h @ router_w).astype(jnp.float32)
    top_vals, top_idx = lax.top_k(logits, TOP_K)
    top_w = jax.nn.softmax(top_vals, axis=-1)
    gate = jnp.sum(jax.nn.one_hot(top_idx, N_EXPERTS, dtype=jnp.float32) * top_w[..., None], axis=-2)
    out = jnp.zeros_like(h)
    for e in range(N_EXPERTS):
        out = out + gate[..., e:e + 1].astype(h.dtype) * swiglu(h, w1[e], w3[e], w2[e])
    return out

def first_inputs(seed: int = 0) -> dict:
    key = jax.random.key(seed)
    ks = jax.random.split(key, 40)
    f32 = jnp.float32

    def nrm(i, shape, scale):
        return scale * jax.random.normal(ks[i], shape, f32)

    def gain(i, shape):
        return 1.0 + nrm(i, shape, 0.02)

    nl = DEPTH
    nd = (DEPTH + 1) // 2
    nm = DEPTH // 2
    res = (2.0 * DEPTH) ** -0.5
    dt = jnp.exp(jax.random.uniform(ks[8], (nl, SSD_HEADS), f32, math.log(1e-3), math.log(1e-1)))
    return {
        'x': nrm(0, (BATCH, SEQ, D_MODEL), 1.0),
        'mix_norm_g': gain(1, (nl, D_MODEL)),
        'w_in': nrm(2, (nl, D_MODEL, IN_COLS), D_MODEL ** -0.5),
        'ret_norm_g': gain(3, (nl, MIX_W)),
        'ssd_conv_w': nrm(4, (nl, CONV_K, SSD_CONV_CH), CONV_K ** -0.5),
        'ssd_conv_b': nrm(5, (nl, SSD_CONV_CH), 0.02),
        'ssd_dt_bias': dt + jnp.log(-jnp.expm1(-dt)),
        'ssd_a_log': jnp.log(jax.random.uniform(ks[9], (nl, SSD_HEADS), f32, 1.0, 16.0)),
        'ssd_d': 1.0 + nrm(10, (nl, SSD_HEADS), 0.1),
        'ssd_norm_g': gain(11, (nl, MIX_W)),
        'gla_w_alpha': nrm(12, (nl, GLA_RANK, GLA_HEADS * GLA_DK), GLA_RANK ** -0.5),
        'gla_b_alpha': nrm(13, (nl, GLA_HEADS * GLA_DK), 0.1),
        'gla_norm_g': gain(14, (nl, MIX_W)),
        'ml_conv_w': nrm(15, (nl, CONV_K, 2 * MIX_W), CONV_K ** -0.5),
        'ml_conv_b': nrm(16, (nl, 2 * MIX_W), 0.02),
        'ml_b_i': nrm(17, (nl, ML_HEADS), 0.1),
        'ml_b_f': jnp.linspace(3.0, 6.0, ML_HEADS, dtype=f32)[None, :] + nrm(18, (nl, ML_HEADS), 0.1),
        'ml_norm_g': gain(19, (nl, MIX_W)),
        'w_branch': nrm(20, (nl, N_BRANCH, MIX_W, D_MODEL), MIX_W ** -0.5),
        'w_out': nrm(21, (nl, D_MODEL, D_MODEL), res * D_MODEL ** -0.5),
        'ffn_norm_g': gain(22, (nl, D_MODEL)),
        'ffn_w1': nrm(23, (nd, D_MODEL, D_FF), D_MODEL ** -0.5),
        'ffn_w3': nrm(24, (nd, D_MODEL, D_FF), D_MODEL ** -0.5),
        'ffn_w2': nrm(25, (nd, D_FF, D_MODEL), res * D_FF ** -0.5),
        'router_w': nrm(26, (nm, D_MODEL, N_EXPERTS), D_MODEL ** -0.5),
        'moe_w1': nrm(27, (nm, N_EXPERTS, D_MODEL, EXPERT_FF), D_MODEL ** -0.5),
        'moe_w3': nrm(28, (nm, N_EXPERTS, D_MODEL, EXPERT_FF), D_MODEL ** -0.5),
        'moe_w2': nrm(29, (nm, N_EXPERTS, EXPERT_FF, D_MODEL), res * EXPERT_FF ** -0.5),
        'final_norm_g': gain(30, (D_MODEL,)),
    }

def first_block(x, mix_norm_g, w_in, ret_norm_g, ssd_conv_w, ssd_conv_b, ssd_dt_bias, ssd_a_log, ssd_d,
              ssd_norm_g, gla_w_alpha, gla_b_alpha, gla_norm_g, ml_conv_w, ml_conv_b, ml_b_i, ml_b_f,
              ml_norm_g, w_branch, w_out, ffn_norm_g, ffn_w1, ffn_w3, ffn_w2, router_w, moe_w1, moe_w3,
              moe_w2, final_norm_g):
    pos = jnp.arange(x.shape[1], dtype=jnp.int32)
    for l in range(DEPTH):
        h = rmsnorm(x, mix_norm_g[l])
        x = x + token_mixers(h, pos, w_in[l], ret_norm_g[l], ssd_conv_w[l], ssd_conv_b[l], ssd_dt_bias[l],
                             ssd_a_log[l], ssd_d[l], ssd_norm_g[l], gla_w_alpha[l], gla_b_alpha[l],
                             gla_norm_g[l], ml_conv_w[l], ml_conv_b[l], ml_b_i[l], ml_b_f[l], ml_norm_g[l],
                             w_branch[l], w_out[l]).astype(x.dtype)
        h = rmsnorm(x, ffn_norm_g[l])
        if l % 2 == 0:
            x = x + swiglu(h, ffn_w1[l // 2], ffn_w3[l // 2], ffn_w2[l // 2]).astype(x.dtype)
        else:
            x = x + moe_ffn(h, router_w[l // 2], moe_w1[l // 2], moe_w3[l // 2], moe_w2[l // 2]).astype(x.dtype)
    return rmsnorm(x, final_norm_g)


Q_BLOCK = 128
NEG_INF = -1e30

MLA_HEADS = 8
QK_NOPE = 64
QK_ROPE = 32
V_HEAD = 64
Q_LORA = 256
KV_LORA = 128
ROPE_THETA = 10000.0
MLA_WIDTH = MLA_HEADS * V_HEAD

POOL_WINDOWS = (2, 4, 8, 16)
POOL_GROUPS = 4
POOL_GROUP_DIM = 64
POOL_WIDTH = POOL_GROUPS * POOL_GROUP_DIM
POOL_MAX_WIN = 16

SGU_BLOCK = 128
SGU_GROUPS = 4
SGU_GROUP_DIM = 64
SGU_WIDTH = SGU_GROUPS * SGU_GROUP_DIM

CONV_K_2 = 3
CONV_WIDTH = 256

D_FF_2 = ((8 * D_MODEL + 3 * 256 - 1) // (3 * 256)) * 256

IN_SIZES_2 = (Q_LORA, KV_LORA, QK_ROPE, POOL_WIDTH, SGU_WIDTH, SGU_WIDTH,
            CONV_WIDTH, CONV_WIDTH, CONV_WIDTH, N_BRANCH * D_MODEL)
IN_WIDTH = sum(IN_SIZES_2)


def rmsnorm_2(x, g):
    xf = x.astype(jnp.float32)
    y = xf * lax.rsqrt(jnp.mean(xf * xf, axis=-1, keepdims=True) + EPS)
    return (y * g.astype(jnp.float32)).astype(x.dtype)

def split_cols(p):
    out = []
    o = 0
    for n in IN_SIZES_2:
        out.append(p[..., o:o + n])
        o += n
    return out

def rope_tables(seq, dtype):
    inv = ROPE_THETA ** (-jnp.arange(0, QK_ROPE, 2, dtype=jnp.float32) / QK_ROPE)
    ang = jnp.arange(seq, dtype=jnp.float32)[:, None] * inv[None, :]
    return jnp.cos(ang).astype(dtype), jnp.sin(ang).astype(dtype)

def apply_rope(x, cos, sin):
    half = x.shape[-1] // 2
    x1, x2 = x[..., :half], x[..., half:]
    return jnp.concatenate([x1 * cos - x2 * sin, x2 * cos + x1 * sin], axis=-1)

def mla_branch(c_q, c_kv, k_r, g_cq, g_ckv, w_uq, w_ukv, cos, sin):
    B, S, _ = c_q.shape
    q = (rmsnorm_2(c_q, g_cq) @ w_uq).reshape(B, S, MLA_HEADS, QK_NOPE + QK_ROPE)
    q_nope = q[..., :QK_NOPE]
    q_rope = apply_rope(q[..., QK_NOPE:], cos[:, None, :], sin[:, None, :])
    kv = (rmsnorm_2(c_kv, g_ckv) @ w_ukv).reshape(B, S, MLA_HEADS, QK_NOPE + V_HEAD)
    k_nope, v = kv[..., :QK_NOPE], kv[..., QK_NOPE:]
    k_rope = apply_rope(k_r, cos, sin)
    scale = (QK_NOPE + QK_ROPE) ** -0.5
    chunk_id = jnp.arange(S) // CHUNK
    outs = []
    for blk in range(S // Q_BLOCK):
        q0 = blk * Q_BLOCK
        kend = q0 + Q_BLOCK
        s = (jnp.einsum('bqhd,bkhd->bhqk', q_nope[:, q0:kend], k_nope[:, :kend])
             + jnp.einsum('bqhr,bkr->bhqk', q_rope[:, q0:kend], k_rope[:, :kend]))
        s = s.astype(jnp.float32) * scale
        mask = chunk_id[q0:kend, None] >= chunk_id[None, :kend]
        s = jnp.where(mask[None, None], s, NEG_INF)
        p = jax.nn.softmax(s, axis=-1).astype(v.dtype)
        outs.append(jnp.einsum('bhqk,bkhd->bqhd', p, v[:, :kend]))
    return jnp.concatenate(outs, axis=1).reshape(B, S, MLA_WIDTH)

def pool_branch(z, w_grp, scale):
    B, S, _ = z.shape
    zg = z.reshape(B, S, POOL_GROUPS, POOL_GROUP_DIM).astype(jnp.float32)
    csp = jnp.pad(jnp.cumsum(zg, axis=1), ((0, 0), (POOL_MAX_WIN, 0), (0, 0), (0, 0)))
    t = jnp.arange(S)
    outs = []
    for g, w in enumerate(POOL_WINDOWS):
        win_sum = (csp[:, POOL_MAX_WIN:POOL_MAX_WIN + S, g]
                   - csp[:, POOL_MAX_WIN - w:POOL_MAX_WIN - w + S, g])
        count = jnp.minimum(t + 1, w).astype(jnp.float32)
        outs.append(win_sum / count[None, :, None] - zg[:, :, g])
    pooled = jnp.stack(outs, axis=2).astype(z.dtype)
    mixed = jnp.einsum('bsgc,gcd->bsgd', pooled, w_grp)
    return mixed.reshape(B, S, POOL_WIDTH) * scale

def sgu_branch(u, v, g_v, w_s, b_s):
    B, S, _ = u.shape
    n = S // SGU_BLOCK
    vn = rmsnorm_2(v, g_v).reshape(B, n, SGU_BLOCK, SGU_GROUPS, SGU_GROUP_DIM)
    pos_chunk = jnp.arange(SGU_BLOCK) // CHUNK
    mask = pos_chunk[:, None] >= pos_chunk[None, :]
    w = jnp.where(mask[None], w_s, 0)
    mixed = jnp.einsum('gij,bnjgc->bnigc', w, vn) + b_s.T[None, None, :, :, None]
    return u * mixed.reshape(B, S, SGU_WIDTH)

def conv_branch(b_gate, c_gate, x_in, w_conv):
    z = c_gate * x_in
    y = lax.conv_general_dilated(z, w_conv, window_strides=(1,),
                                 padding=[(CONV_K_2 - 1, 0)],
                                 dimension_numbers=('NWC', 'WIO', 'NWC'),
                                 feature_group_count=CONV_WIDTH)
    return b_gate * y

def second_inputs(seed: int = 0) -> dict:
    key = jax.random.key(seed)
    ks = iter(jax.random.split(key, 32))

    def nrm(shape, fan_in):
        return jax.random.normal(next(ks), shape, jnp.float32) * (fan_in ** -0.5)

    def gain(shape):
        return 1.0 + 0.1 * jax.random.normal(next(ks), shape, jnp.float32)

    L = DEPTH
    return {
        "x": jax.random.normal(next(ks), (BATCH, SEQ, D_MODEL), jnp.float32),
        "w_in": nrm((L, D_MODEL, IN_WIDTH), D_MODEL),
        "g_pre_mix": gain((L, D_MODEL)),
        "g_cq": gain((L, Q_LORA)),
        "g_ckv": gain((L, KV_LORA)),
        "w_uq": nrm((L, Q_LORA, MLA_HEADS * (QK_NOPE + QK_ROPE)), Q_LORA),
        "w_ukv": nrm((L, KV_LORA, MLA_HEADS * (QK_NOPE + V_HEAD)), KV_LORA),
        "pool_w": nrm((L, POOL_GROUPS, POOL_GROUP_DIM, POOL_GROUP_DIM), POOL_GROUP_DIM),
        "pool_scale": gain((L, POOL_WIDTH)),
        "g_sgu_v": gain((L, SGU_WIDTH)),
        "sgu_w": nrm((L, SGU_GROUPS, SGU_BLOCK, SGU_BLOCK), SGU_BLOCK),
        "sgu_b": gain((L, SGU_GROUPS, SGU_BLOCK)),
        "conv_w": nrm((L, CONV_K_2, 1, CONV_WIDTH), CONV_K_2),
        "w_br_a": nrm((L, MLA_WIDTH, D_MODEL), MLA_WIDTH),
        "w_br_b": nrm((L, POOL_WIDTH, D_MODEL), POOL_WIDTH),
        "w_br_c": nrm((L, SGU_WIDTH, D_MODEL), SGU_WIDTH),
        "w_br_d": nrm((L, CONV_WIDTH, D_MODEL), CONV_WIDTH),
        "w_out": nrm((L, D_MODEL, D_MODEL), D_MODEL),
        "g_post_mix": gain((L, D_MODEL)),
        "g_pre_ffn": gain((L, D_MODEL)),
        "w_ffn_gate": nrm((L, D_MODEL, D_FF_2), D_MODEL),
        "w_ffn_up": nrm((L, D_MODEL, D_FF_2), D_MODEL),
        "w_ffn_down": nrm((L, D_FF_2, D_MODEL), D_FF_2),
        "g_post_ffn": gain((L, D_MODEL)),
    }

def second_block(x, w_in, g_pre_mix, g_cq, g_ckv, w_uq, w_ukv, pool_w, pool_scale,
              g_sgu_v, sgu_w, sgu_b, conv_w, w_br_a, w_br_b, w_br_c, w_br_d,
              w_out, g_post_mix, g_pre_ffn, w_ffn_gate, w_ffn_up, w_ffn_down,
              g_post_ffn):
    B, S, D = x.shape
    cos, sin = rope_tables(S, x.dtype)
    for l in range(DEPTH):
        h = rmsnorm_2(x, g_pre_mix[l])
        (c_q, c_kv, k_r, p_in, s_u, s_v, cv_b, cv_c, cv_x,
         gate_logits) = split_cols(h @ w_in[l])
        y_a = mla_branch(c_q, c_kv, k_r, g_cq[l], g_ckv[l], w_uq[l], w_ukv[l], cos, sin) @ w_br_a[l]
        y_b = pool_branch(p_in, pool_w[l], pool_scale[l]) @ w_br_b[l]
        y_c = sgu_branch(s_u, s_v, g_sgu_v[l], sgu_w[l], sgu_b[l]) @ w_br_c[l]
        y_d = conv_branch(cv_b, cv_c, cv_x, conv_w[l]) @ w_br_d[l]
        gates = jax.nn.sigmoid(gate_logits.astype(jnp.float32)).astype(x.dtype)
        gates = gates.reshape(B, S, N_BRANCH, D)
        merged = (gates[:, :, 0] * y_a + gates[:, :, 1] * y_b
                  + gates[:, :, 2] * y_c + gates[:, :, 3] * y_d)
        x = x + rmsnorm_2(merged @ w_out[l], g_post_mix[l])
        h = rmsnorm_2(x, g_pre_ffn[l])
        f = (jax.nn.silu(h @ w_ffn_gate[l]) * (h @ w_ffn_up[l])) @ w_ffn_down[l]
        x = x + rmsnorm_2(f, g_post_ffn[l])
    return x


def setup_inputs(seed=0):
    out = dict(first_inputs(seed))
    for name, value in second_inputs(seed + 1).items():
        if name != "x":
            out[name + "_2"] = value
    return out


def reference(
    x, mix_norm_g, w_in, ret_norm_g, ssd_conv_w, ssd_conv_b, ssd_dt_bias, ssd_a_log, ssd_d,
    ssd_norm_g, gla_w_alpha, gla_b_alpha, gla_norm_g, ml_conv_w, ml_conv_b, ml_b_i, ml_b_f,
    ml_norm_g, w_branch, w_out, ffn_norm_g, ffn_w1, ffn_w3, ffn_w2, router_w, moe_w1, moe_w3,
    moe_w2, final_norm_g, w_in_2, g_pre_mix_2, g_cq_2, g_ckv_2, w_uq_2, w_ukv_2, pool_w_2,
    pool_scale_2, g_sgu_v_2, sgu_w_2, sgu_b_2, conv_w_2, w_br_a_2, w_br_b_2, w_br_c_2, w_br_d_2,
    w_out_2, g_post_mix_2, g_pre_ffn_2, w_ffn_gate_2, w_ffn_up_2, w_ffn_down_2, g_post_ffn_2,
):
    x = first_block(
        x, mix_norm_g, w_in, ret_norm_g, ssd_conv_w, ssd_conv_b, ssd_dt_bias, ssd_a_log, ssd_d,
        ssd_norm_g, gla_w_alpha, gla_b_alpha, gla_norm_g, ml_conv_w, ml_conv_b, ml_b_i, ml_b_f,
        ml_norm_g, w_branch, w_out, ffn_norm_g, ffn_w1, ffn_w3, ffn_w2, router_w, moe_w1,
        moe_w3, moe_w2, final_norm_g,
    )
    return second_block(
        x, w_in_2, g_pre_mix_2, g_cq_2, g_ckv_2, w_uq_2, w_ukv_2, pool_w_2, pool_scale_2,
        g_sgu_v_2, sgu_w_2, sgu_b_2, conv_w_2, w_br_a_2, w_br_b_2, w_br_c_2, w_br_d_2, w_out_2,
        g_post_mix_2, g_pre_ffn_2, w_ffn_gate_2, w_ffn_up_2, w_ffn_down_2, g_post_ffn_2,
    )


_drawn_inputs = setup_inputs


def setup_inputs(seed=0):
    import zlib

    import numpy as np

    out = dict(_drawn_inputs(seed))
    spreads = {}
    factors = {'ret_norm_g': 4.864,
     'gla_norm_g': 2.789,
     'ml_conv_b': 3.07,
     'ml_b_i': 64.0,
     'ml_norm_g': 8.0,
     'g_cq_2': 5.71,
     'g_ckv_2': 3.471}
    for name, (base, spread) in spreads.items():
        noise = np.random.default_rng([zlib.crc32(name.encode()), seed]).standard_normal(out[name].shape)
        drawn = base * np.exp(spread * noise) if base else spread * noise
        out[name] = jnp.asarray(drawn.astype(out[name].dtype))
    for name, factor in factors.items():
        out[name] = (out[name] * factor).astype(out[name].dtype)
    return out
```

```python
import numpy as np
from contextlib import ExitStack

import concourse.bass as bass
from concourse import mybir

F32 = mybir.dt.float32
I32 = mybir.dt.int32
U32 = mybir.dt.uint32
ALU = mybir.AluOpType
ACT = mybir.ActivationFunctionType
AX = mybir.AxisListType

P = 128
T = 2
S = T * P
D = 1024
KD = D // P
EPS = 1e-6
NH = 4
MW = 256
NBR = 4
FF = 2816
FC = 256
NF = FF // FC
NE = 8
MAXPASS = 11
NEG = -1.0e30

RQ, RV, RG, SZ, SX, SB, SC, SDT = 0, 512, 768, 1024, 1280, 1536, 1792, 2048
GQ, GK, GV, GR, GA, MQ, MK, MV, MO, MI, MF, GATE1 = 2052, 2180, 2308, 2564, 2820, 2836, 3092, 3348, 3604, 3860, 3864, 3868
RANK = 16

CQ, CKV, KR, PI, SU, SV, CB, CC, CX, GATE2 = 0, 256, 384, 416, 672, 928, 1184, 1440, 1696, 1952
AH, NOPE, ROPE, VH = 8, 64, 32, 64
UP_QN, UP_QR, UP_KN, UP_V = 0, 2 * AH * NOPE, 2 * AH * (NOPE + ROPE), 2 * AH * (NOPE + ROPE) + AH * NOPE
POOL_WINDOWS = (2, 4, 8, 16)
BLOCKED = 64

NSLOT = 3
SLOTW = KD * 2 * FC + 2 * D


def shape_constants():
    j, i = np.arange(P)[:, None], np.arange(P)[None, :]
    parts = {}
    parts["ident"] = (j == i)
    parts["tri"] = (j <= i)
    parts["ones"] = np.ones((P, P))
    parts["after"] = (j > i)
    parts["negmask"] = np.where(i < j, NEG, 0.0)
    parts["bigmask"] = np.where(i < j, -NEG, 0.0)
    sel = np.zeros((P, NH, P))
    for h in range(NH):
        sel[h, h, :] = 1
    parts["sel"] = sel.reshape(P, -1)
    parts["iota"] = np.broadcast_to(i, (P, P))
    parts["iotap"] = j
    parts["rank8"] = np.broadcast_to(NE - np.arange(NE)[None, :], (P, NE))
    parts["passno"] = np.broadcast_to(np.arange(MAXPASS)[None, :], (P, MAXPASS))
    half = 32
    inv = (np.float32(10000.0) ** (-np.arange(half, dtype=np.float32) / np.float32(half))).astype(np.float32)
    ang = (np.arange(S, dtype=np.float32)[:, None] * inv[None, :]).astype(np.float32).astype(np.float64)
    parts["cos"] = np.cos(ang).reshape(T, P, half).transpose(1, 0, 2).reshape(P, -1)
    parts["sin"] = np.sin(ang).reshape(T, P, half).transpose(1, 0, 2).reshape(P, -1)
    lg = np.log1p(-np.exp2(-5.0 - np.arange(NH)))
    tok = np.arange(S)[None, :]
    rel = tok - j
    dec = np.stack([np.where(rel >= 0, np.exp(np.maximum(rel, 0) * g), 0.0) * 64 ** -0.5 for g in lg], 1)
    parts["retdecay"] = dec.reshape(P, -1)
    lev = [((j // (2 * b) == i // (2 * b)) & ((j // b) % 2 == 0) & ((i // b) % 2 == 1)) for b in (1, 2, 4, 8, 16, 32, 64)]
    parts["levmask"] = np.stack(lev + [j == i], 1).reshape(P, -1)
    off, at, cols = 0, {}, []
    for k, v in parts.items():
        at[k] = (off, off + v.shape[1])
        off += v.shape[1]
        cols.append(np.asarray(v, np.float32))
    return np.ascontiguousarray(np.concatenate(cols, 1)), at


def shape_constants2():
    parts = {}
    inv = (np.float32(10000.0) ** (-np.arange(0, ROPE, 2, dtype=np.float32) / np.float32(ROPE))).astype(np.float32)
    ang = (np.arange(S, dtype=np.float32)[:, None] * inv[None, :]).astype(np.float32).astype(np.float64)
    parts["cos2"] = np.cos(ang).reshape(T, P, -1).transpose(1, 0, 2).reshape(P, -1)
    parts["sin2"] = np.sin(ang).reshape(T, P, -1).transpose(1, 0, 2).reshape(P, -1)
    j, i = np.arange(S)[:, None], np.arange(S)[None, :]
    win = np.stack([((j <= i) & (j > i - w)) / np.minimum(i + 1, w) - (j == i) for w in POOL_WINDOWS], 1)
    parts["window"] = np.concatenate([win[:P], win[P:, :, P:]], 2).reshape(P, -1)
    early = np.arange(P) < BLOCKED
    parts["rowmask"] = np.broadcast_to(early[None, :], (P, P))
    parts["colmask"] = np.broadcast_to(np.where(early, 0.0, NEG)[None, :], (P, P))
    off, at, cols = 0, {}, []
    for k, v in parts.items():
        at[k] = (off, off + v.shape[1])
        off += v.shape[1]
        cols.append(np.asarray(v, np.float32))
    return np.ascontiguousarray(np.concatenate(cols, 1)), at


CHUNKS1 = [
    (SZ, 512, [("ch", ((SX, 128), (SX + 128, 128))), ("tok", 0, SZ, 256), ("tok", 1, SZ, 256)]),
    (SB, 512, [("ch", ((SB, 128), (SB + 128, 128))), ("ch", ((SC, 128), (SC + 128, 128)))]),
    (GR, 528, [("ch", ((MQ, 128), (MQ + 128, 128))), ("ch", ((GA, RANK),)), ("tok", 0, GR, 256), ("tok", 1, GR, 256)]),
    (MK, 512, [("ch", ((MK, 128), (MK + 128, 128))), ("tok", 0, MV, 256), ("tok", 1, MV, 256)]),
    (SDT, 516, [("ch", ((GQ, 128), (GK, 128))), ("tok2", 0), ("tok2", 1)]),
    (MO, 264, [("tok", 0, MO, 264), ("tok", 1, MO, 264)]),
    (RQ, 512, [("tok", 0, RQ, 512), ("tok", 1, RQ, 512)]),
    (RV, 512, [("tok", 0, RV, 512), ("tok", 1, RV, 512)]),
]
CHUNKS2 = [
    (CQ, 416, [("tok", 0, CQ, 416), ("tok", 1, CQ, 416)]),
    (PI, 512, [("tok", 0, PI, 512), ("tok", 1, PI, 512)]),
    (SV, 512, [("tok", 0, SV, 256), ("tok", 1, SV, 256), ("ch", ((CB, 128), (CB + 128, 128)))]),
    (CC, 512, [("ch", ((CC, 128), (CC + 128, 128))), ("ch", ((CX, 128), (CX + 128, 128)))]),
]
BR_ORDER2 = (3, 1, 2, 0)
BR_ORDER = (1, 3, 0, 2)


def bank_jobs1():
    jobs = [("turn", k) for k in range(4)]
    for c, (_, _, js) in enumerate(CHUNKS1):
        jobs += [("proj", c, j) for j in range(len(js))]
    gates = lambda b: [("gate", b, h, i) for h in range(2) for i in range(T)]
    merge = lambda b: [("yturn", b)] + [("merge", b, h, i) for h in range(2) for i in range(T)]
    jobs += gates(0) + gates(1) + merge(0) + gates(2) + merge(1) + gates(3) + merge(2) + merge(3)
    jobs += [("turn", 4 + k) for k in range(4)] + [("wout", h, i) for h in range(2) for i in range(T)]
    jobs += [("turn", 8 + k) for k in range(4)]
    return jobs


def bank_jobs2():
    gate = lambda b, *ns: [("gate", b, n // 2, n % 2) for n in ns]
    merge = lambda b: [("merge", b, h, i) for h in range(2) for i in range(T)]
    jobs = [("turn", k) for k in range(4)]
    for c, (_, _, js) in enumerate(CHUNKS2):
        jobs += [("proj", c, j) for j in range(len(js))]
    jobs += gate(0, 0, 1, 2, 3) + gate(1, 0, 1) + merge(0) + gate(1, 2, 3) + merge(1) + gate(2, 0, 1, 2, 3)
    jobs += [("yturn", 2, 0)] + merge(2) + gate(3, 0, 1, 2, 3) + [("yturn", 3, 0), ("yturn", 3, 1)] + merge(3)
    jobs += [("turn", 4 + k) for k in range(4)] + [("wout", h, i) for h in range(2) for i in range(T)]
    jobs += [("turn", 8 + k) for k in range(4)]
    return jobs


class Banks:

    def __init__(self, jobs, fill_base, act_base, dve_base, layer):
        self.jobs = jobs
        self.by = ["dve" if j[0] in ("merge", "wout") else "act" for j in jobs]
        n_act, n_dve = self.by.count("act"), self.by.count("dve")
        self.fill0 = fill_base + layer * len(jobs)
        self.act0 = act_base + layer * n_act
        self.dve0 = dve_base + layer * n_dve
        self.end = (self.fill0 + len(jobs), self.act0 + n_act, self.dve0 + n_dve)
        self.index = {j: n for n, j in enumerate(jobs)}

    def filled(self, job):
        return self.fill0 + self.index[job] + 1

    def emptied(self, job):
        n = self.index[job]
        who = self.by[n]
        return who, (self.act0 if who == "act" else self.dve0) + self.by[:n + 1].count(who)


def build(nc, a, out, stop=None):
    cvals, cat = shape_constants()
    cdram = nc.inline_tensor(cvals, name="shape_constants")
    cvals2, cat2 = shape_constants2()
    cdram2 = nc.inline_tensor(cvals2, name="shape_constants2")
    ctx = ExitStack()
    with ctx:
        def sb(name, shape, dt=F32):
            return ctx.enter_context(nc.sbuf_tensor(name, shape, dt))

        def sem(name):
            return ctx.enter_context(nc.semaphore(name))

        ring = sb("ring", [P, NSLOT, SLOTW])
        x = sb("x", [P, T, D])
        xn = sb("xn", [P, T, D])
        hT = sb("hT", [P, KD, S])
        merged = sb("merged", [P, T, D])
        gates = sb("gates", [P, 2, T, D])
        u_ret = sb("u_ret", [P, T, 1024])
        u_z = sb("u_z", [P, T, MW])
        u_gla = sb("u_gla", [P, T, 4 + 2 * MW])
        u_ml = sb("u_ml", [P, T, 2 * MW + 8])
        ch_in = sb("ch_in", [P, 13, S])
        conv = sb("conv", [P, 10, S])
        probs = sb("probs", [P, NH, 384])
        xs = sb("xs", [P, T, MW])
        xdt = sb("xdt", [P, T, MW])
        y = sb("y", [P, T, MW])
        yT = sb("yT", [P, 2, 2, S])
        scratch = sb("scratch", [P, 512])
        cst = sb("cst", [P, cvals.shape[1]])
        gain = sb("gain", [P, D])
        ygain = sb("ygain", [P, D])
        soft = sb("soft", [P, T, 136])
        small = sb("small", [P, 160])
        rows = sb("rows", [P, P])
        perch = sb("perch", [P, P])
        alpha_w = sb("alpha_w", [RANK, 2, P])
        bc = sb("bc", [P, 2, 148])
        ea = sb("ea", [P, 2, 4])
        mrow = merged[0:NH, 0, 0:2 * S].rearrange("p (k s) -> p k s", k=2)

        def const(name):
            lo, hi = cat[name]
            return cst[:, lo:hi]

        ident, tri, ones, after = const("ident"), const("tri"), const("ones"), const("after")
        cosT = const("cos").rearrange("p (t h) -> p t h", t=T)
        sinT = const("sin").rearrange("p (t h) -> p t h", t=T)
        retdecay = const("retdecay").rearrange("p (h i) -> p h i", h=NH)
        levmask = const("levmask").rearrange("p (l i) -> p l i", l=8)
        head_sel = const("sel").rearrange("p (h i) -> p h i", h=NH)
        g1 = gates[:, 1].rearrange("p t d -> p (t d)")
        sp_tmp = [g1[:, 272 * n:272 * (n + 1)] for n in range(6)]
        rot_c = g1[:, 0:1024].rearrange("p (t h c) -> p t h c", t=T, h=8)
        rot_s = g1[:, 1024:2048].rearrange("p (t h c) -> p t h c", t=T, h=8)
        w_seg = ch_in[:, 0:4].rearrange("p b s -> p (b s)").rearrange("p (h t j) -> p h t j", h=NH, t=T)
        w_one = ch_in[:, 4:6].rearrange("p b s -> p (b s)").rearrange("p (h j) -> p h j", h=NH)
        gla_e, gla_k, gla_q = ch_in[:, 0:4], ch_in[:, 4:8], conv[:, 0:4]
        fsg, fh, fhT = xs, u_z, xdt
        gT = sb("gT", [P, S])
        ret_qk = conv[:, 6:10]
        ssq, rstd = small[:, 0:2], small[:, 2:4]
        hs, hr = small[:, 4:12], small[:, 12:20]
        dA = small[:, 20:28]
        e_tok, nb_tok = small[:, 28:36], small[:, 36:44]
        em, den, rden = small[:, 44:52], small[:, 52:60], small[:, 60:68]
        negm = small[:, 68:76]
        r_tmp, r_in = small[:, 76:84], small[:, 84:86]
        g0 = gates[:, 0].rearrange("p t d -> p (t d)")
        router = g1[:, 0:64].rearrange("p (k e) -> p k e", k=KD)
        logit, one1, one2, both = (g1[:, 64 + 16 * n:80 + 16 * n].rearrange("p (t e) -> p t e", t=T) for n in range(4))
        eq, at_, tmp16 = (g1[:, 128 + 16 * n:144 + 16 * n].rearrange("p (t e) -> p t e", t=T) for n in range(3))
        m1, m2, kx, ex = (g1[:, 176 + 2 * n:178 + 2 * n] for n in range(4))
        n_tiles, p_end, p_start, zero8 = (g1[:, 184 + 8 * n:192 + 8 * n] for n in range(4))
        quad = g1[:, 216:224].rearrange("p (q t) -> p q t", q=4)
        e_cmp = g1[:, 224:224 + MAXPASS * NE].rearrange("p (n e) -> p n e", n=MAXPASS)
        e_tab = g1[:, 312:312 + MAXPASS + 1]
        slot_no = g1[:, 324:325]
        diag = g1[:, 384:384 + 8 * P].rearrange("p (q t i) -> p q t i", q=4, t=T)
        quad_b = g0[:, 0:4 * S].rearrange("p (q s) -> p q s", q=4)
        sel = g0[:, 4 * S:5 * S].rearrange("p (t s) -> p t s", t=T)
        selT = g0[:, 5 * S:6 * S]
        sel_tmp = g0[:, 6 * S:7 * S]
        xg = u_ret[:, 0].rearrange("p (k s) -> p k s", k=KD)
        ys = u_ret[:, 1]
        table = sb("table", [1, MAXPASS + 1], I32)

        cst2 = cst[:, cat["retdecay"][0]:cat["retdecay"][0] + cvals2.shape[1]]
        assert cat["retdecay"][0] + cvals2.shape[1] <= cat["levmask"][1] == cvals.shape[1]

        def const2(name):
            lo, hi = cat2[name]
            return cst2[:, lo:hi]

        cos2 = const2("cos2").rearrange("p (t c) -> p t c", t=T)
        sin2 = const2("sin2").rearrange("p (t c) -> p t c", t=T)
        window = const2("window").rearrange("p (g i) -> p g i", g=4)
        lat = u_ret[:, :, 0:416]
        pool_in, sgu_u = u_ret[:, :, 512:768], u_ret[:, :, 768:1024]
        sgu_v = u_gla[:, :, 0:MW]
        k_rot = u_gla[:, :, MW:MW + ROPE]
        cqT, ckvT = ch_in[:, 6:8], ch_in[:, 8]
        conv_b, conv_c, conv_x, convT = ch_in[:, 0:2], ch_in[:, 2:4], ch_in[:, 4:6], conv[:, 0:2]
        qT = conv[0:NOPE + ROPE, 2:10]
        kT = ring[0:NOPE + ROPE, 0, KD * 512:KD * 512 + AH * S].rearrange("p (h s) -> p h s", h=AH)
        v_tok = u_ml[:, :, 0:512]
        q_rope, rope_c, rope_s, q_rot = xs, u_z, xdt, y
        pooled = xdt
        xn_flat = xn[:].rearrange("p t d -> p (t d)")
        probsT = xn_flat[:, 0:4 * 384].rearrange("p (h n) -> p h n", h=4)
        sgu_w = xn_flat[:, 4 * 384:2048].rearrange("p (g j) -> p g j", g=4)
        sgu_wT = scratch[:].rearrange("p (g i) -> p g i", g=4)
        pool_w = soft[:].rearrange("p t n -> p (t n)")[:, 0:P].rearrange("p (a d) -> p a d", a=2)
        poolT, sguT, attT = yT[:, 0], yT[:, 1], ch_in[:, 0:4]
        y_sgu = u_gla[:, :, 0:MW]
        y_att = u_ret[:, :, 0:512]
        mx, nmx, sums, rsum = (small[:, 88 + 8 * n:96 + 8 * n] for n in range(4))
        lat_s, lat_m, lat_r = small[:, 120:126], small[:, 126:130], small[:, 130:134]

        pb = [ctx.enter_context(nc.psum_tensor(f"pb{n}", [P, 512], F32)) for n in range(4)]
        mb = [ctx.enter_context(nc.psum_tensor(f"mb{n}", [P, 512], F32)) for n in range(4)]

        filled, act_emptied, dve_emptied = sem("pb_filled"), sem("pb_act_emptied"), sem("pb_dve_emptied")
        arrived = [sem(f"w_arrived{n}") for n in range(NSLOT)]
        params_in, x_in, gain_in, ygain_in = sem("params_in"), sem("x_in"), sem("gain_in"), sem("ygain_in")
        stored = sem("stored")
        dve_step, act_step = sem("dve_step"), sem("act_step")
        squares, xn_ready = sem("squares"), sem("xn_ready")
        rows_turned, perch_ready, ea_ready = sem("rows_turned"), sem("perch_ready"), sem("ea_ready")
        x_ready = sem("x_ready")
        conv_raw, conv_ready = sem("conv_raw"), sem("conv_ready")
        alpha_mm, sp_abs, sp_exp, soft_ready = sem("alpha_mm"), sem("sp_abs"), sem("sp_exp"), sem("soft_ready")
        cums_mm, g_ready, e_ready, xs_mm, xdt_ready = (sem(s) for s in ("cums_mm", "g_ready", "e_ready", "xs_mm", "xdt_ready"))
        wseg_ready, seg_mm, seg_exp = sem("wseg_ready"), sem("seg_mm"), sem("seg_exp")
        scores_mm, probs_ready, pv_mm, o_read, y_ready = (sem(s) for s in ("scores_mm", "probs_ready", "pv_mm", "o_read", "y_ready"))
        et_mm, mt_ready, mbc_mm, ml_arg, ml_exp, em_ready, negm_ready = (sem(s) for s in (
            "et_mm", "mt_ready", "mbc_mm", "ml_arg", "ml_exp", "em_ready", "negm_ready"))
        rot_ready, qkt_mm, qkt_ready = sem("rot_ready"), sem("qkt_mm"), sem("qkt_ready")
        gla_arg, gla_exp, gla_kq, gla_mm, gla_put = (sem(s) for s in ("gla_arg", "gla_exp", "gla_kq", "gla_mm", "gla_put"))
        merged_ready = sem("merged_ready")
        gu_mm, silu_done, h_ready, ht_mm, ht_ready, ffn_mm = (sem(s) for s in (
            "gu_mm", "silu_done", "h_ready", "ht_mm", "ht_ready", "ffn_mm"))

        router_in, logits_mm, ex_arg, ex_ready = sem("router_in"), sem("logits_mm"), sem("ex_arg"), sem("ex_ready")
        both_ready, rank_mm, diag_ready, quad_mm, table_ready = (sem(s) for s in (
            "both_ready", "rank_mm", "diag_ready", "quad_mm", "table_ready"))
        sel_ready, gather_mm, xg_ready, selT_ready, scatter_mm, ys_ready = (sem(s) for s in (
            "sel_ready", "gather_mm", "xg_ready", "selT_ready", "scatter_mm", "ys_ready"))
        e_arrived = [sem(f"e_arrived{n}") for n in range(NSLOT)]
        e_gu, e_silu, e_h, e_ht_mm, e_ht, e_down = (sem(s) for s in ("e_gu", "e_silu", "e_h", "e_ht_mm", "e_ht", "e_down"))
        zero_ready, moe_mm, final_ready, sel_step = sem("zero_ready"), sem("moe_mm"), sem("final_ready"), sem("sel_step")

        def step_loads(c):
            return 2 * (c < NF) + (c > 0)

        def e_landed(t, c):
            mine = range(c % NSLOT, NF + 1, NSLOT)
            return t * (16 * sum(step_loads(n) for n in mine)) + 16 * sum(step_loads(n) for n in mine if n <= c)

        cst2_in, sgu_in, pool_in_sem = sem("cst2_in"), sem("sgu_in"), sem("pool_in")
        lat_ready, latT_mm, latT_ready, qn_mm, qn_ready, kn_mm, kn_ready, qrv_mm, qrv_ready, q_rot_ready, qrT_mm, qrT_ready = (sem(s) for s in (
            "lat_ready", "latT_mm", "latT_ready", "qn_mm", "qn_ready", "kn_mm", "kn_ready", "qrv_mm", "qrv_ready", "q_rot_ready", "qrT_mm", "qrT_ready"))
        pooled_mm, pooled_ready, poolT_mm, poolT_ready, convT_ready = (sem(s) for s in (
            "pooled_mm", "pooled_ready", "poolT_mm", "poolT_ready", "convT_ready"))
        sgu_turned, sgu_wT_ready, vn_ready, sgu_mm, y_sgu_ready = (sem(s) for s in (
            "sgu_turned", "sgu_wT_ready", "vn_ready", "sgu_mm", "y_sgu_ready"))
        att_mm, att_max, att_exp, probsT_mm, probsT_ready, av_mm, y_att_ready = (sem(s) for s in (
            "att_mm", "att_max", "att_exp", "probsT_mm", "probsT_ready", "av_mm", "y_att_ready"))
        post_in = sem("post_in")
        BK = []
        base = (0, 0, 0)
        for L in range(2):
            BK.append(Banks(bank_jobs1(), *base, 0))
            base = BK[-1].end
        for L in range(2):
            BK.append(Banks(bank_jobs2(), *base, 0))
            base = BK[-1].end

        items, find = [], {}
        uses = [0] * NSLOT

        def add_item(key, loads, free):
            s = sum(i != "experts" for i in items) % NSLOT
            uses[s] += 16 * len(loads)
            find[key] = (s, uses[s])
            items.append((s, loads, free))

        def cols(w, lo, n, at=0):
            return (at, w[:, lo:lo + n].rearrange("(k p) n -> p k n", p=P))

        u_key = []

        def ffn_items(u, key, w1, w3, w2):
            u_key.append(key)
            for c in range(NF + 1):
                loads = []
                if c < NF:
                    loads += [("gu", 0, w1[:, c * FC:(c + 1) * FC].rearrange("(k p) n -> p k n", p=P)),
                              ("gu", 1, w3[:, c * FC:(c + 1) * FC].rearrange("(k p) n -> p k n", p=P))]
                if c > 0:
                    loads += [("down", 0, w2[(c - 1) * FC:c * FC, :].rearrange("(k p) n -> p k n", p=P))]
                add_item((key, c), loads, (ffn_mm, u * NF + c) if c else (gu_mm, T * (u * NF + 1)))

        def slot_view(s, load):
            kind = load[0]
            if kind == "gu":
                v = ring[:, s, 0:KD * 2 * FC].rearrange("p (k g n) -> p k g n", k=KD, g=2)
                return v[:, :, load[1]]
            if kind == "down":
                return ring[:, s, KD * 2 * FC:SLOTW].rearrange("p (k n) -> p k n", k=2)
            k, n = load[2].shape[1:]
            return ring[:, s, load[1]:load[1] + k * n].rearrange("p (k n) -> p k n", k=k)

        for L in range(2):
            B = BK[L]
            w_in = a["w_in"][L]
            for c, (lo, n, js) in enumerate(CHUNKS1):
                add_item((L, "proj", c), [("cols", 0, w_in[:, lo:lo + n].rearrange("(k p) n -> p k n", p=P))],
                         (filled, B.filled(("proj", c, len(js) - 1))))

            def gate_items(b):
                for h in range(2):
                    lo = GATE1 + BR_ORDER[b] * D + h * 512
                    add_item((L, "gate", b, h), [("cols", 0, w_in[:, lo:lo + 512].rearrange("(k p) n -> p k n", p=P))],
                             (filled, B.filled(("gate", b, h, 1))))

            def branch_item(b):
                add_item((L, "branch", b), [("cols", 0, a["w_branch"][L, BR_ORDER[b]].rearrange("(k p) n -> p k n", p=P))],
                         (filled, B.filled(("merge", b, 1, 1))))

            gate_items(0); gate_items(1); branch_item(0); gate_items(2); branch_item(1); gate_items(3)
            branch_item(2); branch_item(3)
            for h in range(2):
                add_item((L, "wout", h), [("cols", 0, a["w_out"][L][:, h * 512:h * 512 + 512].rearrange("(k p) n -> p k n", p=P))],
                         (filled, B.filled(("wout", h, 1))))
            if stop == ("mix", L):
                break
            if L == 0:
                ffn_items(0, (0, "ffn"), a["ffn_w1"][0], a["ffn_w3"][0], a["ffn_w2"][0])
                if stop == ("ffn", 0):
                    break
            else:
                items.append("experts")
        n_layers = L + 1
        has_ffn = lambda L: not (stop == ("mix", L))

        def by_k(src):
            return ("cols", 0, src.rearrange("(k p) n -> p k n", p=P))

        if stop is None:
            for l in range(2):
                L = 2 + l
                B = BK[L]
                w_in = a["w_in_2"][l]
                for c, (lo, n, js) in enumerate(CHUNKS2):
                    add_item((L, "proj", c), [by_k(w_in[:, lo:lo + n])], (filled, B.filled(("proj", c, len(js) - 1))))

                def gates2(b, *hs_):
                    for h in hs_:
                        lo = GATE2 + BR_ORDER2[b] * D + h * 512
                        add_item((L, "gate", b, h), [by_k(w_in[:, lo:lo + 512])], (filled, B.filled(("gate", b, h, 1))))

                def branch2(b):
                    w = a["w_br_" + "abcd"[BR_ORDER2[b]] + "_2"][l]
                    add_item((L, "branch", b), [by_k(w)], (filled, B.filled(("merge", b, 1, 1))))

                gates2(0, 0)
                heads = lambda w: w.rearrange("p (h c) -> p h c", h=AH)
                up = []
                for k in range(2):
                    uq = heads(a["w_uq_2"][l][k * P:(k + 1) * P, :])
                    up += [("cols", UP_QN + k * AH * NOPE, uq[:, :, 0:NOPE]), ("cols", UP_QR + k * AH * ROPE, uq[:, :, NOPE:])]
                ukv = heads(a["w_ukv_2"][l])
                up += [("cols", UP_KN, ukv[:, :, 0:NOPE]), ("cols", UP_V, ukv[:, :, NOPE:])]
                add_item((L, "up"), up, (qrv_mm, l + 1))
                gates2(0, 1); gates2(1, 0); branch2(0); gates2(1, 1); branch2(1); gates2(2, 0, 1); branch2(2)
                gates2(3, 0, 1); branch2(3)
                for h in range(2):
                    add_item((L, "wout", h), [by_k(a["w_out_2"][l][:, h * 512:h * 512 + 512])], (filled, B.filled(("wout", h, 1))))
                ffn_items(1 + l, (L, "ffn"), a["w_ffn_gate_2"][l], a["w_ffn_up_2"][l], a["w_ffn_down_2"][l])

        block = ctx.enter_context(nc.Block())

        def passes(eng):
            eng.wait_ge(table_ready, 1)
            return eng.value_load(table[0:1, MAXPASS:MAXPASS + 1], min_val=1, max_val=MAXPASS)

        def expert_weights(sp):
            n_pass = passes(sp)
            with sp.Fori(0, n_pass) as t:
                e = sp.value_load(table[0:1, bass.ds(t, 1)], min_val=0, max_val=NE - 1)
                for c in range(NF + 1):
                    s = c % NSLOT
                    if c == NSLOT:
                        sp.wait_ge(e_gu, t * NF + 1)
                    else:
                        sp.wait_ge(e_down, t * NF + NF + c - NSLOT + (c < NSLOT))
                    srcs = []
                    if c < NF:
                        for g_, w_ in enumerate((a["moe_w1"], a["moe_w3"])):
                            srcs.append((("gu", g_), w_[0, bass.ds(e, 1), :, c * FC:(c + 1) * FC].rearrange("o (k p) n -> p (o k) n", p=P)))
                    if c:
                        srcs.append((("down", 0), a["moe_w2"][0, bass.ds(e, 1), (c - 1) * FC:c * FC, :].rearrange("o (k p) n -> p (o k) n", p=P)))
                    for load, src in srcs:
                        sp.dma_start(slot_view(s, load), src).then_inc(e_arrived[s], 16)
            sp.wait_ge(e_down, n_pass * NF + NF)

        N_X = 3 + 4

        @block.sync
        def _(sp):
            sp.dma_start(x[:], a["x"][0].rearrange("(t p) d -> p t d", p=P)).then_inc(x_in, 16)
            last = [None] * NSLOT
            for item in items:
                if item == "experts":
                    for s in range(NSLOT):
                        sp.wait_ge(*last[s])
                    expert_weights(sp)
                    last = [None] * NSLOT
                    continue
                s, loads, free = item
                if last[s] is not None:
                    sp.wait_ge(*last[s])
                for load in loads:
                    sp.dma_start(slot_view(s, load), load[2]).then_inc(arrived[s], 16)
                last[s] = free
            if stop is None:
                sp.wait_ge(x_ready, N_X)
            elif n_layers == 2 and has_ffn(1):
                sp.wait_ge(xn_ready, 10)
            elif has_ffn(n_layers - 1):
                sp.wait_ge(x_ready, n_layers)
            else:
                sp.wait_ge(dve_emptied, BK[n_layers - 1].emptied(("wout", 1, 1))[1])
            sp.dma_start(out[0].rearrange("(t p) d -> p t d", p=P), x[:]).then_inc(stored, 16)
            sp.wait_ge(stored, 16)

        N_PARAMS = 5 + 2 * 7
        @block.gpsimd
        def _(pool):
            pool.dma_start(cst[:], cdram[:, :]).then_inc(params_in, 16)
            pool.memset(rows[:], 0.0).then_inc(ea_ready, 1)
            pool.wait_ge(ea_ready, 1)
            for L in range(2):
                o = 50 * L
                pool.dma_start(rows[o:o + 24, :], a["ssd_conv_w"][L].rearrange("k (b c) -> (k b) c", c=P)).then_inc(params_in, 16)
                pool.dma_start(rows[o + 24:o + 30, :], a["ssd_conv_b"][L].rearrange("(b c) -> b c", c=P)).then_inc(params_in, 16)
                pool.dma_start(rows[o + 30:o + 46, :], a["ml_conv_w"][L].rearrange("k (b c) -> (k b) c", c=P)).then_inc(params_in, 16)
                pool.dma_start(rows[o + 46:o + 50, :], a["ml_conv_b"][L].rearrange("(b c) -> b c", c=P)).then_inc(params_in, 16)
            for l in range(2):
                o = 100 + 12 * l
                pool.dma_start(rows[o:o + 6, :], a["conv_w_2"][l].rearrange("k o (b c) -> (k o b) c", c=P)).then_inc(params_in, 16)
                pool.dma_start(rows[o + 6:o + 8, :], a["pool_scale_2"][l].rearrange("(b c) -> b c", c=P)).then_inc(params_in, 16)
                pool.dma_start(rows[o + 8:o + 12, :], a["sgu_b_2"][l]).then_inc(params_in, 16)
            off = 0
            for name, n in (("ssd_dt_bias", 4), ("ssd_a_log", 4), ("ssd_d", 4), ("ml_b_i", 4), ("ml_b_f", 4), ("gla_b_alpha", P)):
                pool.dma_start(bc[:, :, off:off + n], a[name].partition_broadcast(P)).then_inc(params_in, 16)
                off += n
            pool.dma_start(alpha_w[:], a["gla_w_alpha"].rearrange("l r n -> r l n")).then_inc(params_in, 16)

            def load_gain(n, src):
                if n:
                    pool.wait_ge(xn_ready, T * n)
                pool.dma_start(gain[:], src.partition_broadcast(P)).then_inc(gain_in, 16)

            for L in range(n_layers):
                load_gain(2 * L, a["mix_norm_g"][L])
                if L:
                    pool.wait_ge(y_ready, 4 * L)
                for n, name in enumerate(("ret_norm_g", "ssd_norm_g", "gla_norm_g", "ml_norm_g")):
                    pool.dma_start(ygain[:, n * MW:(n + 1) * MW], a[name][L].partition_broadcast(P)).then_inc(ygain_in, 16)
                load_gain(2 * L + 1, a["ffn_norm_g"][L])
            if n_layers == 2 and has_ffn(1):
                pool.wait_ge(merged_ready, 2)
                pool.dma_start(router, a["router_w"][0].rearrange("(k p) e -> p k e", p=P)).then_inc(router_in, 16)
                load_gain(4, a["final_norm_g"])
            if stop is None:
                pool.wait_ge(gla_put, 10)
                pool.dma_start(cst2, cdram2[:, :]).then_inc(cst2_in, 16)
                for l in range(2):
                    L, n = 2 + l, 5 + 4 * l
                    load_gain(n, a["g_pre_mix_2"][l])
                    pool.wait_ge(*((merged_ready, 2 + l)))
                    for lo, w, name in ((0, MW, "g_cq_2"), (MW, P, "g_ckv_2"), (MW + P, MW, "g_sgu_v_2")):
                        pool.dma_start(ygain[:, lo:lo + w], a[name][l].partition_broadcast(P)).then_inc(ygain_in, 16)
                    for aa in range(2):
                        for b_ in range(2):
                            pool.dma_start(pool_w[64 * b_:64 * b_ + 64, aa, :], a["pool_w_2"][l, 2 * aa + b_]).then_inc(pool_in_sem, 16)
                    pool.wait_ge(filled, BK[L].filled(("turn", 3)))
                    pool.dma_start(sgu_w, a["sgu_w_2"][l].rearrange("g i j -> i g j")).then_inc(sgu_in, 16)
                    load_gain(n + 1, a["g_post_mix_2"][l])
                    load_gain(n + 2, a["g_pre_ffn_2"][l])
                    load_gain(n + 3, a["g_post_ffn_2"][l])
        PARAMS_ALL = 16 * (1 + 8 + 6 + 6 + 1)


        @block.tensor
        def _(pe):
            mm, turn = nc.tensor.matmul, nc.tensor.transpose

            def weights(key):
                s, v = find[key]
                pe.wait_ge(arrived[s], v)
                return ring[:, s]

            def open_bank(B, job):
                n = B.index[job]
                if n >= 4:
                    who, v = B.emptied(B.jobs[n - 4])
                    pe.wait_ge(act_emptied if who == "act" else dve_emptied, v)
                return pb[n % 4]

            def turn_jobs(B, first, src, ready):
                for k in range(4):
                    bank = open_bank(B, ("turn", first + k))
                    for i in range(T):
                        pe.wait_ge(*ready(i))
                    for kk in range(2):
                        for i in range(T):
                            ins = turn(bank[:, kk * S + i * P:kk * S + (i + 1) * P],
                                       src[:, i, (2 * k + kk) * P:(2 * k + kk + 1) * P], ident)
                    ins.then_inc(filled, 1)

            def proj_job(B, job, w, chunk_lo, width, spec):
                bank = open_bank(B, job)
                wv = w[:, 0:KD * width].rearrange("p (k n) -> p k n", k=KD)
                if spec[0] == "ch":
                    for n, (col, m) in enumerate(spec[1]):
                        for k in range(KD):
                            ins = mm(bank[0:m, n * S:(n + 1) * S], wv[:, k, col - chunk_lo:col - chunk_lo + m], hT[:, k, :],
                                     start=k == 0, stop=k == KD - 1)
                elif spec[0] == "tok":
                    _, i, col, m = spec
                    for k in range(KD):
                        ins = mm(bank[:, 0:m], hT[:, k, i * P:(i + 1) * P], wv[:, k, col - chunk_lo:col - chunk_lo + m],
                                 start=k == 0, stop=k == KD - 1)
                else:
                    i = spec[1]
                    for lo, col, m in ((0, SDT, 4), (4, GV, MW)):
                        for k in range(KD):
                            ins = mm(bank[:, lo:lo + m], hT[:, k, i * P:(i + 1) * P], wv[:, k, col - chunk_lo:col - chunk_lo + m],
                                     start=k == 0, stop=k == KD - 1)
                ins.then_inc(filled, 1)

            def acted(B, job):
                who, v = B.emptied(job)
                pe.wait_ge(act_emptied if who == "act" else dve_emptied, v)

            def chunk(L, c):
                lo, n, js = CHUNKS1[c]
                w = weights((L, "proj", c))
                for j, spec in enumerate(js):
                    proj_job(BK[L], ("proj", c, j), w, lo, n, spec)

            def gate(L, b, h, i):
                w = weights((L, "gate", b, h))
                proj_job(BK[L], ("gate", b, h, i), w, 0, 512, ("tok", i, 0, 512))

            def merge(L, b):
                bank = open_bank(BK[L], ("yturn", b))
                pe.wait_ge(y_ready, 4 * L + b + 1)
                for kk in range(2):
                    for i in range(T):
                        ins = turn(bank[:, kk * S + i * P:kk * S + (i + 1) * P], y[:, i, kk * P:(kk + 1) * P], ident)
                ins.then_inc(filled, 1)
                w = weights((L, "branch", b))[:, 0:2 * D].rearrange("p (k n) -> p k n", k=2)
                acted(BK[L], ("yturn", b))
                for h in range(2):
                    for i in range(T):
                        bank = open_bank(BK[L], ("merge", b, h, i))
                        for kk in range(2):
                            ins = mm(bank[:], yT[:, b % 2, kk, i * P:(i + 1) * P], w[:, kk, h * 512:(h + 1) * 512],
                                     start=kk == 0, stop=kk == 1)
                        ins.then_inc(filled, 1)

            def score_head(bank, kT, qT):
                mm(bank[:, 0:S], kT[:, 0:P], qT, start=True, stop=True)
                return mm(bank[:, S:S + P], kT[:, P:S], qT[:, P:S], start=True, stop=True)

            def weigh_values(banks, v, w=64, extra=None):
                for i in range(T):
                    for h in range(NH):
                        parts = [(0, i * P)] + ([(1, S)] if i else [])
                        for n, (j, at) in enumerate(parts):
                            ins = mm(banks[i][:, h * w:(h + 1) * w], probs[:, h, at:at + P], v(j, h),
                                     start=n == 0, stop=n == len(parts) - 1)
                        if extra is not None:
                            for n, (j, at) in enumerate(parts):
                                ins = mm(banks[i][:, extra + h:extra + h + 1], probs[:, h, at:at + P], ones[:, 0:1],
                                         start=n == 0, stop=n == len(parts) - 1)
                ins.then_inc(pv_mm, 1)

            def mixers(L):
                B = BK[L]
                acted(B, ("proj", 2, 1))
                if L:
                    pe.wait_ge(gla_put, 5 * L)
                for i in range(T):
                    ins = mm(mb[0][:, i * P:(i + 1) * P], ch_in[0:RANK, 12, i * P:(i + 1) * P], alpha_w[:, L, :],
                             start=True, stop=True)
                ins.then_inc(alpha_mm, 1)
                chunk(L, 6)
                pe.wait_ge(soft_ready, L + 1)
                for i in range(T):
                    for j in range(i + 1):
                        mm(mb[0][:, i * P:(i + 1) * P], soft[:, j, 8:136], tri if j == i else ones, start=j == 0, stop=j == i)
                for i in range(T):
                    for j in range(i + 1):
                        ins = mm(mb[0][:, S + 4 * i:S + 4 * i + 4], tri if j == i else ones, soft[:, j, 4:8], start=j == 0, stop=j == i)
                ins.then_inc(cums_mm, 1)
                pe.wait_ge(conv_ready, 2 * L + 1)
                for kk in range(2):
                    for i in range(T):
                        ins = turn(mb[1][:, i * MW + kk * P:i * MW + (kk + 1) * P], conv[:, kk, i * P:(i + 1) * P], ident)
                ins.then_inc(xs_mm, 1)
                chunk(L, 7)
                pe.wait_ge(wseg_ready, L + 1)
                pe.wait_ge(g_ready, L + 1)
                pe.wait_ge(e_ready, L + 1)
                pe.wait_ge(xdt_ready, L + 1)
                for h in range(NH):
                    m = mb[h]
                    mm(m[:, 0:P], w_seg[:, h, 0], tri, start=True, stop=False)
                    mm(m[:, 0:P], ident, const("negmask"), start=False, stop=True)
                    mm(m[:, P:S], w_seg[:, h, 0], ones, start=True, stop=False)
                    mm(m[:, P:S], w_one[:, h], tri, start=False, stop=True)
                    mm(m[:, S:S + P], w_seg[:, h, 1], tri, start=True, stop=False)
                    mm(m[:, S:S + P], ident, const("negmask"), start=False, stop=True).then_inc(seg_mm, 1)
                gate(L, 0, 0, 0)
                gate(L, 0, 0, 1)
                pe.wait_ge(seg_exp, 4 * (L + 1))
                for g in range(2):
                    ins = score_head(mb[g], conv[:, 2 + g, :], conv[:, 4 + g, :])
                ins.then_inc(scores_mm, 1)
                gate(L, 0, 1, 0)
                pe.wait_ge(probs_ready, 3 * L + 1)
                weigh_values(mb[2:4], lambda j, h: xdt[:, j, h * 64:(h + 1) * 64])
                for i in range(T):
                    ins = turn(mb[0][0:NH, i * P:(i + 1) * P], e_tok[:, 4 * i:4 * i + 4], ident)
                ins.then_inc(et_mm, 1)
                gate(L, 0, 1, 1)
                pe.wait_ge(mt_ready, L + 1)
                pe.wait_ge(o_read, 4 * L + 1)
                for h in range(NH):
                    m = mb[h]
                    mt = mrow[:, 1]
                    mm(m[:, 0:P], head_sel[0:NH, h], mt[:, 0:P], start=True, stop=False)
                    mm(m[:, 0:P], ident, const("bigmask"), start=False, stop=True)
                    mm(m[:, P:S], head_sel[0:NH, h], mt[:, P:S], start=True, stop=True)
                    mm(m[:, S:S + P], head_sel[0:NH, h], mt[:, P:S], start=True, stop=False)
                    ins = mm(m[:, S:S + P], ident, const("bigmask"), start=False, stop=True)
                    if h == 0:
                        for i in range(T):
                            ins = turn(m[:, 384 + 4 * i:388 + 4 * i], mt[:, i * P:(i + 1) * P], ident[0:NH, 0:NH])
                    ins.then_inc(mbc_mm, 1)
                gate(L, 1, 0, 0)
                gate(L, 1, 0, 1)
                pe.wait_ge(ml_arg, 4 * (L + 1))
                pe.wait_ge(conv_ready, 2 * L + 2)
                for h in range(NH):
                    r = 64 * (h % 2)
                    ins = score_head(mb[h], conv[r:r + 64, 8 + h // 2, :], conv[r:r + 64, 6 + h // 2, :])
                ins.then_inc(scores_mm, 1)
                gate(L, 1, 1, 0)
                pe.wait_ge(probs_ready, 3 * L + 2)
                weigh_values(mb[0:2], lambda j, h: u_ml[:, j, h * 64:(h + 1) * 64], extra=MW)
                pe.wait_ge(rot_ready, L + 1)
                for n in range(4):
                    for i in range(T):
                        ins = turn(mb[2 + n // 2][:, (n % 2) * S + i * P:(n % 2) * S + (i + 1) * P],
                                   u_ret[:, i, n * P:(n + 1) * P], ident)
                ins.then_inc(qkt_mm, 1)
                gate(L, 1, 1, 1)
                merge(L, 0)
                pe.wait_ge(qkt_ready, L + 1)
                pe.wait_ge(o_read, 4 * L + 2)
                for h in range(NH):
                    r = 64 * (h % 2)
                    ins = score_head(mb[h], ret_qk[r:r + 64, 2 + h // 2, :], ret_qk[r:r + 64, h // 2, :])
                ins.then_inc(scores_mm, 1)
                gate(L, 2, 0, 0)
                gate(L, 2, 0, 1)
                pe.wait_ge(probs_ready, 3 * L + 3)
                weigh_values(mb[0:2], lambda j, h: u_ret[:, j, 512 + h * 64:512 + (h + 1) * 64])
                gate(L, 2, 1, 0)
                gate(L, 2, 1, 1)
                merge(L, 1)
                pe.wait_ge(o_read, 4 * L + 3)
                for rnd in range(5):
                    if rnd in (0, 2):
                        pe.wait_ge(gla_kq, 2 * L + rnd // 2 + 1)
                    if rnd:
                        pe.wait_ge(gla_put, 5 * L + rnd)
                    for h in range(NH):
                        r = slice(32 * h, 32 * h + 32)
                        if rnd < 4:
                            for s_ in range(2):
                                lev = 2 * rnd + s_
                                for i in range(T):
                                    t_ = slice(i * P, (i + 1) * P)
                                    kk, qq = (gla_k[r, lev % 4, t_], gla_q[r, lev % 4, t_]) if lev < 7 else (
                                        ch_in[r, 11, t_], ch_in[r, 10, t_])
                                    ins = mm(mb[h][:, s_ * S + i * P:s_ * S + (i + 1) * P], kk, qq, start=True, stop=True,
                                             tile_position=(32 * h, 0))
                        else:
                            ins = mm(mb[h][:, 0:P], gla_k[r, 3, 0:P], gla_q[r, 3, P:S], start=True, stop=True,
                                     tile_position=(32 * h, 0))
                    ins.then_inc(gla_mm, 1)
                    if rnd < 4:
                        gate(L, 3, rnd // 2, rnd % 2)
                merge(L, 2)
                pe.wait_ge(gla_put, 5 * L + 5)
                weigh_values(mb[0:2], lambda j, h: u_gla[:, j, 4 + h * 64:4 + (h + 1) * 64])
                merge(L, 3)

            def ffn(u):
                for c in range(NF + 1):
                    g = u * NF + c
                    if c:
                        for i in range(T):
                            pe.wait_ge(h_ready, T * g - T + i + 1)
                        for kk in range(2):
                            for i in range(T):
                                ins = turn(mb[2][:, kk * S + i * P:kk * S + (i + 1) * P], fh[:, i, kk * P:(kk + 1) * P], ident)
                        ins.then_inc(ht_mm, 1)
                    w = weights((u_key[u], c))
                    if c < NF:
                        gu = w[:, 0:KD * 2 * FC].rearrange("p (k n) -> p k n", k=KD)
                        for i in range(T):
                            for k in range(KD):
                                ins = mm(mb[i][:], hT[:, k, i * P:(i + 1) * P], gu[:, k], start=k == 0, stop=k == KD - 1)
                            ins.then_inc(gu_mm, 1)
                    if c:
                        dn = w[:, KD * 2 * FC:SLOTW].rearrange("p (k n) -> p k n", k=2)
                        pe.wait_ge(ht_ready, g)
                        for i in range(T):
                            for h in range(2):
                                for kk in range(2):
                                    ins = mm(pb[2 * i + h][:], fhT[:, kk, i * P:(i + 1) * P], dn[:, kk, h * 512:(h + 1) * 512],
                                             start=c == 1 and kk == 0, stop=c == NF and kk == 1)
                        ins.then_inc(ffn_mm, 1)

            def experts():
                pe.wait_ge(router_in, 16)
                for i in range(T):
                    for k in range(KD):
                        ins = mm(mb[0][:, NE * i:NE * i + NE], hT[:, k, i * P:(i + 1) * P], router[:, k], start=k == 0, stop=k == KD - 1)
                ins.then_inc(logits_mm, 1)
                pe.wait_ge(both_ready, 1)
                mm(mb[1][:, 0:NE], tri, both[:, 0], start=True, stop=True)
                for lo, l0, l1 in ((NE, ones, tri), (2 * NE, ones, ones)):
                    mm(mb[1][:, lo:lo + NE], l0, both[:, 0], start=True, stop=False)
                    ins = mm(mb[1][:, lo:lo + NE], l1, both[:, 1], start=False, stop=True)
                ins.then_inc(rank_mm, 1)
                pe.wait_ge(diag_ready, 1)
                for q in range(4):
                    for i in range(T):
                        ins = mm(mb[2 + q // 2][:, (q % 2) * S + i * P:(q % 2) * S + (i + 1) * P], ones, diag[:, q, i], start=True, stop=True)
                ins.then_inc(quad_mm, 1)
                pe.wait_ge(zero_ready, 1)
                for n in range(4):
                    ins = mm(pb[n][:], ident, scratch[:], start=True, stop=False, skip_group_check=True)
                    if n == 2:
                        ins.then_inc(scatter_mm, 1)
                    if n == 3:
                        ins.then_inc(e_down, NF)
                n_pass = passes(pe)
                with pe.Fori(0, n_pass) as t:
                    pe.wait_ge(sel_ready, t + 1)
                    for k in range(KD):
                        for i in range(T):
                            ins = mm(mb[3 - k // 4][:, (k % 4) * P:(k % 4 + 1) * P], xn[:, i, k * P:(k + 1) * P], sel[:, i],
                                     start=i == 0, stop=i == T - 1)
                    ins.then_inc(gather_mm, 1)
                    pe.wait_ge(xg_ready, t + 1)
                    for c in range(NF + 1):
                        if c:
                            pe.wait_ge(e_h, t * NF + c)
                            for kk in range(2):
                                ins = turn(mb[3][:, kk * P:(kk + 1) * P], fh[:, 0, kk * P:(kk + 1) * P], ident)
                            ins.then_inc(e_ht_mm, 1)
                        pe.wait_ge(e_arrived[c % NSLOT], e_landed(t, c))
                        w = ring[:, c % NSLOT]
                        if c < NF:
                            gu = w[:, 0:KD * 2 * FC].rearrange("p (k n) -> p k n", k=KD)
                            for k in range(KD):
                                ins = mm(mb[2][:], xg[:, k], gu[:, k], start=k == 0, stop=k == KD - 1)
                            ins.then_inc(e_gu, 1)
                        if c:
                            dn = w[:, KD * 2 * FC:SLOTW].rearrange("p (k n) -> p k n", k=2)
                            pe.wait_ge(e_ht, t * NF + c)
                            for h in range(2):
                                for kk in range(2):
                                    ins = mm(mb[h][:], fhT[:, 0, kk * P:(kk + 1) * P], dn[:, kk, h * 512:(h + 1) * 512],
                                             start=c == 1 and kk == 0, stop=c == NF and kk == 1)
                            ins.then_inc(e_down, 1)
                    pe.wait_ge(ys_ready, 2 * t + 2)
                    pe.wait_ge(selT_ready, t + 1)
                    for i in range(T):
                        for h in range(2):
                            ins = mm(pb[2 * i + h][:], selT[:, i * P:(i + 1) * P], ys[:, h * 512:(h + 1) * 512], start=False,
                                     stop=False, skip_group_check=True)
                    ins.then_inc(scatter_mm, 1)
                for n in range(4):
                    ins = mm(pb[n][:], ident, scratch[:], start=False, stop=True, skip_group_check=True)
                ins.then_inc(moe_mm, 1)

            def gate2(L, b, *ns):
                for n in ns:
                    gate(L, b, n // 2, n % 2)

            def chunk2(L, c):
                lo, n, js = CHUNKS2[c]
                w = weights((L, "proj", c))
                for j, spec in enumerate(js):
                    proj_job(BK[L], ("proj", c, j), w, lo, n, spec)

            def merge2(L, b, src, n_k):
                w = weights((L, "branch", b))[:, 0:n_k * D].rearrange("p (k n) -> p k n", k=n_k)
                for h in range(2):
                    for i in range(T):
                        bank = open_bank(BK[L], ("merge", b, h, i))
                        for kk in range(n_k):
                            ins = mm(bank[:], src[:, kk, i * P:(i + 1) * P], w[:, kk, h * 512:(h + 1) * 512],
                                     start=kk == 0, stop=kk == n_k - 1)
                        ins.then_inc(filled, 1)

            def y_turn(L, b, n, src):
                job = ("yturn", b, n)
                bank = open_bank(BK[L], job)
                for kk in range(2):
                    for i in range(T):
                        ins = turn(bank[:, kk * S + i * P:kk * S + (i + 1) * P], src[:, i, (2 * n + kk) * P:(2 * n + kk + 1) * P], ident)
                ins.then_inc(filled, 1)

            def scores2(l, g):
                for hh in range(4):
                    h = 4 * g + hh
                    for n, (i, j) in enumerate(((0, 0), (1, 0), (1, 1))):
                        o = mb[hh][:, n * P:(n + 1) * P]
                        it, jt = slice(i * P, (i + 1) * P), slice(j * P, (j + 1) * P)
                        ins = mm(o, qT[:, h, it], kT[:, h, jt], start=True, stop=i != j)
                        if i == j:
                            ins = mm(o, const2("rowmask")[0:1, :], const2("colmask")[0:1, :], start=False, stop=True)
                    ins.then_inc(att_mm, 1)

            def turn_probs(l, g):
                for hh in range(4):
                    pe.wait_ge(att_exp, 8 * (2 * l + g) + 2 * hh + 2)
                    for n in range(3):
                        ins = turn(mb[hh][:, n * P:(n + 1) * P], probs[:, hh, n * P:(n + 1) * P], ident)
                    ins.then_inc(probsT_mm, 1)

            def att_values(l, g):
                pe.wait_ge(probsT_ready, 2 * l + g + 1)
                for i in range(T):
                    for hh in range(4):
                        parts = [(0, i * P)] + ([(1, S)] if i else [])
                        for n, (j, at) in enumerate(parts):
                            ins = mm(mb[i][:, hh * VH:(hh + 1) * VH], probsT[:, hh, at:at + P],
                                     v_tok[:, j, (4 * g + hh) * VH:(4 * g + hh + 1) * VH], start=n == 0, stop=n == len(parts) - 1)
                ins.then_inc(av_mm, 1)

            def mixers2(l):
                L = 2 + l
                B = BK[L]
                chunk2(L, 0)
                chunk2(L, 1)
                if l == 0:
                    pe.wait_ge(cst2_in, 16)
                acted(B, ("proj", 1, 1))
                for g in range(4):
                    r = slice(64 * (g % 2), 64 * (g % 2) + 64)
                    c0 = (g // 2) * S
                    z = lambda j: pool_in[:, j, g * 64:(g + 1) * 64]
                    mm(mb[0][r, c0:c0 + P], z(0), window[:, g, 0:P], start=True, stop=True)
                    mm(mb[0][r, c0 + P:c0 + S], z(0), window[:, g, P:S], start=True, stop=False)
                    ins = mm(mb[0][r, c0 + P:c0 + S], z(1), window[:, g, S:384], start=False, stop=True)
                ins.then_inc(pooled_mm, 1)
                chunk2(L, 2)
                pe.wait_ge(lat_ready, l + 1)
                for kk in range(2):
                    for i in range(T):
                        turn(mb[1][:, kk * S + i * P:kk * S + (i + 1) * P], lat[:, i, kk * P:(kk + 1) * P], ident)
                for i in range(T):
                    turn(mb[2][:, i * P:(i + 1) * P], lat[:, i, MW:MW + P], ident)
                    ins = turn(mb[2][0:ROPE, S + i * P:S + (i + 1) * P], k_rot[:, i], ident)
                ins.then_inc(latT_mm, 1)
                pe.wait_ge(sgu_in, 16 * (l + 1))
                for g in range(4):
                    ins = turn(mb[3][:, g * P:(g + 1) * P], sgu_w[:, g], ident)
                ins.then_inc(sgu_turned, 1)
                chunk2(L, 3)
                pe.wait_ge(pooled_ready, l + 1)
                pe.wait_ge(pool_in_sem, 64 * (l + 1))
                for g in range(4):
                    r = slice(64 * (g % 2), 64 * (g % 2) + 64)
                    ins = mm(mb[0][r, (g // 2) * S:(g // 2 + 1) * S], pool_w[r, g // 2, :], pooled[r, g // 2, :], start=True, stop=True)
                ins.then_inc(poolT_mm, 1)
                gate2(L, 0, 0, 1)
                pe.wait_ge(latT_ready, l + 1)
                pe.wait_ge(poolT_ready, l + 1)
                pe.wait_ge(sgu_wT_ready, l + 1)
                w = weights((L, "up"))
                w_qn = w[:, UP_QN:UP_QR].rearrange("p (k n) -> p k n", k=2)
                w_qr = w[:, UP_QR:UP_KN].rearrange("p (k n) -> p k n", k=2)
                w_kn, w_v = w[:, UP_KN:UP_V], w[:, UP_V:UP_V + AH * VH]
                for h in range(AH):
                    for k in range(2):
                        ins = mm(mb[h // 2][0:NOPE, (h % 2) * S:(h % 2 + 1) * S], w_qn[:, k, h * NOPE:(h + 1) * NOPE], cqT[:, k],
                                 start=k == 0, stop=k == 1)
                ins.then_inc(qn_mm, 1)
                gate2(L, 0, 2)
                pe.wait_ge(qn_ready, l + 1)
                for h in range(AH):
                    ins = mm(mb[h // 2][0:NOPE, (h % 2) * S:(h % 2 + 1) * S], w_kn[:, h * NOPE:(h + 1) * NOPE], ckvT, start=True, stop=True)
                ins.then_inc(kn_mm, 1)
                gate2(L, 0, 3)
                pe.wait_ge(kn_ready, l + 1)
                for i in range(T):
                    for k in range(2):
                        mm(mb[0][:, i * S:(i + 1) * S], cqT[:, k, i * P:(i + 1) * P], w_qr[:, k], start=k == 0, stop=k == 1)
                    ins = mm(mb[1 + i][:], ckvT[:, i * P:(i + 1) * P], w_v, start=True, stop=True)
                ins.then_inc(qrv_mm, 1)
                pe.wait_ge(vn_ready, l + 1)
                for i in range(T):
                    for g in range(4):
                        ins = mm(mb[3][:, i * MW + g * 64:i * MW + (g + 1) * 64], sgu_wT[:, g], sgu_v[:, i, g * 64:(g + 1) * 64],
                                 start=True, stop=True)
                ins.then_inc(sgu_mm, 1)
                gate2(L, 1, 0, 1)
                pe.wait_ge(q_rot_ready, l + 1)
                for kk in range(2):
                    for i in range(T):
                        ins = turn(mb[0][:, kk * S + i * P:kk * S + (i + 1) * P], q_rot[:, i, kk * P:(kk + 1) * P], ident)
                ins.then_inc(qrT_mm, 1)
                pe.wait_ge(convT_ready, l + 1)
                merge2(L, 0, convT, 2)
                gate2(L, 1, 2)
                pe.wait_ge(qrT_ready, l + 1)
                pe.wait_ge(y_sgu_ready, l + 1)
                scores2(l, 0)
                gate2(L, 1, 3)
                merge2(L, 1, poolT, 2)
                turn_probs(l, 0)
                gate2(L, 2, 0)
                att_values(l, 0)
                gate2(L, 2, 1)
                pe.wait_ge(y_att_ready, 2 * l + 1)
                scores2(l, 1)
                gate2(L, 2, 2, 3)
                turn_probs(l, 1)
                y_turn(L, 2, 0, y_sgu)
                acted(B, ("yturn", 2, 0))
                merge2(L, 2, sguT, 2)
                gate2(L, 3, 0, 1)
                att_values(l, 1)
                gate2(L, 3, 2, 3)
                pe.wait_ge(y_att_ready, 2 * l + 2)
                y_turn(L, 3, 0, y_att)
                y_turn(L, 3, 1, y_att)
                acted(B, ("yturn", 3, 1))
                merge2(L, 3, attT, 4)

            pe.wait_ge(params_in, PARAMS_ALL)
            turn(mb[0][:, 0:P], rows[:], ident).then_inc(rows_turned, 1)
            for L in range(n_layers):
                B = BK[L]
                turn_jobs(B, 0, xn, lambda i: (xn_ready, 4 * L + i + 1))
                for k in range(4):
                    acted(B, ("turn", k))
                if L == 0:
                    pe.wait_ge(perch_ready, 1)
                for c in range(6):
                    chunk(L, c)
                mixers(L)
                turn_jobs(B, 4, merged, lambda i: (merged_ready, L + 1))
                for k in range(4):
                    acted(B, ("turn", 4 + k))
                for h in range(2):
                    w = weights((L, "wout", h))
                    for i in range(T):
                        proj_job(B, ("wout", h, i), w, 0, 512, ("tok", i, 0, 512))
                if not has_ffn(L):
                    break
                turn_jobs(B, 8, xn, lambda i: (xn_ready, 4 * L + 2 + i + 1))
                for k in range(4):
                    acted(B, ("turn", 8 + k))
                if L == 0:
                    ffn(0)
                else:
                    experts()
            if stop is None:
                for l in range(2):
                    L, n = 2 + l, 5 + 4 * l
                    B = BK[L]
                    turn_jobs(B, 0, xn, lambda i: (xn_ready, T * n + i + 1))
                    for k in range(4):
                        acted(B, ("turn", k))
                    mixers2(l)
                    turn_jobs(B, 4, merged, lambda i: (merged_ready, L + 1))
                    for k in range(4):
                        acted(B, ("turn", 4 + k))
                    for h in range(2):
                        w = weights((L, "wout", h))
                        for i in range(T):
                            proj_job(B, ("wout", h, i), w, 0, 512, ("tok", i, 0, 512))
                    turn_jobs(B, 8, xn, lambda i: (xn_ready, T * (n + 2) + i + 1))
                    for k in range(4):
                        acted(B, ("turn", 8 + k))
                    ffn(1 + l)

        @block.scalar
        def _(act):
            f = nc.scalar.activation
            chain = [0]

            def link(ins):
                chain[0] += 1
                ins.then_inc(act_step, 1)
                act.wait_ge(act_step, chain[0])

            def square_sums(n, ready, src=x):
                act.wait_ge(*ready)
                if n:
                    act.wait_ge(xn_ready, T * n)
                for i in range(T):
                    f(merged[:, i, :], src[:, i, :], ACT.Square, accum_out=ssq[:, i:i + 1]).then_inc(squares, 1)

            def empty(B, job, *moves):
                act.wait_ge(filled, B.filled(job))
                for dst, src, fn, sc in moves:
                    ins = f(dst, src, fn, scale=sc)
                ins.then_inc(act_emptied, 1)

            def turned(B, first):
                for k in range(4):
                    bank = pb[B.index[("turn", first + k)] % 4]
                    empty(B, ("turn", first + k), (hT[:, 2 * k:2 * k + 2, :].rearrange("p k s -> p (k s)"), bank[:], ACT.Copy, 1.0))

            def proj(L, c):
                B = BK[L]
                for j, spec in enumerate(CHUNKS1[c][2]):
                    job = ("proj", c, j)
                    bank = pb[B.index[job] % 4]
                    cp = lambda dst, src, fn=ACT.Copy, sc=1.0: (dst, src, fn, sc)
                    if spec[0] == "ch":
                        at = {SX: 0, SB: 2, SC: 4, MQ: 6, MK: 8}
                        col = spec[1][0][0]
                        if col in at:
                            empty(B, job, cp(ch_in[:, at[col]:at[col] + 2].rearrange("p b s -> p (b s)"), bank[:]))
                        elif col == GA:
                            empty(B, job, cp(ch_in[0:RANK, 12], bank[0:RANK, 0:S]))
                        else:
                            empty(B, job, cp(ch_in[:, 10], bank[:, 0:S], sc=32 ** -0.5), cp(ch_in[:, 11], bank[:, S:2 * S]))
                    elif spec[0] == "tok2":
                        i = spec[1]
                        empty(B, job, cp(u_gla[:, i, 0:4 + MW], bank[:, 0:4 + MW]))
                    else:
                        i, col = spec[1], spec[2]
                        if col == SZ:
                            empty(B, job, cp(u_z[:, i, :], bank[:, 0:MW], ACT.Silu))
                        elif col == GR:
                            empty(B, job, cp(u_gla[:, i, 4 + MW:], bank[:, 0:MW], ACT.Silu))
                        elif col == MV:
                            empty(B, job, cp(u_ml[:, i, 0:MW], bank[:, 0:MW]))
                        elif col == MO:
                            empty(B, job, cp(u_ml[:, i, MW:2 * MW], bank[:, 0:MW], ACT.Sigmoid),
                                  cp(u_ml[:, i, 2 * MW:], bank[:, MW:MW + 8]))
                        elif col == RQ:
                            empty(B, job, cp(u_ret[:, i, 0:512], bank[:, 0:512]))
                        else:
                            empty(B, job, cp(u_ret[:, i, 512:768], bank[:, 0:256]), cp(u_ret[:, i, 768:], bank[:, 256:512], ACT.Silu))

            def gate(L, b, h, i):
                job = ("gate", b, h, i)
                B = BK[L]
                if b >= 2:
                    act.wait_ge(dve_emptied, B.emptied(("merge", b - 2, 1, 1))[1])
                empty(B, job, (gates[:, b % 2, i, h * 512:(h + 1) * 512], pb[B.index[job] % 4][:], ACT.Sigmoid, 1.0))

            def yturned(L, b):
                job = ("yturn", b)
                B = BK[L]
                empty(B, job, (yT[:, b % 2].rearrange("p k s -> p (k s)"), pb[B.index[job] % 4][:], ACT.Copy, 1.0))

            def mixers(L):
                act.wait_ge(conv_raw, 2 * L + 1)
                f(conv[:, 0:6].rearrange("p b s -> p (b s)"), conv[:, 0:6].rearrange("p b s -> p (b s)"), ACT.Silu).then_inc(conv_ready, 1)
                proj(L, 3)
                act.wait_ge(conv_raw, 2 * L + 2)
                f(conv[:, 6:10].rearrange("p b s -> p (b s)"), conv[:, 6:10].rearrange("p b s -> p (b s)"), ACT.Silu).then_inc(conv_ready, 1)
                proj(L, 4)
                proj(L, 5)
                proj(L, 6)
                act.wait_ge(sp_abs, L + 1)
                f(sp_tmp[1], sp_tmp[0], ACT.Exp, scale=-1.0).then_inc(sp_exp, 1)
                proj(L, 7)
                act.wait_ge(cums_mm, L + 1)
                f(gT[:], mb[0][:, 0:S], ACT.Copy, scale=-1.0 / 16.0).then_inc(g_ready, 1)
                for h in range(NH):
                    act.wait_ge(seg_mm, 4 * L + h + 1)
                    if L and h == 0:
                        act.wait_ge(pv_mm, 4 * L)
                    f(probs[:, h, :], mb[h][:, 0:384], ACT.Exp).then_inc(seg_exp, 1)
                for h in range(2):
                    for i in range(T):
                        gate(L, 0, h, i)
                act.wait_ge(pv_mm, 4 * L + 1)
                for h in range(NH):
                    act.wait_ge(ml_arg, 4 * L + h + 1)
                    f(probs[:, h, :], probs[:, h, :], ACT.Exp, scale=-1.0).then_inc(ml_exp, 1)
                act.wait_ge(negm_ready, L + 1)
                f(em, negm, ACT.Exp).then_inc(em_ready, 1)
                gate(L, 1, 0, 0)
                gate(L, 1, 0, 1)
                gate(L, 1, 1, 0)
                act.wait_ge(qkt_mm, L + 1)
                for n in range(2):
                    ins = f(ret_qk[:, 2 * n:2 * n + 2].rearrange("p b s -> p (b s)"), mb[2 + n][:], ACT.Copy)
                ins.then_inc(qkt_ready, 1)
                gate(L, 1, 1, 1)
                yturned(L, 0)
                for h in range(2):
                    for i in range(T):
                        gate(L, 2, h, i)
                yturned(L, 1)
                for half in range(2):
                    act.wait_ge(gla_arg, 2 * L + half + 1)
                    f(gla_e.rearrange("p l s -> p (l s)"), gla_e.rearrange("p l s -> p (l s)"), ACT.Exp).then_inc(gla_exp, 1)
                    if half == 0:
                        gate(L, 3, 0, 0)
                        gate(L, 3, 0, 1)
                gate(L, 3, 1, 0)
                gate(L, 3, 1, 1)
                yturned(L, 2)
                yturned(L, 3)

            def ffn(u):
                for c in range(NF + 1):
                    g = u * NF + c
                    if c:
                        act.wait_ge(ht_mm, g)
                        f(fhT[:].rearrange("p k s -> p (k s)"), mb[2][:], ACT.Copy).then_inc(ht_ready, 1)
                    if c < NF:
                        for i in range(T):
                            act.wait_ge(gu_mm, T * g + i + 1)
                            if g:
                                act.wait_ge(h_ready, T * (g - 1) + i + 1)
                            f(fsg[:, i, :], mb[i][:, 0:FC], ACT.Silu).then_inc(silu_done, 1)

            def experts():
                act.wait_ge(ex_arg, 1)
                f(ex, ex, ACT.Exp).then_inc(ex_ready, 1)
                n_pass = passes(act)
                with act.Fori(0, n_pass) as t:
                    act.wait_ge(gather_mm, t + 1)
                    for n in range(2):
                        ins = f(xg[:, 4 * n:4 * n + 4].rearrange("p k s -> p (k s)"), mb[3 - n][:], ACT.Copy)
                    ins.then_inc(xg_ready, 1)
                    for c in range(NF + 1):
                        if c:
                            act.wait_ge(e_ht_mm, t * NF + c)
                            f(fhT[:, 0, :], mb[3][:, 0:2 * P], ACT.Copy).then_inc(e_ht, 1)
                        if c < NF:
                            act.wait_ge(e_gu, t * NF + c + 1)
                            f(fsg[:, 0, :], mb[2][:, 0:FC], ACT.Silu).then_inc(e_silu, 1)
                    act.wait_ge(e_down, t * NF + 2 * NF)
                    f(ys[:, 0:512], mb[0][:], ACT.Copy).then_inc(ys_ready, 1)

            def evac2(L, c):
                B = BK[L]
                flat2 = lambda t_: t_.rearrange("p b s -> p (b s)")
                for j, spec in enumerate(CHUNKS2[c][2]):
                    job = ("proj", c, j)
                    bank = pb[B.index[job] % 4]
                    if spec[0] == "ch":
                        dst = {CB: conv_b, CC: conv_c, CX: conv_x}[spec[1][0][0]]
                        empty(B, job, (flat2(dst), bank[:], ACT.Copy, 1.0))
                    else:
                        i, col, w = spec[1:]
                        dst = {CQ: u_ret[:, i, 0:416], PI: u_ret[:, i, 512:1024], SV: sgu_v[:, i]}[col]
                        empty(B, job, (dst, bank[:, 0:w], ACT.Copy, 1.0))

            def gate2(L, b, *ns):
                B = BK[L]
                for n in ns:
                    job = ("gate", b, n // 2, n % 2)
                    if b >= 2:
                        act.wait_ge(dve_emptied, B.emptied(("merge", b - 2, 1, 1))[1])
                    empty(B, job, (gates[:, b % 2, n % 2, (n // 2) * 512:(n // 2 + 1) * 512], pb[B.index[job] % 4][:], ACT.Sigmoid, 1.0))

            def att_exps(l, g):
                for hh in range(4):
                    act.wait_ge(att_max, 4 * (2 * l + g) + hh + 1)
                    for i, (lo, hi) in enumerate(((0, P), (P, 384))):
                        c = 2 * hh + i
                        f(probs[:, hh, lo:hi], mb[hh][:, lo:hi], ACT.Exp, bias=nmx[:, c:c + 1], scale=(NOPE + ROPE) ** -0.5,
                          accum_out=sums[:, c:c + 1]).then_inc(att_exp, 1)

            def mixers2(l):
                L = 2 + l
                B = BK[L]
                evac2(L, 0)
                evac2(L, 1)
                act.wait_ge(pooled_mm, l + 1)
                f(pooled[:].rearrange("p t n -> p (t n)"), mb[0][:], ACT.Copy).then_inc(pooled_ready, 1)
                evac2(L, 2)
                act.wait_ge(latT_mm, l + 1)
                f(cqT.rearrange("p b s -> p (b s)"), mb[1][:], ACT.Copy)
                f(ckvT, mb[2][:, 0:S], ACT.Copy)
                f(kT[NOPE:NOPE + ROPE], mb[2][0:ROPE, S:2 * S].unsqueeze(1).to_broadcast([ROPE, AH, S]), ACT.Copy).then_inc(latT_ready, 1)
                evac2(L, 3)
                act.wait_ge(poolT_mm, l + 1)
                for aa in range(2):
                    o = 100 + 12 * l + 6 + aa
                    ins = f(poolT[:, aa], mb[0][:, aa * S:(aa + 1) * S], ACT.Copy, scale=perch[:, o:o + 1])
                ins.then_inc(poolT_ready, 1)
                gate2(L, 0, 0, 1)
                for done, ready, dst in ((qn_mm, qn_ready, qT), (kn_mm, kn_ready, kT)):
                    act.wait_ge(done, l + 1)
                    for n in range(4):
                        ins = f(dst[0:NOPE, 2 * n:2 * n + 2], mb[n][0:NOPE, :].rearrange("p (h s) -> p h s", h=2), ACT.Copy)
                    ins.then_inc(ready, 1)
                    gate2(L, 0, 2 if done is qn_mm else 3)
                act.wait_ge(qrv_mm, l + 1)
                f(q_rope[:].rearrange("p t n -> p (t n)"), mb[0][:], ACT.Copy)
                for i in range(T):
                    ins = f(v_tok[:, i], mb[1 + i][:], ACT.Copy)
                ins.then_inc(qrv_ready, 1)
                gate2(L, 1, 0, 1)
                act.wait_ge(qrT_mm, l + 1)
                for hh in range(4):
                    ins = f(qT[NOPE:NOPE + ROPE, hh:AH:4], mb[0][32 * hh:32 * hh + 32, :].rearrange("p (g s) -> p g s", g=2), ACT.Copy)
                ins.then_inc(qrT_ready, 1)
                gate2(L, 1, 2)
                att_exps(l, 0)
                gate2(L, 1, 3)
                gate2(L, 2, 0, 1)
                act.wait_ge(probsT_mm, 8 * l + 4)
                att_exps(l, 1)
                gate2(L, 2, 2, 3)
                job = ("yturn", 2, 0)
                empty(B, job, (sguT.rearrange("p k s -> p (k s)"), pb[B.index[job] % 4][:], ACT.Copy, 1.0))
                gate2(L, 3, 0, 1, 2, 3)
                for n in range(2):
                    job = ("yturn", 3, n)
                    empty(B, job, (attT[:, 2 * n:2 * n + 2].rearrange("p k s -> p (k s)"), pb[B.index[job] % 4][:], ACT.Copy, 1.0))

            act.wait_ge(params_in, PARAMS_ALL)
            f(ea[:], bc[:, :, 4:8], ACT.Exp).then_inc(ea_ready, 1)
            for L in range(n_layers):
                square_sums(2 * L, (x_in, 16) if L == 0 else (x_ready, L))
                turned(BK[L], 0)
                for c in range(3):
                    proj(L, c)
                mixers(L)
                turned(BK[L], 4)
                if not has_ffn(L):
                    break
                square_sums(2 * L + 1, (dve_emptied, BK[L].emptied(("wout", 1, 1))[1]))
                turned(BK[L], 8)
                if L == 0:
                    ffn(0)
                else:
                    experts()
                    square_sums(4, (x_ready, 2))
            if stop is None:
                for l in range(2):
                    L, n = 2 + l, 5 + 4 * l
                    square_sums(n, (x_ready, 3 + 2 * l))
                    turned(BK[L], 0)
                    mixers2(l)
                    turned(BK[L], 4)
                    square_sums(n + 1, (dve_emptied, BK[L].emptied(("wout", 1, 1))[1]), xn)
                    square_sums(n + 2, (x_ready, 4 + 2 * l))
                    turned(BK[L], 8)
                    ffn(1 + l)
                    square_sums(n + 3, (post_in, l + 1), xn)

        @block.vector
        def _(v):
            tt, ts, stt, cp = nc.vector.tensor_tensor, nc.vector.tensor_scalar, nc.vector.scalar_tensor_tensor, nc.vector.tensor_copy
            chain = [0]

            def link(ins):
                chain[0] += 1
                ins.then_inc(dve_step, 1)
                v.wait_ge(dve_step, chain[0])

            def acted(B, job):
                v.wait_ge(act_emptied, B.emptied(job)[1])

            def rsqrt(r, m):
                t = r_tmp[:, 0:m.shape[1]]
                link(ts(r.bitcast(I32), m.bitcast(I32), 1, None, ALU.arith_shift_right))
                link(ts(r.bitcast(I32), r.bitcast(I32), -1.0, float(0x5F3759DF), ALU.mult, ALU.add))
                for _ in range(3):
                    link(tt(t, r, r, ALU.mult))
                    link(stt(out=t, in0=t, scalar=-0.5, in1=m, op0=ALU.mult, op1=ALU.mult))
                    link(stt(out=r, in0=t, scalar=1.5, in1=r, op0=ALU.add, op1=ALU.mult))

            def norm(n, dst=xn):
                v.wait_ge(squares, T * (n + 1))
                link(ts(r_in, ssq, 1.0 / D, EPS, ALU.mult, ALU.add))
                rsqrt(rstd, r_in)
                v.wait_ge(gain_in, 16 * (n + 1))
                for i in range(T):
                    stt(out=dst[:, i, :], in0=x[:, i, :], scalar=rstd[:, i:i + 1], in1=gain[:], op0=ALU.mult,
                        op1=ALU.mult).then_inc(xn_ready, 1)

            def convolve(L, first, count, wcol, bcol):
                for b in range(count):
                    blk, o = first + b, 50 * L
                    w = lambda k: perch[:, o + wcol + k * count + b:o + wcol + k * count + b + 1]
                    link(ts(conv[:, blk, :], ch_in[:, blk, :], w(3), perch[:, o + bcol + b:o + bcol + b + 1], ALU.mult, ALU.add))
                    for s in range(1, 4):
                        ins = stt(out=conv[:, blk, s:S], in0=ch_in[:, blk, 0:S - s], scalar=w(3 - s), in1=conv[:, blk, s:S],
                                  op0=ALU.mult, op1=ALU.add)
                        if s < 3:
                            link(ins)
                        elif b < count - 1:
                            link(ins)
                ins.then_inc(conv_raw, 1)

            def softplus(L):
                X = soft[:].rearrange("p t n -> p (t n)")
                b = bc[:, L]
                link(tt(soft[:, :, 0:4], u_gla[:, :, 0:4], b[:, 0:4].unsqueeze(1).to_broadcast([P, T, 4]), ALU.add))
                for lo, n, src, bias in ((4, 4, u_ml[:, :, 2 * MW + 4:2 * MW + 8], b[:, 16:20]),
                                         (8, P, mb[0][:, 0:S].rearrange("p (t n) -> p t n", t=T), b[:, 20:148])):
                    link(stt(out=soft[:, :, lo:lo + n], in0=src, scalar=-1.0, in1=bias.unsqueeze(1).to_broadcast([P, T, n]),
                             op0=ALU.mult, op1=ALU.subtract))
                stt(out=sp_tmp[0], in0=X, scalar=-1.0, in1=X, op0=ALU.mult, op1=ALU.max).then_inc(sp_abs, 1)
                v.wait_ge(sp_exp, L + 1)
                z, t2, s1, s2, q = sp_tmp[1], sp_tmp[2], sp_tmp[3], sp_tmp[4], sp_tmp[5]
                link(ts(t2, z, 2.0, None, ALU.add))
                link(nc.vector.reciprocal(t2, t2))
                link(tt(s1, z, t2, ALU.mult))
                link(tt(s2, s1, s1, ALU.mult))
                link(ts(q, s2, 1.0 / 15.0, None, ALU.mult))
                for d in (13, 11, 9, 7, 5, 3):
                    link(stt(out=q, in0=q, scalar=1.0 / d, in1=s2, op0=ALU.add, op1=ALU.mult))
                link(stt(out=q, in0=q, scalar=1.0, in1=s1, op0=ALU.add, op1=ALU.mult))
                link(ts(X, X, 0.0, None, ALU.max))
                stt(out=X, in0=q, scalar=2.0, in1=X, op0=ALU.mult, op1=ALU.add).then_inc(soft_ready, 1)
                v.wait_ge(soft_ready, L + 1)

            def head_norm(L, b, branch, act_gate, whole):
                n = 1 if whole else NH
                w = MW // n
                sq = scratch[:].rearrange("p (t n) -> p t n", t=T)
                link(tt(sq, y[:], y[:], ALU.mult))
                ss, rr = hs[:, 0:T * n], hr[:, 0:T * n]
                link(nc.vector.tensor_reduce(ss, scratch[:].rearrange("p (g w) -> p g w", w=w), AX.X, ALU.add))
                link(ts(ss, ss, 1.0 / w, EPS, ALU.mult, ALU.add))
                rsqrt(rr, ss)
                yv = y[:].rearrange("p t (h w) -> p (t h) w", h=n)
                link(tt(yv, yv, rr.unsqueeze(2).to_broadcast([P, T * n, w]), ALU.mult))
                v.wait_ge(ygain_in, 64 * (L + 1))
                gb = ygain[:, branch * MW:(branch + 1) * MW].unsqueeze(1).to_broadcast([P, T, MW])
                if act_gate is not None:
                    link(tt(y[:], y[:], gb, ALU.mult))
                    tt(y[:], y[:], act_gate, ALU.mult).then_inc(y_ready, 1)
                else:
                    tt(y[:], y[:], gb, ALU.mult).then_inc(y_ready, 1)
                v.wait_ge(y_ready, 4 * L + b + 1)

            def take_y(L, b):
                v.wait_ge(pv_mm, 4 * L + b + 1)
                if b:
                    v.wait_ge(filled, BK[L].filled(("yturn", b - 1)))

            def merge(L, b):
                B = BK[L]
                for h in range(2):
                    for i in range(T):
                        job = ("merge", b, h, i)
                        bank = pb[B.index[job] % 4]
                        g = gates[:, b % 2, i, h * 512:(h + 1) * 512]
                        m = merged[:, i, h * 512:(h + 1) * 512]
                        acted(B, ("gate", b, h, i))
                        v.wait_ge(filled, B.filled(job))
                        if b == 0:
                            tt(m, bank[:], g, ALU.mult).then_inc(dve_emptied, 1)
                        else:
                            tt(g, bank[:], g, ALU.mult).then_inc(dve_emptied, 1)
                        v.wait_ge(dve_emptied, B.emptied(job)[1])
                        if b:
                            ins = tt(m, m, g, ALU.add)
                            if (b, h, i) == (3, 1, 1):
                                ins.then_inc(merged_ready, 1)
                            else:
                                link(ins)

            def gla_levels(L, half):
                if half:
                    v.wait_ge(gla_mm, 5 * L + 2)
                for n in range(4):
                    b = 1 << (4 * half + n)
                    g = gT[:].rearrange("p (m s b) -> p m s b", s=2, b=b)
                    e = gla_e[:, n].rearrange("p (m s b) -> p m s b", s=2, b=b)
                    ref = g[:, :, 0, b - 1:b].to_broadcast([P, S // (2 * b), b])
                    tt(e[:, :, 0], ref, g[:, :, 0], ALU.subtract)
                    ins = tt(e[:, :, 1], g[:, :, 1], ref, ALU.subtract)
                ins.then_inc(gla_arg, 1)
                v.wait_ge(gla_exp, 2 * L + half + 1)
                tt(gla_k, gla_e, ch_in[:, 11:12].to_broadcast([P, 4, S]), ALU.mult)
                tt(gla_q, gla_e, ch_in[:, 10:11].to_broadcast([P, 4, S]), ALU.mult).then_inc(gla_kq, 1)

            def gla_put_levels(L, rnd):
                v.wait_ge(gla_mm, 5 * L + rnd + 1)
                for h in range(NH):
                    if rnd == 4:
                        ins = cp(probs[:, h, P:S], mb[h][:, 0:P])
                        continue
                    dst = probs[:, h, :].rearrange("p (a i) -> p a i", i=P)[:, 0:3:2, :]
                    for s_ in range(2):
                        src = mb[h][:, s_ * S:(s_ + 1) * S].rearrange("p (a i) -> p a i", i=P)
                        msk = levmask[:, 2 * rnd + s_].bitcast(U32).unsqueeze(1).to_broadcast([P, T, P])
                        ins = nc.vector.copy_predicated(dst, msk, src)
                        if not (h == NH - 1 and s_ == 1):
                            link(ins)
                ins.then_inc(gla_put, 1)
                v.wait_ge(gla_put, 5 * L + rnd + 1)

            def mixers(L):
                B = BK[L]
                acted(B, ("proj", 0, 0))
                acted(B, ("proj", 1, 1))
                if L:
                    v.wait_ge(pv_mm, 4 * L)
                convolve(L, 0, 6, 0, 24)
                acted(B, ("proj", 3, 0))
                convolve(L, 6, 4, 30, 46)
                acted(B, ("proj", 5, 1))
                v.wait_ge(alpha_mm, L + 1)
                softplus(L)
                v.wait_ge(ea_ready, 2)
                link(stt(out=dA.rearrange("p (t h) -> p t h", t=T), in0=soft[:, :, 0:4], scalar=-1.0,
                         in1=ea[:, L].unsqueeze(1).to_broadcast([P, T, 4]), op0=ALU.mult, op1=ALU.mult))
                dAh = dA.rearrange("p (t h) -> p h t", t=T)
                for t_ in range(T):
                    tt(w_seg[:, :, t_], after.unsqueeze(1).to_broadcast([P, NH, P]),
                       dAh[:, :, t_:t_ + 1].to_broadcast([P, NH, P]), ALU.mult)
                tt(w_one, ones.unsqueeze(1).to_broadcast([P, NH, P]), dAh[:, :, 1:2].to_broadcast([P, NH, P]),
                   ALU.mult).then_inc(wseg_ready, 1)
                acted(B, ("proj", 6, 1))
                for i in range(T):
                    u = u_ret[:, i, 0:512].rearrange("p (g h c) -> p g h c", g=8, h=2)
                    pc = rot_c[:, i].rearrange("p g (h c) -> p g h c", h=2)
                    ps_ = rot_s[:, i].rearrange("p g (h c) -> p g h c", h=2)
                    for h in range(2):
                        tt(pc[:, :, h], u[:, :, h], cosT[:, i].unsqueeze(1).to_broadcast([P, 8, 32]), ALU.mult)
                        link(tt(ps_[:, :, h], u[:, :, h], sinT[:, i].unsqueeze(1).to_broadcast([P, 8, 32]), ALU.mult))
                    tt(u[:, :, 0], pc[:, :, 0], ps_[:, :, 1], ALU.subtract)
                    ins = tt(u[:, :, 1], ps_[:, :, 0], pc[:, :, 1], ALU.add)
                ins.then_inc(rot_ready, 1)
                v.wait_ge(g_ready, L + 1)
                nb3, e3 = nb_tok.rearrange("p (t h) -> p t h", t=T), e_tok.rearrange("p (t h) -> p t h", t=T)
                link(cp(nb_tok, mb[0][:, S:S + 8]))
                link(tt(e3, u_ml[:, :, 2 * MW:2 * MW + 4], bc[:, L, 12:16].unsqueeze(1).to_broadcast([P, T, 4]), ALU.add))
                tt(e3, e3, nb3, ALU.add).then_inc(e_ready, 1)
                v.wait_ge(e_ready, L + 1)
                v.wait_ge(xs_mm, L + 1)
                link(cp(xs[:].rearrange("p t n -> p (t n)"), mb[1][:]))
                for i in range(T):
                    ins = tt(xdt[:, i].rearrange("p (h w) -> p h w", h=NH), xs[:, i].rearrange("p (h w) -> p h w", h=NH),
                             soft[:, i, 0:4].unsqueeze(2).to_broadcast([P, NH, 64]), ALU.mult)
                ins.then_inc(xdt_ready, 1)
                v.wait_ge(scores_mm, 3 * L + 1)
                for h in range(NH):
                    v.wait_ge(seg_exp, 4 * L + h + 1)
                    ins = tt(probs[:, h, :], probs[:, h, :], mb[h // 2][:, 0:384], ALU.mult)
                ins.then_inc(probs_ready, 1)
                take_y(L, 0)
                for i in range(T):
                    link(tt(y[:, i].rearrange("p (h w) -> p h w", h=NH), xs[:, i].rearrange("p (h w) -> p h w", h=NH),
                            bc[:, L, 8:12].unsqueeze(2).to_broadcast([P, NH, 64]), ALU.mult))
                    ins = tt(y[:, i], y[:, i], mb[2 + i][:, 0:MW], ALU.add)
                    if i == 0:
                        link(ins)
                ins.then_inc(o_read, 1)
                v.wait_ge(o_read, 4 * L + 1)
                v.wait_ge(et_mm, L + 1)
                link(cp(mrow[:, 0], mb[0][0:NH, 0:S]))
                nc.vector.tensor_tensor_scan(mrow[:, 1], mrow[:, 0], mrow[:, 0], 0.0, ALU.max, ALU.max).then_inc(mt_ready, 1)
                link(tt(y[:], y[:], u_z[:], ALU.mult))
                head_norm(L, 0, 1, None, True)
                for h in range(NH):
                    v.wait_ge(mbc_mm, 4 * L + h + 1)
                    if h == 0:
                        tt(negm, nb_tok, mb[0][:, 384:392], ALU.subtract).then_inc(negm_ready, 1)
                    ts(probs[:, h, 0:S], mb[h][:, 0:S], e_tok[:, h:h + 1], 0.0, ALU.subtract, ALU.max)
                    ts(probs[:, h, S:384], mb[h][:, S:384], e_tok[:, 4 + h:5 + h], 0.0, ALU.subtract, ALU.max).then_inc(ml_arg, 1)
                v.wait_ge(scores_mm, 3 * L + 2)
                for h in range(NH):
                    v.wait_ge(ml_exp, 4 * L + h + 1)
                    ins = stt(out=probs[:, h, :], in0=probs[:, h, :], scalar=64 ** -0.5, in1=mb[h][:, 0:384], op0=ALU.mult, op1=ALU.mult)
                ins.then_inc(probs_ready, 1)
                take_y(L, 1)
                v.wait_ge(em_ready, L + 1)
                for i in range(T):
                    link(cp(den[:, 4 * i:4 * i + 4], mb[i][:, MW:MW + 4]))
                link(stt(out=den, in0=den, scalar=-1.0, in1=den, op0=ALU.mult, op1=ALU.max))
                link(tt(den, den, em, ALU.max))
                link(nc.vector.reciprocal(rden, den))
                for i in range(T):
                    ins = tt(y[:, i].rearrange("p (h w) -> p h w", h=NH), mb[i][:, 0:MW].rearrange("p (h w) -> p h w", h=NH),
                             rden[:, 4 * i:4 * i + 4].unsqueeze(2).to_broadcast([P, NH, 64]), ALU.mult)
                ins.then_inc(o_read, 1)
                v.wait_ge(o_read, 4 * L + 2)
                head_norm(L, 1, 3, u_ml[:, :, MW:2 * MW], False)
                merge(L, 0)
                v.wait_ge(scores_mm, 3 * L + 3)
                v.wait_ge(pv_mm, 4 * L + 2)
                for h in range(NH):
                    tt(probs[:, h, 0:S], mb[h][:, 0:S], retdecay[:, h, 0:S], ALU.mult)
                    ins = tt(probs[:, h, S:384], mb[h][:, S:384], retdecay[:, h, 0:P], ALU.mult)
                ins.then_inc(probs_ready, 1)
                gla_levels(L, 0)
                take_y(L, 2)
                for i in range(T):
                    ins = cp(y[:, i], mb[i][:, 0:MW])
                ins.then_inc(o_read, 1)
                v.wait_ge(o_read, 4 * L + 3)
                head_norm(L, 2, 0, u_ret[:, :, 768:1024], False)
                merge(L, 1)
                v.wait_ge(pv_mm, 4 * L + 3)
                link(nc.vector.memset(probs[:].rearrange("p h n -> p (h n)"), 0.0))
                gla_put_levels(L, 0)
                gla_put_levels(L, 1)
                gla_levels(L, 1)
                gla_put_levels(L, 2)
                gla_put_levels(L, 3)
                gla_put_levels(L, 4)
                merge(L, 2)
                take_y(L, 3)
                for i in range(T):
                    ins = cp(y[:, i], mb[i][:, 0:MW])
                ins.then_inc(o_read, 1)
                v.wait_ge(o_read, 4 * L + 4)
                head_norm(L, 3, 2, u_gla[:, :, 4 + MW:], False)
                merge(L, 3)

            def normed(src, n_g, cols, gcol, m, r, w):
                for i in range(T):
                    ins = stt(out=src[:, i, cols], in0=src[:, i, cols], scalar=r[:, i:i + 1], in1=ygain[:, gcol:gcol + w],
                              op0=ALU.mult, op1=ALU.mult)
                return ins

            def rope(dst, src, c_, s_, n):
                for i in range(T):
                    sv = src(i)
                    pc = c_[:, i, 0:n * ROPE].rearrange("p (g h c) -> p g h c", g=n, h=2)
                    ps_ = s_[:, i, 0:n * ROPE].rearrange("p (g h c) -> p g h c", g=n, h=2)
                    for h in range(2):
                        tt(pc[:, :, h], sv[:, :, h], cos2[:, i].unsqueeze(1).to_broadcast([P, n, ROPE // 2]), ALU.mult)
                        link(tt(ps_[:, :, h], sv[:, :, h], sin2[:, i].unsqueeze(1).to_broadcast([P, n, ROPE // 2]), ALU.mult))
                    d = dst(i)
                    tt(d[:, :, 0], pc[:, :, 0], ps_[:, :, 1], ALU.subtract)
                    ins = tt(d[:, :, 1], pc[:, :, 1], ps_[:, :, 0], ALU.add)
                return ins

            def post_norm(n):
                v.wait_ge(squares, T * (n + 1))
                link(ts(r_in, ssq, 1.0 / D, EPS, ALU.mult, ALU.add))
                rsqrt(rstd, r_in)
                v.wait_ge(gain_in, 16 * (n + 1))
                for i in range(T):
                    stt(out=xn[:, i, :], in0=xn[:, i, :], scalar=rstd[:, i:i + 1], in1=gain[:], op0=ALU.mult,
                        op1=ALU.mult).then_inc(xn_ready, 1)
                v.wait_ge(xn_ready, T * (n + 1))
                xf, nf = x[:].rearrange("p t d -> p (t d)"), xn[:].rearrange("p t d -> p (t d)")
                tt(xf, xf, nf, ALU.add).then_inc(x_ready, 1)

            def merge2(L, b):
                B = BK[L]
                for h in range(2):
                    for i in range(T):
                        job = ("merge", b, h, i)
                        bank = pb[B.index[job] % 4]
                        g = gates[:, b % 2, i, h * 512:(h + 1) * 512]
                        m = merged[:, i, h * 512:(h + 1) * 512]
                        acted(B, ("gate", b, h, i))
                        v.wait_ge(filled, B.filled(job))
                        tt(m if b == 0 else g, bank[:], g, ALU.mult).then_inc(dve_emptied, 1)
                        v.wait_ge(dve_emptied, B.emptied(job)[1])
                        if b:
                            ins = tt(m, m, g, ALU.add)
                            if (b, h, i) == (3, 1, 1):
                                ins.then_inc(merged_ready, 1)
                            else:
                                link(ins)

            def att_maxima(l, g):
                for hh in range(4):
                    v.wait_ge(att_mm, 4 * (2 * l + g) + hh + 1)
                    if g or l:
                        v.wait_ge(att_exp, 8 * (2 * l + g))
                    for i, (lo, hi) in enumerate(((0, P), (P, 384))):
                        c = 2 * hh + i
                        link(nc.vector.tensor_reduce(mx[:, c:c + 1], mb[hh][:, lo:hi], AX.X, ALU.max))
                    ts(nmx[:, 2 * hh:2 * hh + 2], mx[:, 2 * hh:2 * hh + 2], -(NOPE + ROPE) ** -0.5, None, ALU.mult).then_inc(att_max, 1)

            def take_probsT(l, g):
                for hh in range(4):
                    v.wait_ge(probsT_mm, 4 * (2 * l + g) + hh + 1)
                    ins = cp(probsT[:, hh, :], mb[hh][:, 0:384])
                ins.then_inc(probsT_ready, 1)
                link(nc.vector.reciprocal(rsum, sums))

            def take_att(l, g):
                v.wait_ge(av_mm, 2 * l + g + 1)
                r3 = rsum.rearrange("p (h t) -> p t h", t=T)
                for i in range(T):
                    ins = tt(y_att[:, i, g * MW:(g + 1) * MW].rearrange("p (h w) -> p h w", h=4),
                             mb[i][:, 0:MW].rearrange("p (h w) -> p h w", h=4), r3[:, i].unsqueeze(2).to_broadcast([P, 4, VH]), ALU.mult)
                ins.then_inc(y_att_ready, 1)

            def mixers2(l):
                L = 2 + l
                B = BK[L]
                acted(B, ("proj", 0, 1))
                if l == 0:
                    v.wait_ge(cst2_in, 16)
                for i in range(T):
                    sq = u_z[:].rearrange("p t n -> p (t n)")[:, 0:384]
                    link(tt(sq, lat[:, i, 0:384], lat[:, i, 0:384], ALU.mult))
                    link(nc.vector.tensor_reduce(lat_s[:, 3 * i:3 * i + 3], sq.rearrange("p (g n) -> p g n", g=3), AX.X, ALU.add))
                s3 = lat_s.rearrange("p (t g) -> p t g", g=3)
                link(tt(lat_m[:, 0:2], s3[:, :, 0], s3[:, :, 1], ALU.add))
                link(ts(lat_m[:, 0:2], lat_m[:, 0:2], 1.0 / MW, EPS, ALU.mult, ALU.add))
                link(ts(lat_m[:, 2:4], s3[:, :, 2], 1.0 / P, EPS, ALU.mult, ALU.add))
                rsqrt(lat_r, lat_m)
                v.wait_ge(ygain_in, 16 * 8 + 48 * (l + 1))
                normed(lat, 2, slice(0, MW), 0, None, lat_r[:, 0:2], MW)
                normed(lat, 2, slice(MW, MW + P), MW, None, lat_r[:, 2:4], P)
                ins = (rope(lambda i: k_rot[:, i].rearrange("p (n h c) -> p n h c", n=1, h=2),
                          lambda i: lat[:, i, KR:KR + ROPE].rearrange("p (n h c) -> p n h c", n=1, h=2), rope_c, xs, 1))
                ins.then_inc(lat_ready, 1)
                v.wait_ge(lat_ready, l + 1)
                acted(B, ("proj", 2, 1))
                sq = u_z[:]
                link(tt(sq, sgu_v, sgu_v, ALU.mult))
                link(nc.vector.tensor_reduce(lat_m[:, 0:2], sq, AX.X, ALU.add))
                link(ts(lat_m[:, 0:2], lat_m[:, 0:2], 1.0 / MW, EPS, ALU.mult, ALU.add))
                rsqrt(lat_r[:, 0:2], lat_m[:, 0:2])
                normed(sgu_v, 2, slice(0, MW), MW + P, None, lat_r[:, 0:2], MW).then_inc(vn_ready, 1)
                v.wait_ge(sgu_turned, l + 1)
                link(cp(scratch[:], mb[3][:]))
                nc.vector.memset(sgu_wT[BLOCKED:P, :, 0:BLOCKED], 0.0).then_inc(sgu_wT_ready, 1)
                acted(B, ("proj", 3, 1))
                link(tt(conv_c, conv_c, conv_x, ALU.mult))
                for b in range(2):
                    o = 100 + 12 * l
                    w = lambda k: perch[:, o + 2 * k + b:o + 2 * k + b + 1]
                    link(ts(convT[:, b], conv_c[:, b], w(2), None, ALU.mult))
                    for s_ in (1, 2):
                        link(stt(out=convT[:, b, s_:S], in0=conv_c[:, b, 0:S - s_], scalar=w(2 - s_), in1=convT[:, b, s_:S],
                                 op0=ALU.mult, op1=ALU.add))
                tt(convT, convT, conv_b, ALU.mult).then_inc(convT_ready, 1)
                v.wait_ge(qrv_ready, l + 1)
                v.wait_ge(poolT_mm, l + 1)
                rope(lambda i: q_rot[:, i].rearrange("p (g h c) -> p g h c", g=AH, h=2),
                     lambda i: q_rope[:, i].rearrange("p (g h c) -> p g h c", g=AH, h=2), rope_c, rope_s, AH).then_inc(q_rot_ready, 1)
                v.wait_ge(sgu_mm, l + 1)
                for i in range(T):
                    for g in range(4):
                        o = 100 + 12 * l + 8 + g
                        cs = slice(g * 64, (g + 1) * 64)
                        ins = stt(out=y_sgu[:, i, cs], in0=mb[3][:, i * MW + g * 64:i * MW + (g + 1) * 64], scalar=perch[:, o:o + 1],
                                  in1=sgu_u[:, i, cs], op0=ALU.add, op1=ALU.mult)
                ins.then_inc(y_sgu_ready, 1)
                merge2(L, 0)
                att_maxima(l, 0)
                merge2(L, 1)
                take_probsT(l, 0)
                take_att(l, 0)
                att_maxima(l, 1)
                take_probsT(l, 1)
                merge2(L, 2)
                take_att(l, 1)
                merge2(L, 3)

            def take_out(L):
                B = BK[L]
                for h in range(2):
                    for i in range(T):
                        job = ("wout", h, i)
                        v.wait_ge(filled, B.filled(job))
                        cp(xn[:, i, h * 512:(h + 1) * 512], pb[B.index[job] % 4][:]).then_inc(dve_emptied, 1)
                v.wait_ge(dve_emptied, B.emptied(("wout", 1, 1))[1])

            def add_out(L):
                B = BK[L]
                for h in range(2):
                    for i in range(T):
                        job = ("wout", h, i)
                        v.wait_ge(filled, B.filled(job))
                        xv = x[:, i, h * 512:(h + 1) * 512]
                        ins = tt(xv, xv, pb[B.index[job] % 4][:], ALU.add)
                        ins.then_inc(dve_emptied, 1)
                v.wait_ge(dve_emptied, B.emptied(("wout", 1, 1))[1])

            def ffn(u, add=True):
                for c in range(NF):
                    g = u * NF + c
                    for i in range(T):
                        v.wait_ge(silu_done, T * g + i + 1)
                        if g:
                            v.wait_ge(ht_mm, g)
                        tt(fh[:, i, :], fsg[:, i, :], mb[i][:, FC:2 * FC], ALU.mult).then_inc(h_ready, 1)
                v.wait_ge(ffn_mm, (u + 1) * NF)
                if not add:
                    for i in range(T):
                        for h in range(2):
                            ins = cp(xn[:, i, h * 512:(h + 1) * 512], pb[2 * i + h][:])
                    ins.then_inc(post_in, 1)
                    return
                for i in range(T):
                    for h in range(2):
                        xv = x[:, i, h * 512:(h + 1) * 512]
                        ins = tt(xv, xv, pb[2 * i + h][:], ALU.add)
                        if (i, h) != (1, 1):
                            link(ins)
                ins.then_inc(x_ready, 1)

            def route():
                v.wait_ge(logits_mm, 1)
                link(cp(logit.rearrange("p t e -> p (t e)"), mb[0][:, 0:2 * NE]))
                rk = const("rank8").unsqueeze(1).to_broadcast([P, T, NE])
                wide = lambda col: col.unsqueeze(2).to_broadcast([P, T, NE])
                for src, top, one in ((logit, m1, one1), (tmp16, m2, one2)):
                    link(nc.vector.tensor_reduce(top, src, AX.X, ALU.max))
                    link(tt(eq, src, wide(top), ALU.is_equal))
                    link(tt(eq, eq, rk, ALU.mult))
                    link(nc.vector.tensor_reduce(kx, eq, AX.X, ALU.max))
                    link(tt(one, rk, wide(kx), ALU.is_equal))
                    if src is logit:
                        link(stt(out=tmp16, in0=one1, scalar=NEG, in1=logit, op0=ALU.mult, op1=ALU.add))
                tt(ex, m2, m1, ALU.subtract).then_inc(ex_arg, 1)
                tt(both, one1, one2, ALU.add).then_inc(both_ready, 1)
                v.wait_ge(ex_ready, 1)
                w1, w2 = quad[:, 2], quad[:, 3]
                link(ts(w2, ex, 1.0, None, ALU.add))
                link(nc.vector.reciprocal(w1, w2))
                link(tt(w2, ex, w1, ALU.mult))
                v.wait_ge(rank_mm, 1)
                cnt = mb[1][:, 2 * NE:3 * NE]
                link(ts(zero8, cnt, 0.5, None, ALU.is_gt))
                link(stt(out=n_tiles, in0=cnt, scalar=P + 0.5, in1=zero8, op0=ALU.is_gt, op1=ALU.add))
                link(nc.vector.memset(zero8, 0.0))
                link(nc.vector.tensor_tensor_scan(p_end, n_tiles, zero8, 0.0, ALU.add, ALU.add))
                link(tt(p_start, p_end, n_tiles, ALU.subtract))
                link(ts(p_start, p_start, float(P), -1.0, ALU.mult, ALU.add))
                link(tt(at_, mb[1][:, 0:2 * NE].rearrange("p (t e) -> p t e", t=T), p_start.unsqueeze(1).to_broadcast([P, T, NE]), ALU.add))
                for q, one in enumerate((one1, one2)):
                    link(tt(eq, at_, one, ALU.mult))
                    link(nc.vector.tensor_reduce(quad[:, q], eq, AX.X, ALU.add))
                for q in range(4):
                    for i in range(T):
                        ins = ts(diag[:, q, i], ident, quad[:, q, i:i + 1], None, ALU.mult)
                ins.then_inc(diag_ready, 1)
                link(tt(e_cmp, p_end.unsqueeze(1).to_broadcast([P, MAXPASS, NE]),
                        const("passno").unsqueeze(2).to_broadcast([P, MAXPASS, NE]), ALU.is_le))
                link(nc.vector.tensor_reduce(e_tab[:, 0:MAXPASS], e_cmp, AX.X, ALU.add))
                link(ts(e_tab[:, 0:MAXPASS], e_tab[:, 0:MAXPASS], float(NE - 1), None, ALU.min))
                link(cp(e_tab[:, MAXPASS:], p_end[:, NE - 1:NE]))
                link(cp(slot_no, const("iotap")))
                cp(table[:], e_tab[0:1, :]).then_inc(table_ready, 1)
                nc.vector.memset(scratch[:], 0.0).then_inc(zero_ready, 1)
                v.wait_ge(quad_mm, 1)
                for n in range(2):
                    link(cp(quad_b[:, 2 * n:2 * n + 2].rearrange("p q s -> p (q s)"), mb[2 + n][:]))

            def select_places(step):
                for i in range(T):
                    step(ts(sel[:, i], const("iota"), quad[:, 0, i:i + 1], None, ALU.is_equal))
                    ins = stt(out=sel[:, i], in0=const("iota"), scalar=quad[:, 1, i:i + 1], in1=sel[:, i], op0=ALU.is_equal, op1=ALU.add)
                    if i == 0:
                        step(ins)
                ins.then_inc(sel_ready, 1)

            def experts():
                route()
                select_places(link)
                n_pass = passes(v)
                with v.Fori(0, n_pass) as t:
                    n = [0]
                    STEPS = 7

                    def step(ins):
                        n[0] += 1
                        ins.then_inc(sel_step, 1)
                        v.wait_ge(sel_step, t * STEPS + n[0])

                    v.wait_ge(scatter_mm, t + 1)
                    step(stt(out=selT, in0=quad_b[:, 0], scalar=slot_no, in1=quad_b[:, 2], op0=ALU.is_equal, op1=ALU.mult))
                    step(stt(out=sel_tmp, in0=quad_b[:, 1], scalar=slot_no, in1=quad_b[:, 3], op0=ALU.is_equal, op1=ALU.mult))
                    tt(selT, selT, sel_tmp, ALU.add).then_inc(selT_ready, 1)
                    v.wait_ge(selT_ready, t + 1)
                    step(ts(slot_no, slot_no, float(P), None, ALU.add))
                    for c in range(NF):
                        v.wait_ge(e_silu, t * NF + c + 1)
                        tt(fh[:, 0, :], fsg[:, 0, :], mb[2][:, FC:2 * FC], ALU.mult).then_inc(e_h, 1)
                        if c == 0:
                            v.wait_ge(sel_ready, t + 1)
                            qv = quad[:, 0:2].rearrange("p q t -> p (q t)")
                            step(ts(qv, qv, -float(P), None, ALU.add))
                            select_places(step)
                    v.wait_ge(e_down, t * NF + 2 * NF)
                    cp(ys[:, 512:1024], mb[1][:]).then_inc(ys_ready, 1)
                assert n[0] == 7, n[0]
                v.wait_ge(moe_mm, 1)
                for i in range(T):
                    for h in range(2):
                        xv = x[:, i, h * 512:(h + 1) * 512]
                        ins = tt(xv, xv, pb[2 * i + h][:], ALU.add)
                        if (i, h) != (1, 1):
                            link(ins)
                ins.then_inc(x_ready, 1)

            v.wait_ge(rows_turned, 1)
            cp(perch[:], mb[0][:, 0:P]).then_inc(perch_ready, 1)
            v.wait_ge(perch_ready, 1)
            for L in range(n_layers):
                norm(2 * L)
                mixers(L)
                add_out(L)
                if not has_ffn(L):
                    break
                norm(2 * L + 1)
                if L == 0:
                    ffn(0)
                else:
                    experts()
                    norm(4, x)
                    v.wait_ge(xn_ready, 10)
                    link(nc.vector.memset(scratch[:, 0:1], 0.0))
                    nc.vector.memset(scratch[:, 0:1], 0.0).then_inc(x_ready, 1)
            if stop is None:
                for l in range(2):
                    L, n = 2 + l, 5 + 4 * l
                    norm(n)
                    mixers2(l)
                    take_out(L)
                    post_norm(n + 1)
                    norm(n + 2)
                    ffn(1 + l, add=False)
                    post_norm(n + 3)


INPUTS = ["x", "mix_norm_g", "w_in", "ret_norm_g", "ssd_conv_w", "ssd_conv_b", "ssd_dt_bias", "ssd_a_log", "ssd_d", "ssd_norm_g",
          "gla_w_alpha", "gla_b_alpha", "gla_norm_g", "ml_conv_w", "ml_conv_b", "ml_b_i", "ml_b_f", "ml_norm_g", "w_branch", "w_out",
          "ffn_norm_g", "ffn_w1", "ffn_w3", "ffn_w2", "router_w", "moe_w1", "moe_w3", "moe_w2", "final_norm_g",
          "w_in_2", "g_pre_mix_2", "g_cq_2", "g_ckv_2", "w_uq_2", "w_ukv_2", "pool_w_2", "pool_scale_2", "g_sgu_v_2", "sgu_w_2",
          "sgu_b_2", "conv_w_2", "w_br_a_2", "w_br_b_2", "w_br_c_2", "w_br_d_2", "w_out_2", "g_post_mix_2", "g_pre_ffn_2",
          "w_ffn_gate_2", "w_ffn_up_2", "w_ffn_down_2", "g_post_ffn_2"]
STOP = None


def kernel(**inputs):
    import numpy as _np
    import concourse.bacc as _bacc
    from concourse.bass_utils import run_bass_kernel_spmd as _run

    nc = _bacc.Bacc("TRN2", target_bir_lowering=False, num_devices=1)
    arrays, args = {}, {}
    for name in INPUTS:
        arr = _np.ascontiguousarray(inputs[name])
        arrays["in_" + name] = arr
        args[name] = nc.dram_tensor("in_" + name, arr.shape, mybir.dt.from_np(arr.dtype), kind="ExternalInput").ap()
    out = nc.dram_tensor("out", (1, S, D), F32, kind="ExternalOutput").ap()
    build(nc, args, out, STOP)
    return _run(nc, [arrays], core_ids=[0]).results[0]["out"]
```

```python
import numpy as np
from contextlib import ExitStack

import concourse.bass as bass
from concourse import mybir

F32 = mybir.dt.float32
F32R = mybir.dt.float32r
I32 = mybir.dt.int32
U32 = mybir.dt.uint32
ALU = mybir.AluOpType
ACT = mybir.ActivationFunctionType
AX = mybir.AxisListType

P = 128
T = 2
S = T * P
D = 1024
KD = D // P
EPS = 1e-6
NH = 4
MW = 256
NBR = 4
FF = 2816
FC = 256
NF = FF // FC
NE = 8
MAXPASS = 11
NEG = -1.0e30

RQ, RV, RG, SZ, SX, SB, SC, SDT = 0, 512, 768, 1024, 1280, 1536, 1792, 2048
GQ, GK, GV, GR, GA, MQ, MK, MV, MO, MI, MF, GATE1 = 2052, 2180, 2308, 2564, 2820, 2836, 3092, 3348, 3604, 3860, 3864, 3868
RANK = 16

CQ, CKV, KR, PI, SU, SV, CB, CC, CX, GATE2 = 0, 256, 384, 416, 672, 928, 1184, 1440, 1696, 1952
AH, NOPE, ROPE, VH = 8, 64, 32, 64
UP_QN, UP_QR, UP_KN, UP_V = 0, 2 * AH * NOPE, 2 * AH * (NOPE + ROPE), 2 * AH * (NOPE + ROPE) + AH * NOPE
POOL_WINDOWS = (2, 4, 8, 16)
BLOCKED = 64

NSLOT = 3
SLOTW = KD * 2 * FC + 2 * D

PIECE = 1024
NPIECE = 4
GU_PIECES, DN_PIECES = KD * 2 * FC // PIECE, 2 * D // PIECE


def pieces(c):
    return (GU_PIECES + DN_PIECES) * c - DN_PIECES * (c > 0)


ALL_PIECES = (GU_PIECES + DN_PIECES) * NF
PIECE_LIST = [(c, q) for c in range(NF + 1) for q in range(GU_PIECES + DN_PIECES)
              if (q < GU_PIECES and c < NF) or (q >= GU_PIECES and c > 0)]
assert len(PIECE_LIST) == ALL_PIECES and all(PIECE_LIST[pieces(c)][0] == c for c in range(NF + 1))


def shape_constants():
    j, i = np.arange(P)[:, None], np.arange(P)[None, :]
    parts = {}
    parts["ident"] = (j == i)
    parts["tri"] = (j <= i)
    parts["ones"] = np.ones((P, P))
    parts["after"] = (j > i)
    parts["negmask"] = np.where(i < j, NEG, 0.0)
    parts["bigmask"] = np.where(i < j, -NEG, 0.0)
    sel = np.zeros((P, NH, P))
    for h in range(NH):
        sel[h, h, :] = 1
    parts["sel"] = sel.reshape(P, -1)
    parts["iota"] = np.broadcast_to(i, (P, P))
    parts["iotap"] = j
    parts["rank8"] = np.broadcast_to(NE - np.arange(NE)[None, :], (P, NE))
    parts["passno"] = np.broadcast_to(np.arange(MAXPASS)[None, :], (P, MAXPASS))
    half = 32
    inv = (np.float32(10000.0) ** (-np.arange(half, dtype=np.float32) / np.float32(half))).astype(np.float32)
    ang = (np.arange(S, dtype=np.float32)[:, None] * inv[None, :]).astype(np.float32).astype(np.float64)
    parts["cos"] = np.cos(ang).reshape(T, P, half).transpose(1, 0, 2).reshape(P, -1)
    parts["sin"] = np.sin(ang).reshape(T, P, half).transpose(1, 0, 2).reshape(P, -1)
    lg = np.log1p(-np.exp2(-5.0 - np.arange(NH)))
    tok = np.arange(S)[None, :]
    rel = tok - j
    dec = np.stack([np.where(rel >= 0, np.exp(np.maximum(rel, 0) * g), 0.0) * 64 ** -0.5 for g in lg], 1)
    parts["retdecay"] = dec.reshape(P, -1)
    lev = [((j // (2 * b) == i // (2 * b)) & ((j // b) % 2 == 0) & ((i // b) % 2 == 1)) for b in (1, 2, 4, 8, 16, 32, 64)]
    parts["levmask"] = np.stack(lev + [j == i], 1).reshape(P, -1)
    off, at, cols = 0, {}, []
    for k, v in parts.items():
        at[k] = (off, off + v.shape[1])
        off += v.shape[1]
        cols.append(np.asarray(v, np.float32))
    return np.ascontiguousarray(np.concatenate(cols, 1)), at


def shape_constants2():
    parts = {}
    inv = (np.float32(10000.0) ** (-np.arange(0, ROPE, 2, dtype=np.float32) / np.float32(ROPE))).astype(np.float32)
    ang = (np.arange(S, dtype=np.float32)[:, None] * inv[None, :]).astype(np.float32).astype(np.float64)
    parts["cos2"] = np.cos(ang).reshape(T, P, -1).transpose(1, 0, 2).reshape(P, -1)
    parts["sin2"] = np.sin(ang).reshape(T, P, -1).transpose(1, 0, 2).reshape(P, -1)
    j, i = np.arange(S)[:, None], np.arange(S)[None, :]
    win = np.stack([((j <= i) & (j > i - w)) / np.minimum(i + 1, w) - (j == i) for w in POOL_WINDOWS], 1)
    parts["window"] = np.concatenate([win[:P], win[P:, :, P:]], 2).reshape(P, -1)
    early = np.arange(P) < BLOCKED
    parts["rowmask"] = np.broadcast_to(early[None, :], (P, P))
    parts["colmask"] = np.broadcast_to(np.where(early, 0.0, NEG)[None, :], (P, P))
    off, at, cols = 0, {}, []
    for k, v in parts.items():
        at[k] = (off, off + v.shape[1])
        off += v.shape[1]
        cols.append(np.asarray(v, np.float32))
    return np.ascontiguousarray(np.concatenate(cols, 1)), at


CHUNKS1 = [
    (SZ, 512, [("ch", ((SX, 128), (SX + 128, 128))), ("tok", 0, SZ, 256), ("tok", 1, SZ, 256)]),
    (SB, 512, [("ch", ((SB, 128), (SB + 128, 128))), ("ch", ((SC, 128), (SC + 128, 128)))]),
    (GR, 528, [("ch", ((MQ, 128), (MQ + 128, 128))), ("ch", ((GA, RANK),)), ("tok", 0, GR, 256), ("tok", 1, GR, 256)]),
    (MK, 512, [("ch", ((MK, 128), (MK + 128, 128))), ("tok", 0, MV, 256), ("tok", 1, MV, 256)]),
    (SDT, 516, [("ch", ((GQ, 128), (GK, 128))), ("tok2", 0), ("tok2", 1)]),
    (MO, 264, [("tok", 0, MO, 264), ("tok", 1, MO, 264)]),
    (RQ, 512, [("tok", 0, RQ, 512), ("tok", 1, RQ, 512)]),
    (RV, 512, [("tok", 0, RV, 512), ("tok", 1, RV, 512)]),
]
CHUNKS2 = [
    (CQ, 416, [("tok", 0, CQ, 416), ("tok", 1, CQ, 416)]),
    (PI, 512, [("tok", 0, PI, 512), ("tok", 1, PI, 512)]),
    (SV, 512, [("tok", 0, SV, 256), ("tok", 1, SV, 256), ("ch", ((CB, 128), (CB + 128, 128)))]),
    (CC, 512, [("ch", ((CC, 128), (CC + 128, 128))), ("ch", ((CX, 128), (CX + 128, 128)))]),
]
BR_ORDER2 = (3, 1, 2, 0)
BR_ORDER = (1, 3, 0, 2)


def bank_jobs1():
    jobs = [("turn", k) for k in range(4)]
    for c, (_, _, js) in enumerate(CHUNKS1):
        jobs += [("proj", c, j) for j in range(len(js))]
    gates = lambda b: [("gate", b, h, i) for h in range(2) for i in range(T)]
    merge = lambda b: [("yturn", b)] + [("merge", b, h, i) for h in range(2) for i in range(T)]
    jobs += gates(0) + gates(1) + merge(0) + gates(2) + merge(1) + gates(3) + merge(2) + merge(3)
    jobs += [("turn", 4 + k) for k in range(4)] + [("wout", h, i) for h in range(2) for i in range(T)]
    jobs += [("turn", 8 + k) for k in range(4)]
    return jobs


def bank_jobs2():
    gate = lambda b, *ns: [("gate", b, n // 2, n % 2) for n in ns]
    merge = lambda b: [("merge", b, h, i) for h in range(2) for i in range(T)]
    jobs = [("turn", k) for k in range(4)]
    for c, (_, _, js) in enumerate(CHUNKS2):
        jobs += [("proj", c, j) for j in range(len(js))]
    jobs += gate(0, 0, 1, 2, 3) + gate(1, 0, 1) + merge(0) + gate(1, 2, 3) + merge(1) + gate(2, 0, 1, 2, 3)
    jobs += [("yturn", 2, 0)] + merge(2) + gate(3, 0, 1, 2, 3) + [("yturn", 3, 0), ("yturn", 3, 1)] + merge(3)
    jobs += [("turn", 4 + k) for k in range(4)] + [("wout", h, i) for h in range(2) for i in range(T)]
    jobs += [("turn", 8 + k) for k in range(4)]
    return jobs


class Banks:

    def __init__(self, jobs, fill_base, act_base, dve_base, layer):
        self.jobs = jobs
        self.by = ["dve" if j[0] in ("merge", "wout") else "act" for j in jobs]
        n_act, n_dve = self.by.count("act"), self.by.count("dve")
        self.fill0 = fill_base + layer * len(jobs)
        self.act0 = act_base + layer * n_act
        self.dve0 = dve_base + layer * n_dve
        self.end = (self.fill0 + len(jobs), self.act0 + n_act, self.dve0 + n_dve)
        self.index = {j: n for n, j in enumerate(jobs)}

    def filled(self, job):
        return self.fill0 + self.index[job] + 1

    def emptied(self, job):
        n = self.index[job]
        who = self.by[n]
        return who, (self.act0 if who == "act" else self.dve0) + self.by[:n + 1].count(who)


def build(nc, a, out):
    cvals, cat = shape_constants()
    cdram = nc.inline_tensor(cvals, name="shape_constants")
    cvals2, cat2 = shape_constants2()
    cdram2 = nc.inline_tensor(cvals2, name="shape_constants2")
    ctx = ExitStack()
    with ctx:
        def sb(name, shape, dt=F32):
            return ctx.enter_context(nc.sbuf_tensor(name, shape, dt))

        def sem(name):
            return ctx.enter_context(nc.semaphore(name))

        ring = sb("ring", [P, NSLOT, SLOTW])
        x = sb("x", [P, T, D])
        xn = sb("xn", [P, T, D])
        hT = sb("hT", [P, KD, S])
        merged = sb("merged", [P, T, D])
        gates = sb("gates", [P, 2, T, D])
        u_z = sb("u_z", [P, T, MW])
        xs = sb("xs", [P, T, MW])
        scratch = sb("scratch", [P, 512])
        cst = sb("cst", [P, cvals.shape[1]])
        gain = sb("gain", [P, D])
        ygain = sb("ygain", [P, D])
        soft = sb("soft", [P, T, 136])
        small = sb("small", [P, 160])
        rows = sb("rows", [P, P])
        perch = sb("perch", [P, P])
        alpha_w = sb("alpha_w", [RANK, 2, P])
        bc = sb("bc", [P, 2, 148])
        ea = sb("ea", [P, 2, 4])
        gT = sb("gT", [P, S])
        table = sb("table", [1, MAXPASS + 1], I32)
        with ExitStack() as mixers_memory:
            def mix(name, shape, dt=F32):
                return mixers_memory.enter_context(nc.sbuf_tensor(name, shape, dt))

            u_ret = mix("u_ret", [P, T, 1024])
            u_gla = mix("u_gla", [P, T, 4 + 2 * MW])
            u_ml = mix("u_ml", [P, T, 2 * MW + 8])
            ch_in = mix("ch_in", [P, 13, S])
            conv = mix("conv", [P, 10, S])
            probs = mix("probs", [P, NH, 384])
            xdt = mix("xdt", [P, T, MW])
            y = mix("y", [P, T, MW])
            yT = mix("yT", [P, 2, 2, S])
        w_hi = sb("w_hi", [P, NPIECE, PIECE], F32R)
        w_lo = sb("w_lo", [P, NPIECE, PIECE], F32R)
        hT_hi = sb("hT_hi", [P, KD, S], F32R)
        hT_lo = sb("hT_lo", [P, KD, S], F32R)
        fhT_hi = sb("fhT_hi", [P, 2, S], F32R)
        fhT_lo = sb("fhT_lo", [P, 2, S], F32R)
        mrow = merged[0:NH, 0, 0:2 * S].rearrange("p (k s) -> p k s", k=2)

        def const(name):
            lo, hi = cat[name]
            return cst[:, lo:hi]

        ident, tri, ones, after = const("ident"), const("tri"), const("ones"), const("after")
        cosT = const("cos").rearrange("p (t h) -> p t h", t=T)
        sinT = const("sin").rearrange("p (t h) -> p t h", t=T)
        retdecay = const("retdecay").rearrange("p (h i) -> p h i", h=NH)
        levmask = const("levmask").rearrange("p (l i) -> p l i", l=8)
        head_sel = const("sel").rearrange("p (h i) -> p h i", h=NH)
        g1 = gates[:, 1].rearrange("p t d -> p (t d)")
        sp_tmp = [g1[:, 272 * n:272 * (n + 1)] for n in range(6)]
        rot_c = g1[:, 0:1024].rearrange("p (t h c) -> p t h c", t=T, h=8)
        rot_s = g1[:, 1024:2048].rearrange("p (t h c) -> p t h c", t=T, h=8)
        w_seg = ch_in[:, 0:4].rearrange("p b s -> p (b s)").rearrange("p (h t j) -> p h t j", h=NH, t=T)
        w_one = ch_in[:, 4:6].rearrange("p b s -> p (b s)").rearrange("p (h j) -> p h j", h=NH)
        gla_e, gla_k, gla_q = ch_in[:, 0:4], ch_in[:, 4:8], conv[:, 0:4]
        fsg, fh = xs, u_z
        ret_qk = conv[:, 6:10]
        ssq, rstd, ssq_half = small[:, 0:2], small[:, 2:4], small[:, 136:140]
        hs, hr = small[:, 4:12], small[:, 12:20]
        dA = small[:, 20:28]
        e_tok, nb_tok = small[:, 28:36], small[:, 36:44]
        em, den, rden = small[:, 44:52], small[:, 52:60], small[:, 60:68]
        negm = small[:, 68:76]
        r_tmp, r_in = small[:, 76:84], small[:, 84:86]
        g0 = gates[:, 0].rearrange("p t d -> p (t d)")
        router = g1[:, 0:64].rearrange("p (k e) -> p k e", k=KD)
        logit, one1, one2, both = (g1[:, 64 + 16 * n:80 + 16 * n].rearrange("p (t e) -> p t e", t=T) for n in range(4))
        eq, at_, tmp16 = (g1[:, 128 + 16 * n:144 + 16 * n].rearrange("p (t e) -> p t e", t=T) for n in range(3))
        m1, m2, kx, ex = (g1[:, 176 + 2 * n:178 + 2 * n] for n in range(4))
        n_tiles, p_end, p_start, zero8 = (g1[:, 184 + 8 * n:192 + 8 * n] for n in range(4))
        quad = g1[:, 216:224].rearrange("p (q t) -> p q t", q=4)
        e_cmp = g1[:, 224:224 + MAXPASS * NE].rearrange("p (n e) -> p n e", n=MAXPASS)
        e_tab = g1[:, 312:312 + MAXPASS + 1]
        slot_no = g1[:, 324:325]
        diag = g1[:, 384:384 + 8 * P].rearrange("p (q t i) -> p q t i", q=4, t=T)
        quad_b = g0[:, 0:4 * S].rearrange("p (q s) -> p q s", q=4)
        sel = g0[:, 4 * S:5 * S].rearrange("p (t s) -> p t s", t=T)
        selT = g0[:, 5 * S:6 * S]
        sel_tmp = g0[:, 6 * S:7 * S]
        xg_hi, xg_lo = hT_hi[:, :, 0:P], hT_lo[:, :, 0:P]
        ys = merged[:, 1]

        cst2 = cst[:, cat["retdecay"][0]:cat["retdecay"][0] + cvals2.shape[1]]
        assert cat["retdecay"][0] + cvals2.shape[1] <= cat["levmask"][1] == cvals.shape[1]

        def const2(name):
            lo, hi = cat2[name]
            return cst2[:, lo:hi]

        cos2 = const2("cos2").rearrange("p (t c) -> p t c", t=T)
        sin2 = const2("sin2").rearrange("p (t c) -> p t c", t=T)
        window = const2("window").rearrange("p (g i) -> p g i", g=4)
        lat = u_ret[:, :, 0:416]
        pool_in, sgu_u = u_ret[:, :, 512:768], u_ret[:, :, 768:1024]
        sgu_v = u_gla[:, :, 0:MW]
        k_rot = u_gla[:, :, MW:MW + ROPE]
        cqT, ckvT = ch_in[:, 6:8], ch_in[:, 8]
        conv_b, conv_c, conv_x, convT = ch_in[:, 0:2], ch_in[:, 2:4], ch_in[:, 4:6], conv[:, 0:2]
        qT = conv[0:NOPE + ROPE, 2:10]
        kT = ring[0:NOPE + ROPE, 0, KD * 512:KD * 512 + AH * S].rearrange("p (h s) -> p h s", h=AH)
        v_tok = u_ml[:, :, 0:512]
        q_rope, rope_c, rope_s, q_rot = xs, u_z, xdt, y
        pooled = xdt
        xn_flat = xn[:].rearrange("p t d -> p (t d)")
        probsT = xn_flat[:, 0:4 * 384].rearrange("p (h n) -> p h n", h=4)
        sgu_w = xn_flat[:, 4 * 384:2048].rearrange("p (g j) -> p g j", g=4)
        sgu_wT = scratch[:].rearrange("p (g i) -> p g i", g=4)
        pool_w = soft[:].rearrange("p t n -> p (t n)")[:, 0:P].rearrange("p (a d) -> p a d", a=2)
        poolT, sguT, attT = yT[:, 0], yT[:, 1], ch_in[:, 0:4]
        y_sgu = u_gla[:, :, 0:MW]
        y_att = u_ret[:, :, 0:512]
        mx, nmx, sums, rsum = (small[:, 88 + 8 * n:96 + 8 * n] for n in range(4))
        lat_s, lat_m, lat_r = small[:, 120:126], small[:, 126:130], small[:, 130:134]

        pb = [ctx.enter_context(nc.psum_tensor(f"pb{n}", [P, 512], F32)) for n in range(4)]
        mb = [ctx.enter_context(nc.psum_tensor(f"mb{n}", [P, 512], F32)) for n in range(4)]

        filled, act_emptied, dve_emptied = sem("pb_filled"), sem("pb_act_emptied"), sem("pb_dve_emptied")
        arrived = [sem(f"w_arrived{n}") for n in range(NSLOT)]
        params_in, x_in, gain_in, ygain_in = sem("params_in"), [sem(f"x_in{i}") for i in range(T)], sem("gain_in"), sem("ygain_in")
        stored = sem("stored")
        dve_step = sem("dve_step")
        squares, xn_ready = sem("squares"), sem("xn_ready")
        rows_turned, perch_ready, ea_ready = sem("rows_turned"), sem("perch_ready"), sem("ea_ready")
        x_ready = sem("x_ready")
        ident_in, tables_in, first_gain_in, rstd_ready = sem("ident_in"), sem("tables_in"), sem("first_gain_in"), sem("rstd_ready")
        pre_gain_in, ffn_gain_in = sem("pre_gain_in"), [sem(f"ffn_gain_in{k}") for k in range(2)]
        conv_raw, conv_ready = sem("conv_raw"), sem("conv_ready")
        alpha_mm, sp_abs, sp_exp, soft_ready = sem("alpha_mm"), sem("sp_abs"), sem("sp_exp"), sem("soft_ready")
        cums_mm, g_ready, e_ready, xs_mm, xdt_ready = (sem(s) for s in ("cums_mm", "g_ready", "e_ready", "xs_mm", "xdt_ready"))
        wseg_ready, seg_mm, seg_exp = sem("wseg_ready"), sem("seg_mm"), sem("seg_exp")
        scores_mm, probs_ready, pv_mm, o_read, y_ready = (sem(s) for s in ("scores_mm", "probs_ready", "pv_mm", "o_read", "y_ready"))
        et_mm, mt_ready, mbc_mm, ml_arg, ml_exp, em_ready, negm_ready = (sem(s) for s in (
            "et_mm", "mt_ready", "mbc_mm", "ml_arg", "ml_exp", "em_ready", "negm_ready"))
        rot_ready, qkt_mm, qkt_ready = sem("rot_ready"), sem("qkt_mm"), sem("qkt_ready")
        gla_arg, gla_exp, gla_kq, gla_mm, gla_put = (sem(s) for s in ("gla_arg", "gla_exp", "gla_kq", "gla_mm", "gla_put"))
        merged_ready = sem("merged_ready")
        gu_mm, silu_done, h_ready, ht_mm, ht_hi, ht_ready = (sem(s) for s in (
            "gu_mm", "silu_done", "h_ready", "ht_mm", "ht_hi", "ht_ready"))
        w_hi_ready, w_split, w_used, hT_split = (sem(s) for s in ("w_hi_ready", "w_split", "w_used", "hT_split"))
        e_hi_ready, e_split, e_used, xg_hi_ready = (sem(s) for s in ("e_hi_ready", "e_split", "e_used", "xg_hi_ready"))

        router_in, logits_mm, ex_arg, ex_ready = sem("router_in"), sem("logits_mm"), sem("ex_arg"), sem("ex_ready")
        both_ready, rank_mm, diag_ready, quad_mm, table_ready = (sem(s) for s in (
            "both_ready", "rank_mm", "diag_ready", "quad_mm", "table_ready"))
        sel_ready, gather_mm, xg_ready, selT_ready, scatter_mm, ys_ready = (sem(s) for s in (
            "sel_ready", "gather_mm", "xg_ready", "selT_ready", "scatter_mm", "ys_ready"))
        e_arrived = [sem(f"e_arrived{n}") for n in range(NSLOT)]
        e_silu, e_h, e_ht_mm, e_ht_hi, e_ht = (sem(s) for s in ("e_silu", "e_h", "e_ht_mm", "e_ht_hi", "e_ht"))
        zero_ready, moe_mm, sel_step = sem("zero_ready"), sem("moe_mm"), sem("sel_step")

        def step_loads(c):
            return 2 * (c < NF) + (c > 0)

        def e_landed(t, c):
            mine = range(c % NSLOT, NF + 1, NSLOT)
            return t * (16 * sum(step_loads(n) for n in mine)) + 16 * sum(step_loads(n) for n in mine if n <= c)

        cst2_in, sgu_in, pool_in_sem = sem("cst2_in"), sem("sgu_in"), sem("pool_in")
        lat_ready, latT_mm, latT_ready, qn_mm, qn_ready, kn_mm, kn_ready, qrv_mm, qrv_ready, q_rot_ready, qrT_mm, qrT_ready = (sem(s) for s in (
            "lat_ready", "latT_mm", "latT_ready", "qn_mm", "qn_ready", "kn_mm", "kn_ready", "qrv_mm", "qrv_ready", "q_rot_ready", "qrT_mm", "qrT_ready"))
        pooled_mm, pooled_ready, poolT_mm, poolT_ready, convT_ready = (sem(s) for s in (
            "pooled_mm", "pooled_ready", "poolT_mm", "poolT_ready", "convT_ready"))
        sgu_turned, sgu_wT_ready, vn_ready, sgu_mm, y_sgu_ready = (sem(s) for s in (
            "sgu_turned", "sgu_wT_ready", "vn_ready", "sgu_mm", "y_sgu_ready"))
        att_mm, att_max, att_exp, probsT_mm, probsT_ready, av_mm, y_att_ready = (sem(s) for s in (
            "att_mm", "att_max", "att_exp", "probsT_mm", "probsT_ready", "av_mm", "y_att_ready"))
        BK = []
        base = (0, 0, 0)
        for L in range(2):
            BK.append(Banks(bank_jobs1(), *base, 0))
            base = BK[-1].end
        for L in range(2):
            BK.append(Banks(bank_jobs2(), *base, 0))
            base = BK[-1].end

        items, find = [], {}
        uses = [0] * NSLOT

        def add_item(key, loads, free):
            s = sum(i != "experts" for i in items) % NSLOT
            uses[s] += 16 * len(loads)
            find[key] = (s, uses[s])
            items.append((s, loads, free))

        def cols(w, lo, n, at=0):
            return (at, w[:, lo:lo + n].rearrange("(k p) n -> p k n", p=P))

        u_key = []

        def ffn_items(u, key, w1, w3, w2):
            u_key.append(key)
            for c in range(NF + 1):
                loads = []
                if c < NF:
                    loads += [("gu", 0, w1[:, c * FC:(c + 1) * FC].rearrange("(k p) n -> p k n", p=P)),
                              ("gu", 1, w3[:, c * FC:(c + 1) * FC].rearrange("(k p) n -> p k n", p=P))]
                if c > 0:
                    loads += [("down", 0, w2[(c - 1) * FC:c * FC, :].rearrange("(k p) n -> p k n", p=P))]
                add_item((key, c), loads, (w_split, u * ALL_PIECES + (pieces(c + 1) if c < NF else ALL_PIECES)))

        def slot_view(s, load):
            kind = load[0]
            if kind == "gu":
                v = ring[:, s, 0:KD * 2 * FC].rearrange("p (k g n) -> p k g n", k=KD, g=2)
                return v[:, :, load[1]]
            if kind == "down":
                return ring[:, s, KD * 2 * FC:SLOTW].rearrange("p (k n) -> p k n", k=2)
            k, n = load[2].shape[1:]
            return ring[:, s, load[1]:load[1] + k * n].rearrange("p (k n) -> p k n", k=k)

        for L in range(2):
            B = BK[L]
            w_in = a["w_in"][L]
            for c, (lo, n, js) in enumerate(CHUNKS1):
                add_item((L, "proj", c), [("cols", 0, w_in[:, lo:lo + n].rearrange("(k p) n -> p k n", p=P))],
                         (filled, B.filled(("proj", c, len(js) - 1))))

            def gate_items(b):
                for h in range(2):
                    lo = GATE1 + BR_ORDER[b] * D + h * 512
                    add_item((L, "gate", b, h), [("cols", 0, w_in[:, lo:lo + 512].rearrange("(k p) n -> p k n", p=P))],
                             (filled, B.filled(("gate", b, h, 1))))

            def branch_item(b):
                add_item((L, "branch", b), [("cols", 0, a["w_branch"][L, BR_ORDER[b]].rearrange("(k p) n -> p k n", p=P))],
                         (filled, B.filled(("merge", b, 1, 1))))

            gate_items(0); gate_items(1); branch_item(0); gate_items(2); branch_item(1); gate_items(3)
            branch_item(2); branch_item(3)
            for h in range(2):
                add_item((L, "wout", h), [("cols", 0, a["w_out"][L][:, h * 512:h * 512 + 512].rearrange("(k p) n -> p k n", p=P))],
                         (filled, B.filled(("wout", h, 1))))
            if L == 0:
                ffn_items(0, (0, "ffn"), a["ffn_w1"][0], a["ffn_w3"][0], a["ffn_w2"][0])
            else:
                items.append("experts")

        def by_k(src):
            return ("cols", 0, src.rearrange("(k p) n -> p k n", p=P))

        for l in range(2):
            L = 2 + l
            B = BK[L]
            w_in = a["w_in_2"][l]
            for c, (lo, n, js) in enumerate(CHUNKS2):
                add_item((L, "proj", c), [by_k(w_in[:, lo:lo + n])], (filled, B.filled(("proj", c, len(js) - 1))))

            def gates2(b, *hs_):
                for h in hs_:
                    lo = GATE2 + BR_ORDER2[b] * D + h * 512
                    add_item((L, "gate", b, h), [by_k(w_in[:, lo:lo + 512])], (filled, B.filled(("gate", b, h, 1))))

            def branch2(b):
                w = a["w_br_" + "abcd"[BR_ORDER2[b]] + "_2"][l]
                add_item((L, "branch", b), [by_k(w)], (filled, B.filled(("merge", b, 1, 1))))

            gates2(0, 0)
            heads = lambda w: w.rearrange("p (h c) -> p h c", h=AH)
            up = []
            for k in range(2):
                uq = heads(a["w_uq_2"][l][k * P:(k + 1) * P, :])
                up += [("cols", UP_QN + k * AH * NOPE, uq[:, :, 0:NOPE]), ("cols", UP_QR + k * AH * ROPE, uq[:, :, NOPE:])]
            ukv = heads(a["w_ukv_2"][l])
            up += [("cols", UP_KN, ukv[:, :, 0:NOPE]), ("cols", UP_V, ukv[:, :, NOPE:])]
            add_item((L, "up"), up, (qrv_mm, l + 1))
            gates2(0, 1); gates2(1, 0); branch2(0); gates2(1, 1); branch2(1); gates2(2, 0, 1); branch2(2)
            gates2(3, 0, 1); branch2(3)
            for h in range(2):
                add_item((L, "wout", h), [by_k(a["w_out_2"][l][:, h * 512:h * 512 + 512])], (filled, B.filled(("wout", h, 1))))
            ffn_items(1 + l, (L, "ffn"), a["w_ffn_gate_2"][l], a["w_ffn_up_2"][l], a["w_ffn_down_2"][l])

        def place_free(n):
            return n - NPIECE + 1 if n >= NPIECE else max(m for m in range(ALL_PIECES) if m % NPIECE == n) - ALL_PIECES + 1

        def slot_split(c):
            return pieces(c + 1) if c < NF else ALL_PIECES

        GAINS = [(gain[:], first_gain_in, 16, None)]
        GAINS += [(gain[:], gain_in, 16 * n, n - 1) for n in range(1, 5)]
        GAINS += [(merged[:, 0], pre_gain_in, 16, None)]
        for l in range(2):
            if l:
                GAINS.append((gain[:], gain_in, 16 * 6, 6))
            GAINS.append((gain[:], gain_in, 16 * (5 + 2 * l), 4 + 5 * l))
            GAINS += [(gates[:, 1, k], ffn_gain_in[k], 16 * (l + 1), None) for k in range(2)]

        block = ctx.enter_context(nc.Block())

        def passes(eng):
            eng.wait_ge(table_ready, 1)
            return eng.value_load(table[0:1, MAXPASS:MAXPASS + 1], min_val=1, max_val=MAXPASS)

        def expert_weights(sp):
            n_pass = passes(sp)
            with sp.Fori(0, n_pass) as t:
                e = sp.value_load(table[0:1, bass.ds(t, 1)], min_val=0, max_val=NE - 1)
                for c in range(NF + 1):
                    s = c % NSLOT
                    sp.wait_ge(e_split, t * ALL_PIECES + (ALL_PIECES + slot_split(c - NSLOT) if c >= NSLOT else slot_split(NF + 1 - NSLOT + c)))
                    srcs = []
                    if c < NF:
                        for g_, w_ in enumerate((a["moe_w1"], a["moe_w3"])):
                            srcs.append((("gu", g_), w_[0, bass.ds(e, 1), :, c * FC:(c + 1) * FC].rearrange("o (k p) n -> p (o k) n", p=P)))
                    if c:
                        srcs.append((("down", 0), a["moe_w2"][0, bass.ds(e, 1), (c - 1) * FC:c * FC, :].rearrange("o (k p) n -> p (o k) n", p=P)))
                    for load, src in srcs:
                        sp.dma_start(slot_view(s, load), src).then_inc(e_arrived[s], 16)
            sp.wait_ge(e_split, n_pass * ALL_PIECES + ALL_PIECES)

        LAST_NORM = 4 + 4 * 2

        @block.sync
        def _(sp):
            for i in range(T):
                sp.dma_start(x[:, i], a["x"][0, i * P:(i + 1) * P, :]).then_inc(x_in[i], 16)
            last = [None] * NSLOT
            for item in items:
                if item == "experts":
                    for s in range(NSLOT):
                        sp.wait_ge(*last[s])
                    expert_weights(sp)
                    last = [None] * NSLOT
                    continue
                s, loads, free = item
                if last[s] is not None:
                    sp.wait_ge(*last[s])
                for load in loads:
                    sp.dma_start(slot_view(s, load), load[2]).then_inc(arrived[s], 16)
                last[s] = free
            for i in range(T):
                sp.wait_ge(xn_ready, T * LAST_NORM + i + 1)
                sp.dma_start(out[0, i * P:(i + 1) * P, :], x[:, i]).then_inc(stored, 16)
            sp.wait_ge(stored, 16 * T)

        @block.gpsimd
        def _(pool):
            pool.memset(rows[:], 0.0).then_inc(ea_ready, 1)
            pool.wait_ge(ea_ready, 1)
            for L in range(2):
                o = 50 * L
                pool.dma_start(rows[o:o + 24, :], a["ssd_conv_w"][L].rearrange("k (b c) -> (k b) c", c=P)).then_inc(params_in, 16)
                pool.dma_start(rows[o + 24:o + 30, :], a["ssd_conv_b"][L].rearrange("(b c) -> b c", c=P)).then_inc(params_in, 16)
                pool.dma_start(rows[o + 30:o + 46, :], a["ml_conv_w"][L].rearrange("k (b c) -> (k b) c", c=P)).then_inc(params_in, 16)
                pool.dma_start(rows[o + 46:o + 50, :], a["ml_conv_b"][L].rearrange("(b c) -> b c", c=P)).then_inc(params_in, 16)
            for l in range(2):
                o = 100 + 12 * l
                pool.dma_start(rows[o:o + 6, :], a["conv_w_2"][l].rearrange("k o (b c) -> (k o b) c", c=P)).then_inc(params_in, 16)
                pool.dma_start(rows[o + 6:o + 8, :], a["pool_scale_2"][l].rearrange("(b c) -> b c", c=P)).then_inc(params_in, 16)
                pool.dma_start(rows[o + 8:o + 12, :], a["sgu_b_2"][l]).then_inc(params_in, 16)
            off = 0
            for name, n in (("ssd_dt_bias", 4), ("ssd_a_log", 4), ("ssd_d", 4), ("ml_b_i", 4), ("ml_b_f", 4), ("gla_b_alpha", P)):
                pool.dma_start(bc[:, :, off:off + n], a[name].partition_broadcast(P)).then_inc(params_in, 16)
                off += n
            pool.dma_start(alpha_w[:], a["gla_w_alpha"].rearrange("l r n -> r l n")).then_inc(params_in, 16)

            def load_gain(n, src):
                place, landed, _, former = GAINS[n]
                if former is not None:
                    pool.wait_ge(xn_ready, T * (former + 1))
                pool.dma_start(place, src.partition_broadcast(P)).then_inc(landed, 16)

            for L in range(2):
                if L:
                    load_gain(2 * L, a["mix_norm_g"][L])
                    pool.wait_ge(y_ready, 4 * L)
                for n, name in enumerate(("ret_norm_g", "ssd_norm_g", "gla_norm_g", "ml_norm_g")):
                    pool.dma_start(ygain[:, n * MW:(n + 1) * MW], a[name][L].partition_broadcast(P)).then_inc(ygain_in, 16)
                load_gain(2 * L + 1, a["ffn_norm_g"][L])
            pool.wait_ge(merged_ready, 2)
            pool.dma_start(router, a["router_w"][0].rearrange("(k p) e -> p k e", p=P)).then_inc(router_in, 16)
            load_gain(4, a["final_norm_g"])
            pool.wait_ge(filled, BK[1].filled(("turn", 7)))
            load_gain(5, a["g_pre_mix_2"][0])
            pool.wait_ge(gla_put, 10)
            pool.dma_start(cst2, cdram2[:, :]).then_inc(cst2_in, 16)
            for l in range(2):
                L, n = 2 + l, 5 + 4 * l
                if l:
                    load_gain(n, a["g_pre_mix_2"][l])
                load_gain(n + 1, a["g_post_mix_2"][l])
                pool.wait_ge(merged_ready, 2 + l)
                for lo, w, name in ((0, MW, "g_cq_2"), (MW, P, "g_ckv_2"), (MW + P, MW, "g_sgu_v_2")):
                    pool.dma_start(ygain[:, lo:lo + w], a[name][l].partition_broadcast(P)).then_inc(ygain_in, 16)
                for aa in range(2):
                    for b_ in range(2):
                        pool.dma_start(pool_w[64 * b_:64 * b_ + 64, aa, :], a["pool_w_2"][l, 2 * aa + b_]).then_inc(pool_in_sem, 16)
                pool.wait_ge(filled, BK[L].filled(("turn", 3)))
                pool.dma_start(sgu_w, a["sgu_w_2"][l].rearrange("g i j -> i g j")).then_inc(sgu_in, 16)
                pool.wait_ge(merged_ready, L + 1)
                load_gain(n + 2, a["g_pre_ffn_2"][l])
                load_gain(n + 3, a["g_post_ffn_2"][l])
        PARAMS_ALL = 16 * (8 + 6 + 6 + 1)


        @block.tensor
        def _(pe):
            mm, turn = nc.tensor.matmul, nc.tensor.transpose

            def weights(key):
                s, v = find[key]
                pe.wait_ge(arrived[s], v)
                return ring[:, s]

            def open_bank(B, job):
                n = B.index[job]
                if n >= 4:
                    who, v = B.emptied(B.jobs[n - 4])
                    pe.wait_ge(act_emptied if who == "act" else dve_emptied, v)
                return pb[n % 4]

            def turn_jobs(B, first, src, ready):
                for k in range(4):
                    bank = open_bank(B, ("turn", first + k))
                    for i in range(T):
                        pe.wait_ge(*ready(i))
                    for kk in range(2):
                        for i in range(T):
                            ins = turn(bank[:, kk * S + i * P:kk * S + (i + 1) * P],
                                       src[:, i, (2 * k + kk) * P:(2 * k + kk + 1) * P], ident)
                    ins.then_inc(filled, 1)

            def proj_job(B, job, w, chunk_lo, width, spec):
                bank = open_bank(B, job)
                wv = w[:, 0:KD * width].rearrange("p (k n) -> p k n", k=KD)
                if spec[0] == "ch":
                    for n, (col, m) in enumerate(spec[1]):
                        for k in range(KD):
                            ins = mm(bank[0:m, n * S:(n + 1) * S], wv[:, k, col - chunk_lo:col - chunk_lo + m], hT[:, k, :],
                                     start=k == 0, stop=k == KD - 1)
                elif spec[0] == "tok":
                    _, i, col, m = spec
                    for k in range(KD):
                        ins = mm(bank[:, 0:m], hT[:, k, i * P:(i + 1) * P], wv[:, k, col - chunk_lo:col - chunk_lo + m],
                                 start=k == 0, stop=k == KD - 1)
                else:
                    i = spec[1]
                    for lo, col, m in ((0, SDT, 4), (4, GV, MW)):
                        for k in range(KD):
                            ins = mm(bank[:, lo:lo + m], hT[:, k, i * P:(i + 1) * P], wv[:, k, col - chunk_lo:col - chunk_lo + m],
                                     start=k == 0, stop=k == KD - 1)
                ins.then_inc(filled, 1)

            def acted(B, job):
                who, v = B.emptied(job)
                pe.wait_ge(act_emptied if who == "act" else dve_emptied, v)

            def chunk(L, c):
                lo, n, js = CHUNKS1[c]
                w = weights((L, "proj", c))
                for j, spec in enumerate(js):
                    proj_job(BK[L], ("proj", c, j), w, lo, n, spec)

            def gate(L, b, h, i):
                w = weights((L, "gate", b, h))
                proj_job(BK[L], ("gate", b, h, i), w, 0, 512, ("tok", i, 0, 512))

            def merge(L, b):
                bank = open_bank(BK[L], ("yturn", b))
                pe.wait_ge(y_ready, 4 * L + b + 1)
                for kk in range(2):
                    for i in range(T):
                        ins = turn(bank[:, kk * S + i * P:kk * S + (i + 1) * P], y[:, i, kk * P:(kk + 1) * P], ident)
                ins.then_inc(filled, 1)
                w = weights((L, "branch", b))[:, 0:2 * D].rearrange("p (k n) -> p k n", k=2)
                acted(BK[L], ("yturn", b))
                for h in range(2):
                    for i in range(T):
                        bank = open_bank(BK[L], ("merge", b, h, i))
                        for kk in range(2):
                            ins = mm(bank[:], yT[:, b % 2, kk, i * P:(i + 1) * P], w[:, kk, h * 512:(h + 1) * 512],
                                     start=kk == 0, stop=kk == 1)
                        ins.then_inc(filled, 1)

            def score_head(bank, kT, qT):
                mm(bank[:, 0:S], kT[:, 0:P], qT, start=True, stop=True)
                return mm(bank[:, S:S + P], kT[:, P:S], qT[:, P:S], start=True, stop=True)

            def weigh_values(banks, v, w=64, extra=None):
                for i in range(T):
                    for h in range(NH):
                        parts = [(0, i * P)] + ([(1, S)] if i else [])
                        for n, (j, at) in enumerate(parts):
                            ins = mm(banks[i][:, h * w:(h + 1) * w], probs[:, h, at:at + P], v(j, h),
                                     start=n == 0, stop=n == len(parts) - 1)
                        if extra is not None:
                            for n, (j, at) in enumerate(parts):
                                ins = mm(banks[i][:, extra + h:extra + h + 1], probs[:, h, at:at + P], ones[:, 0:1],
                                         start=n == 0, stop=n == len(parts) - 1)
                ins.then_inc(pv_mm, 1)

            def mixers(L):
                B = BK[L]
                acted(B, ("proj", 2, 1))
                if L:
                    pe.wait_ge(gla_put, 5 * L)
                for i in range(T):
                    ins = mm(mb[0][:, i * P:(i + 1) * P], ch_in[0:RANK, 12, i * P:(i + 1) * P], alpha_w[:, L, :],
                             start=True, stop=True)
                ins.then_inc(alpha_mm, 1)
                chunk(L, 6)
                chunk(L, 7)
                pe.wait_ge(soft_ready, L + 1)
                for i in range(T):
                    for j in range(i + 1):
                        mm(mb[0][:, i * P:(i + 1) * P], soft[:, j, 8:136], tri if j == i else ones, start=j == 0, stop=j == i)
                for i in range(T):
                    for j in range(i + 1):
                        ins = mm(mb[0][:, S + 4 * i:S + 4 * i + 4], tri if j == i else ones, soft[:, j, 4:8], start=j == 0, stop=j == i)
                ins.then_inc(cums_mm, 1)
                pe.wait_ge(conv_ready, 2 * L + 1)
                for kk in range(2):
                    for i in range(T):
                        ins = turn(mb[1][:, i * MW + kk * P:i * MW + (kk + 1) * P], conv[:, kk, i * P:(i + 1) * P], ident)
                ins.then_inc(xs_mm, 1)
                gate(L, 0, 0, 0)
                gate(L, 0, 0, 1)
                pe.wait_ge(wseg_ready, L + 1)
                pe.wait_ge(g_ready, L + 1)
                pe.wait_ge(e_ready, L + 1)
                pe.wait_ge(xdt_ready, L + 1)
                for h in range(NH):
                    m = mb[h]
                    mm(m[:, 0:P], w_seg[:, h, 0], tri, start=True, stop=False)
                    mm(m[:, 0:P], ident, const("negmask"), start=False, stop=True)
                    mm(m[:, P:S], w_seg[:, h, 0], ones, start=True, stop=False)
                    mm(m[:, P:S], w_one[:, h], tri, start=False, stop=True)
                    mm(m[:, S:S + P], w_seg[:, h, 1], tri, start=True, stop=False)
                    mm(m[:, S:S + P], ident, const("negmask"), start=False, stop=True).then_inc(seg_mm, 1)
                gate(L, 0, 1, 0)
                pe.wait_ge(seg_exp, 4 * (L + 1))
                for i in range(T):
                    ins = turn(mb[3][0:NH, i * P:(i + 1) * P], e_tok[:, 4 * i:4 * i + 4], ident)
                ins.then_inc(et_mm, 1)
                for g in range(2):
                    ins = score_head(mb[g], conv[:, 2 + g, :], conv[:, 4 + g, :])
                ins.then_inc(scores_mm, 1)
                gate(L, 0, 1, 1)
                pe.wait_ge(mt_ready, L + 1)
                pe.wait_ge(probs_ready, 3 * L + 1)
                weigh_values(mb[2:4], lambda j, h: xdt[:, j, h * 64:(h + 1) * 64])
                gate(L, 1, 0, 0)
                pe.wait_ge(o_read, 4 * L + 1)
                for h in range(NH):
                    m = mb[h]
                    mt = mrow[:, 1]
                    mm(m[:, 0:P], head_sel[0:NH, h], mt[:, 0:P], start=True, stop=False)
                    mm(m[:, 0:P], ident, const("bigmask"), start=False, stop=True)
                    mm(m[:, P:S], head_sel[0:NH, h], mt[:, P:S], start=True, stop=True)
                    mm(m[:, S:S + P], head_sel[0:NH, h], mt[:, P:S], start=True, stop=False)
                    ins = mm(m[:, S:S + P], ident, const("bigmask"), start=False, stop=True)
                    if h == 0:
                        for i in range(T):
                            ins = turn(m[:, 384 + 4 * i:388 + 4 * i], mt[:, i * P:(i + 1) * P], ident[0:NH, 0:NH])
                    ins.then_inc(mbc_mm, 1)
                gate(L, 1, 0, 1)
                pe.wait_ge(ml_arg, 4 * (L + 1))
                pe.wait_ge(conv_ready, 2 * L + 2)
                for h in range(NH):
                    r = 64 * (h % 2)
                    ins = score_head(mb[h], conv[r:r + 64, 8 + h // 2, :], conv[r:r + 64, 6 + h // 2, :])
                ins.then_inc(scores_mm, 1)
                gate(L, 1, 1, 0)
                pe.wait_ge(probs_ready, 3 * L + 2)
                weigh_values(mb[0:2], lambda j, h: u_ml[:, j, h * 64:(h + 1) * 64], extra=MW)
                pe.wait_ge(rot_ready, L + 1)
                for n in range(4):
                    for i in range(T):
                        ins = turn(mb[2 + n // 2][:, (n % 2) * S + i * P:(n % 2) * S + (i + 1) * P],
                                   u_ret[:, i, n * P:(n + 1) * P], ident)
                ins.then_inc(qkt_mm, 1)
                gate(L, 1, 1, 1)
                merge(L, 0)
                pe.wait_ge(qkt_ready, L + 1)
                pe.wait_ge(o_read, 4 * L + 2)
                for h in range(NH):
                    r = 64 * (h % 2)
                    ins = score_head(mb[h], ret_qk[r:r + 64, 2 + h // 2, :], ret_qk[r:r + 64, h // 2, :])
                ins.then_inc(scores_mm, 1)
                gate(L, 2, 0, 0)
                gate(L, 2, 0, 1)
                pe.wait_ge(probs_ready, 3 * L + 3)
                weigh_values(mb[0:2], lambda j, h: u_ret[:, j, 512 + h * 64:512 + (h + 1) * 64])
                gate(L, 2, 1, 0)
                gate(L, 2, 1, 1)
                merge(L, 1)
                pe.wait_ge(o_read, 4 * L + 3)
                for rnd in range(5):
                    if rnd in (0, 2):
                        pe.wait_ge(gla_kq, 2 * L + rnd // 2 + 1)
                    if rnd:
                        pe.wait_ge(gla_put, 5 * L + rnd)
                    for h in range(NH):
                        r = slice(32 * h, 32 * h + 32)
                        if rnd < 4:
                            for s_ in range(2):
                                lev = 2 * rnd + s_
                                for i in range(T):
                                    t_ = slice(i * P, (i + 1) * P)
                                    kk, qq = (gla_k[r, lev % 4, t_], gla_q[r, lev % 4, t_]) if lev < 7 else (
                                        ch_in[r, 11, t_], ch_in[r, 10, t_])
                                    ins = mm(mb[h][:, s_ * S + i * P:s_ * S + (i + 1) * P], kk, qq, start=True, stop=True,
                                             tile_position=(32 * h, 0))
                        else:
                            ins = mm(mb[h][:, 0:P], gla_k[r, 3, 0:P], gla_q[r, 3, P:S], start=True, stop=True,
                                     tile_position=(32 * h, 0))
                    ins.then_inc(gla_mm, 1)
                    if rnd < 4:
                        gate(L, 3, rnd // 2, rnd % 2)
                merge(L, 2)
                pe.wait_ge(gla_put, 5 * L + 5)
                weigh_values(mb[0:2], lambda j, h: u_gla[:, j, 4 + h * 64:4 + (h + 1) * 64])
                merge(L, 3)

            def split_product(o, a_hi, a_lo, n, cols, start, stop):
                hi, lo = w_hi[:, n % NPIECE, cols], w_lo[:, n % NPIECE, cols]
                mm(o, a_hi, hi, start=start, stop=False)
                mm(o, a_lo, hi, start=False, stop=False)
                return mm(o, a_hi, lo, start=False, stop=stop)

            def ffn(u):
                for c in range(NF + 1):
                    g = u * NF + c
                    if c:
                        for i in range(T):
                            pe.wait_ge(h_ready, T * g - T + i + 1)
                        for kk in range(2):
                            for i in range(T):
                                ins = turn(mb[2][:, kk * S + i * P:kk * S + (i + 1) * P], fh[:, i, kk * P:(kk + 1) * P], ident)
                        ins.then_inc(ht_mm, 1)
                    for n, (pc, q) in enumerate(PIECE_LIST):
                        if pc != c:
                            continue
                        if c == 0:
                            pe.wait_ge(hT_split, 4 * u + q + 1)
                        if q == GU_PIECES:
                            pe.wait_ge(ht_ready, g)
                        pe.wait_ge(w_split, u * ALL_PIECES + n + 1)
                        m = n + u * ALL_PIECES
                        for i in range(T):
                            it = slice(i * P, (i + 1) * P)
                            if q < GU_PIECES:
                                for kk in range(2):
                                    k = 2 * q + kk
                                    ins = split_product(mb[i][:], hT_hi[:, k, it], hT_lo[:, k, it], m,
                                                        slice(kk * 512, (kk + 1) * 512), k == 0, k == KD - 1)
                                if q == GU_PIECES - 1 and i == 0:
                                    ins.then_inc(gu_mm, 1)
                            else:
                                kk = q - GU_PIECES
                                for h in range(2):
                                    ins = split_product(pb[2 * i + h][:], fhT_hi[:, kk, it], fhT_lo[:, kk, it], m,
                                                        slice(h * 512, (h + 1) * 512), c == 1 and kk == 0, c == NF and kk == 1)
                        ins.then_inc(w_used, 1)

            def experts():
                pe.wait_ge(router_in, 16)
                for i in range(T):
                    for k in range(KD):
                        ins = mm(mb[0][:, NE * i:NE * i + NE], hT[:, k, i * P:(i + 1) * P], router[:, k], start=k == 0, stop=k == KD - 1)
                ins.then_inc(logits_mm, 1)
                pe.wait_ge(both_ready, 1)
                mm(mb[1][:, 0:NE], tri, both[:, 0], start=True, stop=True)
                for lo, l0, l1 in ((NE, ones, tri), (2 * NE, ones, ones)):
                    mm(mb[1][:, lo:lo + NE], l0, both[:, 0], start=True, stop=False)
                    ins = mm(mb[1][:, lo:lo + NE], l1, both[:, 1], start=False, stop=True)
                ins.then_inc(rank_mm, 1)
                pe.wait_ge(diag_ready, 1)
                for q in range(4):
                    for i in range(T):
                        ins = mm(mb[2 + q // 2][:, (q % 2) * S + i * P:(q % 2) * S + (i + 1) * P], ones, diag[:, q, i], start=True, stop=True)
                ins.then_inc(quad_mm, 1)
                pe.wait_ge(zero_ready, 1)
                for n in range(4):
                    ins = mm(pb[n][:], ident, scratch[:], start=True, stop=False, skip_group_check=True)
                    if n == 2:
                        ins.then_inc(scatter_mm, 1)
                    if n == 3:
                        ins.then_inc(e_used, NPIECE)

                def gather():
                    for k in range(KD):
                        for i in range(T):
                            ins = mm(mb[3 - k // 4][:, (k % 4) * P:(k % 4 + 1) * P], xn[:, i, k * P:(k + 1) * P], sel[:, i],
                                     start=i == 0, stop=i == T - 1)
                    ins.then_inc(gather_mm, 1)

                pe.wait_ge(sel_ready, 1)
                gather()
                n_pass = passes(pe)
                with pe.Fori(0, n_pass) as t:
                    pe.wait_ge(xg_ready, t + 1)
                    for n, (c, q) in enumerate(PIECE_LIST):
                        if c and n == pieces(c):
                            pe.wait_ge(e_h, t * NF + c)
                            for kk in range(2):
                                ins = turn(mb[3][:, kk * P:(kk + 1) * P], fh[:, 0, kk * P:(kk + 1) * P], ident)
                            ins.then_inc(e_ht_mm, 1)
                        if q == GU_PIECES:
                            pe.wait_ge(e_ht, t * NF + c)
                        pe.wait_ge(e_split, t * ALL_PIECES + ALL_PIECES + n + 1)
                        if q < GU_PIECES:
                            for kk in range(2):
                                k = 2 * q + kk
                                ins = split_product(mb[2][:], xg_hi[:, k], xg_lo[:, k], n, slice(kk * 512, (kk + 1) * 512),
                                                    k == 0, k == KD - 1)
                        else:
                            kk = q - GU_PIECES
                            for h in range(2):
                                ins = split_product(mb[h][:], fhT_hi[:, kk, 0:P], fhT_lo[:, kk, 0:P], n,
                                                    slice(h * 512, (h + 1) * 512), c == 1 and kk == 0, c == NF and kk == 1)
                        ins.then_inc(e_used, 1)
                    pe.wait_ge(sel_ready, t + 2)
                    gather()
                    pe.wait_ge(ys_ready, 2 * t + 2)
                    pe.wait_ge(selT_ready, t + 1)
                    for i in range(T):
                        for h in range(2):
                            ins = mm(pb[2 * i + h][:], selT[:, i * P:(i + 1) * P], ys[:, h * 512:(h + 1) * 512], start=False,
                                     stop=False, skip_group_check=True)
                    ins.then_inc(scatter_mm, 1)
                for n in range(4):
                    ins = mm(pb[n][:], ident, scratch[:], start=False, stop=True, skip_group_check=True)
                ins.then_inc(moe_mm, 1)

            def gate2(L, b, *ns):
                for n in ns:
                    gate(L, b, n // 2, n % 2)

            def chunk2(L, c):
                lo, n, js = CHUNKS2[c]
                w = weights((L, "proj", c))
                for j, spec in enumerate(js):
                    proj_job(BK[L], ("proj", c, j), w, lo, n, spec)

            def merge2(L, b, src, n_k):
                w = weights((L, "branch", b))[:, 0:n_k * D].rearrange("p (k n) -> p k n", k=n_k)
                for h in range(2):
                    for i in range(T):
                        bank = open_bank(BK[L], ("merge", b, h, i))
                        for kk in range(n_k):
                            ins = mm(bank[:], src[:, kk, i * P:(i + 1) * P], w[:, kk, h * 512:(h + 1) * 512],
                                     start=kk == 0, stop=kk == n_k - 1)
                        ins.then_inc(filled, 1)

            def y_turn(L, b, n, src):
                job = ("yturn", b, n)
                bank = open_bank(BK[L], job)
                for kk in range(2):
                    for i in range(T):
                        ins = turn(bank[:, kk * S + i * P:kk * S + (i + 1) * P], src[:, i, (2 * n + kk) * P:(2 * n + kk + 1) * P], ident)
                ins.then_inc(filled, 1)

            def scores2(l, g):
                for hh in range(4):
                    h = 4 * g + hh
                    for n, (i, j) in enumerate(((0, 0), (1, 0), (1, 1))):
                        o = mb[hh][:, n * P:(n + 1) * P]
                        it, jt = slice(i * P, (i + 1) * P), slice(j * P, (j + 1) * P)
                        ins = mm(o, qT[:, h, it], kT[:, h, jt], start=True, stop=i != j)
                        if i == j:
                            ins = mm(o, const2("rowmask")[0:1, :], const2("colmask")[0:1, :], start=False, stop=True)
                    ins.then_inc(att_mm, 1)

            def turn_probs(l, g):
                for hh in range(4):
                    pe.wait_ge(att_exp, 8 * (2 * l + g) + 2 * hh + 2)
                    for n in range(3):
                        ins = turn(mb[hh][:, n * P:(n + 1) * P], probs[:, hh, n * P:(n + 1) * P], ident)
                    ins.then_inc(probsT_mm, 1)

            def att_values(l, g):
                pe.wait_ge(probsT_ready, 2 * l + g + 1)
                for i in range(T):
                    for hh in range(4):
                        parts = [(0, i * P)] + ([(1, S)] if i else [])
                        for n, (j, at) in enumerate(parts):
                            ins = mm(mb[i][:, hh * VH:(hh + 1) * VH], probsT[:, hh, at:at + P],
                                     v_tok[:, j, (4 * g + hh) * VH:(4 * g + hh + 1) * VH], start=n == 0, stop=n == len(parts) - 1)
                ins.then_inc(av_mm, 1)

            def mixers2(l):
                L = 2 + l
                B = BK[L]
                chunk2(L, 0)
                chunk2(L, 1)
                if l == 0:
                    pe.wait_ge(cst2_in, 16)
                acted(B, ("proj", 1, 1))
                for g in range(4):
                    r = slice(64 * (g % 2), 64 * (g % 2) + 64)
                    c0 = (g // 2) * S
                    z = lambda j: pool_in[:, j, g * 64:(g + 1) * 64]
                    mm(mb[0][r, c0:c0 + P], z(0), window[:, g, 0:P], start=True, stop=True)
                    mm(mb[0][r, c0 + P:c0 + S], z(0), window[:, g, P:S], start=True, stop=False)
                    ins = mm(mb[0][r, c0 + P:c0 + S], z(1), window[:, g, S:384], start=False, stop=True)
                ins.then_inc(pooled_mm, 1)
                chunk2(L, 2)
                pe.wait_ge(lat_ready, l + 1)
                for kk in range(2):
                    for i in range(T):
                        turn(mb[1][:, kk * S + i * P:kk * S + (i + 1) * P], lat[:, i, kk * P:(kk + 1) * P], ident)
                for i in range(T):
                    turn(mb[2][:, i * P:(i + 1) * P], lat[:, i, MW:MW + P], ident)
                    ins = turn(mb[2][0:ROPE, S + i * P:S + (i + 1) * P], k_rot[:, i], ident)
                ins.then_inc(latT_mm, 1)
                pe.wait_ge(sgu_in, 16 * (l + 1))
                for g in range(4):
                    ins = turn(mb[3][:, g * P:(g + 1) * P], sgu_w[:, g], ident)
                ins.then_inc(sgu_turned, 1)
                chunk2(L, 3)
                pe.wait_ge(pooled_ready, l + 1)
                pe.wait_ge(pool_in_sem, 64 * (l + 1))
                for g in range(4):
                    r = slice(64 * (g % 2), 64 * (g % 2) + 64)
                    ins = mm(mb[0][r, (g // 2) * S:(g // 2 + 1) * S], pool_w[r, g // 2, :], pooled[r, g // 2, :], start=True, stop=True)
                ins.then_inc(poolT_mm, 1)
                gate2(L, 0, 0, 1)
                pe.wait_ge(latT_ready, l + 1)
                pe.wait_ge(poolT_ready, l + 1)
                pe.wait_ge(sgu_wT_ready, l + 1)
                w = weights((L, "up"))
                w_qn = w[:, UP_QN:UP_QR].rearrange("p (k n) -> p k n", k=2)
                w_qr = w[:, UP_QR:UP_KN].rearrange("p (k n) -> p k n", k=2)
                w_kn, w_v = w[:, UP_KN:UP_V], w[:, UP_V:UP_V + AH * VH]
                for h in range(AH):
                    for k in range(2):
                        ins = mm(mb[h // 2][0:NOPE, (h % 2) * S:(h % 2 + 1) * S], w_qn[:, k, h * NOPE:(h + 1) * NOPE], cqT[:, k],
                                 start=k == 0, stop=k == 1)
                ins.then_inc(qn_mm, 1)
                gate2(L, 0, 2)
                pe.wait_ge(qn_ready, l + 1)
                for h in range(AH):
                    ins = mm(mb[h // 2][0:NOPE, (h % 2) * S:(h % 2 + 1) * S], w_kn[:, h * NOPE:(h + 1) * NOPE], ckvT, start=True, stop=True)
                ins.then_inc(kn_mm, 1)
                gate2(L, 0, 3)
                pe.wait_ge(kn_ready, l + 1)
                for i in range(T):
                    for k in range(2):
                        mm(mb[0][:, i * S:(i + 1) * S], cqT[:, k, i * P:(i + 1) * P], w_qr[:, k], start=k == 0, stop=k == 1)
                    ins = mm(mb[1 + i][:], ckvT[:, i * P:(i + 1) * P], w_v, start=True, stop=True)
                ins.then_inc(qrv_mm, 1)
                pe.wait_ge(vn_ready, l + 1)
                for i in range(T):
                    for g in range(4):
                        ins = mm(mb[3][:, i * MW + g * 64:i * MW + (g + 1) * 64], sgu_wT[:, g], sgu_v[:, i, g * 64:(g + 1) * 64],
                                 start=True, stop=True)
                ins.then_inc(sgu_mm, 1)
                gate2(L, 1, 0, 1)
                pe.wait_ge(q_rot_ready, l + 1)
                for kk in range(2):
                    for i in range(T):
                        ins = turn(mb[0][:, kk * S + i * P:kk * S + (i + 1) * P], q_rot[:, i, kk * P:(kk + 1) * P], ident)
                ins.then_inc(qrT_mm, 1)
                pe.wait_ge(convT_ready, l + 1)
                merge2(L, 0, convT, 2)
                gate2(L, 1, 2)
                pe.wait_ge(qrT_ready, l + 1)
                pe.wait_ge(y_sgu_ready, l + 1)
                scores2(l, 0)
                gate2(L, 1, 3)
                merge2(L, 1, poolT, 2)
                turn_probs(l, 0)
                gate2(L, 2, 0)
                att_values(l, 0)
                gate2(L, 2, 1)
                pe.wait_ge(y_att_ready, 2 * l + 1)
                scores2(l, 1)
                gate2(L, 2, 2, 3)
                turn_probs(l, 1)
                y_turn(L, 2, 0, y_sgu)
                acted(B, ("yturn", 2, 0))
                merge2(L, 2, sguT, 2)
                gate2(L, 3, 0, 1)
                att_values(l, 1)
                gate2(L, 3, 2, 3)
                pe.wait_ge(y_att_ready, 2 * l + 2)
                y_turn(L, 3, 0, y_att)
                y_turn(L, 3, 1, y_att)
                acted(B, ("yturn", 3, 1))
                merge2(L, 3, attT, 4)

            pe.wait_ge(ident_in, 16)
            for L in range(2):
                B = BK[L]
                turn_jobs(B, 0, xn, lambda i: (xn_ready, 4 * L + i + 1))
                for k in range(4):
                    acted(B, ("turn", k))
                chunk(L, 0)
                if L == 0:
                    pe.wait_ge(params_in, PARAMS_ALL)
                    pe.wait_ge(tables_in, 16)
                    turn(mb[0][:, 0:P], rows[:], ident).then_inc(rows_turned, 1)
                for c in range(1, 6):
                    chunk(L, c)
                if L == 0:
                    pe.wait_ge(perch_ready, 1)
                mixers(L)
                turn_jobs(B, 4, merged, lambda i: (merged_ready, L + 1))
                for k in range(4):
                    acted(B, ("turn", 4 + k))
                for h in range(2):
                    w = weights((L, "wout", h))
                    for i in range(T):
                        proj_job(B, ("wout", h, i), w, 0, 512, ("tok", i, 0, 512))
                turn_jobs(B, 8, xn, lambda i: (xn_ready, 4 * L + 2 + i + 1))
                for k in range(4):
                    acted(B, ("turn", 8 + k))
                if L == 0:
                    ffn(0)
                else:
                    experts()
            for l in range(2):
                L, n = 2 + l, 5 + 4 * l
                B = BK[L]
                turn_jobs(B, 0, xn, lambda i: (xn_ready, T * n + i + 1))
                for k in range(4):
                    acted(B, ("turn", k))
                mixers2(l)
                turn_jobs(B, 4, merged, lambda i: (merged_ready, L + 1))
                for k in range(4):
                    acted(B, ("turn", 4 + k))
                for h in range(2):
                    w = weights((L, "wout", h))
                    for i in range(T):
                        proj_job(B, ("wout", h, i), w, 0, 512, ("tok", i, 0, 512))
                turn_jobs(B, 8, xn, lambda i: (xn_ready, T * (n + 2) + i + 1))
                for k in range(4):
                    acted(B, ("turn", 8 + k))
                ffn(1 + l)

        @block.scalar
        def _(act):
            f = nc.scalar.activation
            def square_sums(n, ready):
                if n:
                    act.wait_ge(xn_ready, T * n)
                for i in range(T):
                    act.wait_ge(*ready(i))
                    f(gates[:, 0, i, :], x[:, i, :], ACT.Square, accum_out=ssq[:, i:i + 1]).then_inc(squares, 1)

            def bank_squares(n, bank):
                act.wait_ge(xn_ready, T * n)
                for h in range(2):
                    for i in range(T):
                        src, ready = bank(h, i)
                        act.wait_ge(*ready)
                        ins = f(gates[:, 0, i, h * 512:(h + 1) * 512], src[:], ACT.Square, accum_out=ssq_half[:, 2 * h + i:2 * h + i + 1])
                        if h:
                            ins.then_inc(squares, 1)

            def empty(B, job, *moves):
                act.wait_ge(filled, B.filled(job))
                for dst, src, fn, sc in moves:
                    ins = f(dst, src, fn, scale=sc)
                ins.then_inc(act_emptied, 1)

            def turned(B, first, dst=hT):
                for k in range(4):
                    bank = pb[B.index[("turn", first + k)] % 4]
                    empty(B, ("turn", first + k), (dst[:, 2 * k:2 * k + 2, :].rearrange("p k s -> p (k s)"), bank[:], ACT.Copy, 1.0))

            def proj(L, c):
                B = BK[L]
                for j, spec in enumerate(CHUNKS1[c][2]):
                    job = ("proj", c, j)
                    bank = pb[B.index[job] % 4]
                    cp = lambda dst, src, fn=ACT.Copy, sc=1.0: (dst, src, fn, sc)
                    if spec[0] == "ch":
                        at = {SX: 0, SB: 2, SC: 4, MQ: 6, MK: 8}
                        col = spec[1][0][0]
                        if col in at:
                            empty(B, job, cp(ch_in[:, at[col]:at[col] + 2].rearrange("p b s -> p (b s)"), bank[:]))
                        elif col == GA:
                            empty(B, job, cp(ch_in[0:RANK, 12], bank[0:RANK, 0:S]))
                        else:
                            empty(B, job, cp(ch_in[:, 10], bank[:, 0:S], sc=32 ** -0.5), cp(ch_in[:, 11], bank[:, S:2 * S]))
                    elif spec[0] == "tok2":
                        i = spec[1]
                        empty(B, job, cp(u_gla[:, i, 0:4 + MW], bank[:, 0:4 + MW]))
                    else:
                        i, col = spec[1], spec[2]
                        if col == SZ:
                            empty(B, job, cp(u_z[:, i, :], bank[:, 0:MW], ACT.Silu))
                        elif col == GR:
                            empty(B, job, cp(u_gla[:, i, 4 + MW:], bank[:, 0:MW], ACT.Silu))
                        elif col == MV:
                            empty(B, job, cp(u_ml[:, i, 0:MW], bank[:, 0:MW]))
                        elif col == MO:
                            empty(B, job, cp(u_ml[:, i, MW:2 * MW], bank[:, 0:MW], ACT.Sigmoid),
                                  cp(u_ml[:, i, 2 * MW:], bank[:, MW:MW + 8]))
                        elif col == RQ:
                            empty(B, job, cp(u_ret[:, i, 0:512], bank[:, 0:512]))
                        else:
                            empty(B, job, cp(u_ret[:, i, 512:768], bank[:, 0:256]), cp(u_ret[:, i, 768:], bank[:, 256:512], ACT.Silu))

            def gate(L, b, h, i):
                job = ("gate", b, h, i)
                B = BK[L]
                if b >= 2:
                    act.wait_ge(dve_emptied, B.emptied(("merge", b - 2, 1, 1))[1])
                empty(B, job, (gates[:, b % 2, i, h * 512:(h + 1) * 512], pb[B.index[job] % 4][:], ACT.Sigmoid, 1.0))

            def yturned(L, b):
                job = ("yturn", b)
                B = BK[L]
                empty(B, job, (yT[:, b % 2].rearrange("p k s -> p (k s)"), pb[B.index[job] % 4][:], ACT.Copy, 1.0))

            def mixers(L):
                act.wait_ge(conv_raw, 2 * L + 1)
                f(conv[:, 0:6].rearrange("p b s -> p (b s)"), conv[:, 0:6].rearrange("p b s -> p (b s)"), ACT.Silu).then_inc(conv_ready, 1)
                proj(L, 3)
                act.wait_ge(conv_raw, 2 * L + 2)
                f(conv[:, 6:10].rearrange("p b s -> p (b s)"), conv[:, 6:10].rearrange("p b s -> p (b s)"), ACT.Silu).then_inc(conv_ready, 1)
                proj(L, 4)
                proj(L, 5)
                proj(L, 6)
                act.wait_ge(sp_abs, L + 1)
                f(sp_tmp[1], sp_tmp[0], ACT.Exp, scale=-1.0).then_inc(sp_exp, 1)
                proj(L, 7)
                act.wait_ge(cums_mm, L + 1)
                f(gT[:], mb[0][:, 0:S], ACT.Copy, scale=-1.0 / 16.0).then_inc(g_ready, 1)
                for h in range(NH):
                    act.wait_ge(seg_mm, 4 * L + h + 1)
                    if L and h == 0:
                        act.wait_ge(pv_mm, 4 * L)
                    f(probs[:, h, :], mb[h][:, 0:384], ACT.Exp).then_inc(seg_exp, 1)
                for h in range(2):
                    for i in range(T):
                        gate(L, 0, h, i)
                act.wait_ge(pv_mm, 4 * L + 1)
                for h in range(NH):
                    act.wait_ge(ml_arg, 4 * L + h + 1)
                    f(probs[:, h, :], probs[:, h, :], ACT.Exp, scale=-1.0).then_inc(ml_exp, 1)
                act.wait_ge(negm_ready, L + 1)
                f(em, negm, ACT.Exp).then_inc(em_ready, 1)
                gate(L, 1, 0, 0)
                gate(L, 1, 0, 1)
                gate(L, 1, 1, 0)
                act.wait_ge(qkt_mm, L + 1)
                for n in range(2):
                    ins = f(ret_qk[:, 2 * n:2 * n + 2].rearrange("p b s -> p (b s)"), mb[2 + n][:], ACT.Copy)
                ins.then_inc(qkt_ready, 1)
                gate(L, 1, 1, 1)
                yturned(L, 0)
                for h in range(2):
                    for i in range(T):
                        gate(L, 2, h, i)
                yturned(L, 1)
                for half in range(2):
                    act.wait_ge(gla_arg, 2 * L + half + 1)
                    f(gla_e.rearrange("p l s -> p (l s)"), gla_e.rearrange("p l s -> p (l s)"), ACT.Exp).then_inc(gla_exp, 1)
                    if half == 0:
                        gate(L, 3, 0, 0)
                        gate(L, 3, 0, 1)
                gate(L, 3, 1, 0)
                gate(L, 3, 1, 1)
                yturned(L, 2)
                yturned(L, 3)

            def high_parts(u, lo, hi):
                for n in range(lo, hi):
                    c, q = PIECE_LIST[n]
                    slot, landed = find[(u_key[u], c)]
                    if n in (lo, pieces(c)):
                        act.wait_ge(arrived[slot], landed)
                    m = u * ALL_PIECES + n
                    if m >= NPIECE:
                        act.wait_ge(w_used, m - NPIECE + 1)
                    f(w_hi[:, m % NPIECE], ring[:, slot, q * PIECE:(q + 1) * PIECE], ACT.Copy).then_inc(w_hi_ready, 1)

            def ffn(u):
                at = NPIECE
                for c in range(NF + 1):
                    g = u * NF + c
                    if c:
                        high_parts(u, at, min(pieces(c) + 3, ALL_PIECES))
                        at = min(pieces(c) + 3, ALL_PIECES)
                        act.wait_ge(ht_mm, g)
                        f(fhT_hi[:].rearrange("p k s -> p (k s)"), mb[2][:], ACT.Copy).then_inc(ht_hi, 1)
                    if c < NF:
                        high_parts(u, at, pieces(c + 1) + 1)
                        at = pieces(c + 1) + 1
                        if c == 0:
                            act.wait_ge(rstd_ready, u + 1)
                        for i in range(T):
                            if i == 0:
                                act.wait_ge(gu_mm, g + 1)
                            else:
                                act.wait_ge(w_used, u * ALL_PIECES + pieces(c) + GU_PIECES)
                            if g:
                                act.wait_ge(h_ready, T * (g - 1) + i + 1)
                            f(fsg[:, i, :], mb[i][:, 0:FC], ACT.Silu, scale=rstd[:, i:i + 1]).then_inc(silu_done, 1)
                assert at == ALL_PIECES

            def experts():
                act.wait_ge(ex_arg, 1)
                f(ex, ex, ACT.Exp).then_inc(ex_ready, 1)
                n_pass = passes(act)
                with act.Fori(0, n_pass) as t:
                    def high_parts(lo, hi):
                        for n in range(lo, hi):
                            c, q = PIECE_LIST[n]
                            if n == pieces(c):
                                act.wait_ge(e_arrived[c % NSLOT], e_landed(t, c))
                            act.wait_ge(e_used, t * ALL_PIECES + place_free(n) + NPIECE)
                            f(w_hi[:, n % NPIECE], ring[:, c % NSLOT, q * PIECE:(q + 1) * PIECE], ACT.Copy).then_inc(e_hi_ready, 1)

                    high_parts(0, 3)
                    at = 3
                    act.wait_ge(gather_mm, t + 1)
                    for n in range(2):
                        ins = f(xg_hi[:, 4 * n:4 * n + 4], mb[3 - n][:].rearrange("p (k s) -> p k s", k=4), ACT.Copy)
                    ins.then_inc(xg_hi_ready, 1)
                    for c in range(NF + 1):
                        if c:
                            high_parts(at, min(pieces(c) + 3, ALL_PIECES))
                            at = min(pieces(c) + 3, ALL_PIECES)
                            act.wait_ge(e_ht_mm, t * NF + c)
                            f(fhT_hi[:, :, 0:P], mb[3][:, 0:2 * P].rearrange("p (k s) -> p k s", k=2), ACT.Copy).then_inc(e_ht_hi, 1)
                        if c < NF:
                            high_parts(at, pieces(c + 1) + 1)
                            at = pieces(c + 1) + 1
                            act.wait_ge(e_used, t * ALL_PIECES + pieces(c) + GU_PIECES + NPIECE)
                            f(fsg[:, 0, :], mb[2][:, 0:FC], ACT.Silu).then_inc(e_silu, 1)
                    act.wait_ge(e_used, t * ALL_PIECES + ALL_PIECES + NPIECE)
                    f(ys[:, 0:512], mb[0][:], ACT.Copy).then_inc(ys_ready, 1)

            def evac2(L, c):
                B = BK[L]
                flat2 = lambda t_: t_.rearrange("p b s -> p (b s)")
                for j, spec in enumerate(CHUNKS2[c][2]):
                    job = ("proj", c, j)
                    bank = pb[B.index[job] % 4]
                    if spec[0] == "ch":
                        dst = {CB: conv_b, CC: conv_c, CX: conv_x}[spec[1][0][0]]
                        empty(B, job, (flat2(dst), bank[:], ACT.Copy, 1.0))
                    else:
                        i, col, w = spec[1:]
                        dst = {CQ: u_ret[:, i, 0:416], PI: u_ret[:, i, 512:1024], SV: sgu_v[:, i]}[col]
                        empty(B, job, (dst, bank[:, 0:w], ACT.Copy, 1.0))

            def gate2(L, b, *ns):
                B = BK[L]
                for n in ns:
                    job = ("gate", b, n // 2, n % 2)
                    if b >= 2:
                        act.wait_ge(dve_emptied, B.emptied(("merge", b - 2, 1, 1))[1])
                    empty(B, job, (gates[:, b % 2, n % 2, (n // 2) * 512:(n // 2 + 1) * 512], pb[B.index[job] % 4][:], ACT.Sigmoid, 1.0))

            def att_exps(l, g):
                for hh in range(4):
                    act.wait_ge(att_max, 4 * (2 * l + g) + hh + 1)
                    for i, (lo, hi) in enumerate(((0, P), (P, 384))):
                        c = 2 * hh + i
                        f(probs[:, hh, lo:hi], mb[hh][:, lo:hi], ACT.Exp, bias=nmx[:, c:c + 1], scale=(NOPE + ROPE) ** -0.5,
                          accum_out=sums[:, c:c + 1]).then_inc(att_exp, 1)

            def mixers2(l):
                L = 2 + l
                B = BK[L]
                evac2(L, 0)
                evac2(L, 1)
                act.wait_ge(pooled_mm, l + 1)
                f(pooled[:].rearrange("p t n -> p (t n)"), mb[0][:], ACT.Copy).then_inc(pooled_ready, 1)
                evac2(L, 2)
                act.wait_ge(latT_mm, l + 1)
                f(cqT.rearrange("p b s -> p (b s)"), mb[1][:], ACT.Copy)
                f(ckvT, mb[2][:, 0:S], ACT.Copy)
                f(kT[NOPE:NOPE + ROPE], mb[2][0:ROPE, S:2 * S].unsqueeze(1).to_broadcast([ROPE, AH, S]), ACT.Copy).then_inc(latT_ready, 1)
                evac2(L, 3)
                act.wait_ge(poolT_mm, l + 1)
                for aa in range(2):
                    o = 100 + 12 * l + 6 + aa
                    ins = f(poolT[:, aa], mb[0][:, aa * S:(aa + 1) * S], ACT.Copy, scale=perch[:, o:o + 1])
                ins.then_inc(poolT_ready, 1)
                gate2(L, 0, 0, 1)
                for done, ready, dst in ((qn_mm, qn_ready, qT), (kn_mm, kn_ready, kT)):
                    act.wait_ge(done, l + 1)
                    for n in range(4):
                        ins = f(dst[0:NOPE, 2 * n:2 * n + 2], mb[n][0:NOPE, :].rearrange("p (h s) -> p h s", h=2), ACT.Copy)
                    ins.then_inc(ready, 1)
                    gate2(L, 0, 2 if done is qn_mm else 3)
                act.wait_ge(qrv_mm, l + 1)
                f(q_rope[:].rearrange("p t n -> p (t n)"), mb[0][:], ACT.Copy)
                for i in range(T):
                    ins = f(v_tok[:, i], mb[1 + i][:], ACT.Copy)
                ins.then_inc(qrv_ready, 1)
                gate2(L, 1, 0, 1)
                act.wait_ge(qrT_mm, l + 1)
                for hh in range(4):
                    ins = f(qT[NOPE:NOPE + ROPE, hh:AH:4], mb[0][32 * hh:32 * hh + 32, :].rearrange("p (g s) -> p g s", g=2), ACT.Copy)
                ins.then_inc(qrT_ready, 1)
                gate2(L, 1, 2)
                att_exps(l, 0)
                gate2(L, 1, 3)
                gate2(L, 2, 0, 1)
                act.wait_ge(probsT_mm, 8 * l + 4)
                att_exps(l, 1)
                gate2(L, 2, 2, 3)
                job = ("yturn", 2, 0)
                empty(B, job, (sguT.rearrange("p k s -> p (k s)"), pb[B.index[job] % 4][:], ACT.Copy, 1.0))
                gate2(L, 3, 0, 1, 2, 3)
                for n in range(2):
                    job = ("yturn", 3, n)
                    empty(B, job, (attT[:, 2 * n:2 * n + 2].rearrange("p k s -> p (k s)"), pb[B.index[job] % 4][:], ACT.Copy, 1.0))

            act.dma_start(cst[:, 0:P], cdram[:, 0:P]).then_inc(ident_in, 16)
            act.dma_start(gain[:], a["mix_norm_g"][0].partition_broadcast(P)).then_inc(first_gain_in, 16)
            act.dma_start(cst[:, P:], cdram[:, P:]).then_inc(tables_in, 16)
            for L in range(2):
                square_sums(2 * L, lambda i: (x_in[i], 16) if L == 0 else (x_ready, i + 1))
                turned(BK[L], 0)
                proj(L, 0)
                if L == 0:
                    act.wait_ge(params_in, PARAMS_ALL)
                    f(ea[:], bc[:, :, 4:8], ACT.Exp).then_inc(ea_ready, 1)
                proj(L, 1)
                proj(L, 2)
                mixers(L)
                turned(BK[L], 4)
                if L == 0:
                    high_parts(0, 0, NPIECE)
                square_sums(2 * L + 1, lambda i: (dve_emptied, BK[L].emptied(("wout", 1, i))[1]))
                turned(BK[L], 8, hT_hi if L == 0 else hT)
                if L == 0:
                    ffn(0)
                else:
                    experts()
                    square_sums(4, lambda i: (x_ready, T + i + 1))
            for l in range(2):
                L, n = 2 + l, 5 + 4 * l
                square_sums(n, lambda i: (xn_ready, T * (n - 1) + i + 1))
                turned(BK[L], 0)
                mixers2(l)
                turned(BK[L], 4)
                high_parts(1 + l, 0, NPIECE)
                bank_squares(n + 1, lambda h, i: (pb[BK[L].index[("wout", h, i)] % 4], (filled, BK[L].filled(("wout", h, i)))))
                square_sums(n + 2, lambda i: (xn_ready, T * (n + 1) + i + 1))
                turned(BK[L], 8, hT_hi)
                ffn(1 + l)
                bank_squares(n + 3, lambda h, i: (pb[2 * i + h], (w_used, (2 + l) * ALL_PIECES)))

        @block.vector
        def _(v):
            tt, ts, stt, cp = nc.vector.tensor_tensor, nc.vector.tensor_scalar, nc.vector.scalar_tensor_tensor, nc.vector.tensor_copy
            chain = [0]

            def link(ins):
                chain[0] += 1
                ins.then_inc(dve_step, 1)
                v.wait_ge(dve_step, chain[0])

            def acted(B, job):
                v.wait_ge(act_emptied, B.emptied(job)[1])

            def rsqrt(r, m, done=None):
                t = r_tmp[:, 0:m.shape[1]]
                link(ts(r.bitcast(I32), m.bitcast(I32), 1, None, ALU.arith_shift_right))
                link(ts(r.bitcast(I32), r.bitcast(I32), -1.0, float(0x5F3759DF), ALU.mult, ALU.add))
                for step in range(3):
                    link(tt(t, r, r, ALU.mult))
                    link(stt(out=t, in0=t, scalar=-0.5, in1=m, op0=ALU.mult, op1=ALU.mult))
                    ins = stt(out=r, in0=t, scalar=1.5, in1=r, op0=ALU.add, op1=ALU.mult)
                    if step < 2 or done is None:
                        link(ins)
                    else:
                        ins.then_inc(done[0], 1)
                        v.wait_ge(*done)

            def gains_landed(n):
                place, landed, count, _ = GAINS[n]
                v.wait_ge(landed, count)
                return place

            def norm(n, dst=xn):
                v.wait_ge(squares, T * (n + 1))
                link(ts(r_in, ssq, 1.0 / D, EPS, ALU.mult, ALU.add))
                rsqrt(rstd, r_in)
                g = gains_landed(n)
                for i in range(T):
                    stt(out=dst[:, i, :], in0=x[:, i, :], scalar=rstd[:, i:i + 1], in1=g, op0=ALU.mult,
                        op1=ALU.mult).then_inc(xn_ready, 1)

            def convolve(L, first, count, wcol, bcol):
                for b in range(count):
                    blk, o = first + b, 50 * L
                    w = lambda k: perch[:, o + wcol + k * count + b:o + wcol + k * count + b + 1]
                    link(ts(conv[:, blk, :], ch_in[:, blk, :], w(3), perch[:, o + bcol + b:o + bcol + b + 1], ALU.mult, ALU.add))
                    for s in range(1, 4):
                        ins = stt(out=conv[:, blk, s:S], in0=ch_in[:, blk, 0:S - s], scalar=w(3 - s), in1=conv[:, blk, s:S],
                                  op0=ALU.mult, op1=ALU.add)
                        if s < 3:
                            link(ins)
                        elif b < count - 1:
                            link(ins)
                ins.then_inc(conv_raw, 1)

            def softplus(L):
                X = soft[:].rearrange("p t n -> p (t n)")
                b = bc[:, L]
                link(tt(soft[:, :, 0:4], u_gla[:, :, 0:4], b[:, 0:4].unsqueeze(1).to_broadcast([P, T, 4]), ALU.add))
                for lo, n, src, bias in ((4, 4, u_ml[:, :, 2 * MW + 4:2 * MW + 8], b[:, 16:20]),
                                         (8, P, mb[0][:, 0:S].rearrange("p (t n) -> p t n", t=T), b[:, 20:148])):
                    link(stt(out=soft[:, :, lo:lo + n], in0=src, scalar=-1.0, in1=bias.unsqueeze(1).to_broadcast([P, T, n]),
                             op0=ALU.mult, op1=ALU.subtract))
                stt(out=sp_tmp[0], in0=X, scalar=-1.0, in1=X, op0=ALU.mult, op1=ALU.max).then_inc(sp_abs, 1)
                v.wait_ge(sp_exp, L + 1)
                z, t2, s1, s2, q = sp_tmp[1], sp_tmp[2], sp_tmp[3], sp_tmp[4], sp_tmp[5]
                link(ts(t2, z, 2.0, None, ALU.add))
                link(nc.vector.reciprocal(t2, t2))
                link(tt(s1, z, t2, ALU.mult))
                link(tt(s2, s1, s1, ALU.mult))
                link(ts(q, s2, 1.0 / 15.0, None, ALU.mult))
                for d in (13, 11, 9, 7, 5, 3):
                    link(stt(out=q, in0=q, scalar=1.0 / d, in1=s2, op0=ALU.add, op1=ALU.mult))
                link(stt(out=q, in0=q, scalar=1.0, in1=s1, op0=ALU.add, op1=ALU.mult))
                link(ts(X, X, 0.0, None, ALU.max))
                stt(out=X, in0=q, scalar=2.0, in1=X, op0=ALU.mult, op1=ALU.add).then_inc(soft_ready, 1)
                v.wait_ge(soft_ready, L + 1)

            def head_norm(L, b, branch, act_gate, whole):
                n = 1 if whole else NH
                w = MW // n
                sq = scratch[:].rearrange("p (t n) -> p t n", t=T)
                link(tt(sq, y[:], y[:], ALU.mult))
                ss, rr = hs[:, 0:T * n], hr[:, 0:T * n]
                link(nc.vector.tensor_reduce(ss, scratch[:].rearrange("p (g w) -> p g w", w=w), AX.X, ALU.add))
                link(ts(ss, ss, 1.0 / w, EPS, ALU.mult, ALU.add))
                rsqrt(rr, ss)
                yv = y[:].rearrange("p t (h w) -> p (t h) w", h=n)
                link(tt(yv, yv, rr.unsqueeze(2).to_broadcast([P, T * n, w]), ALU.mult))
                v.wait_ge(ygain_in, 64 * (L + 1))
                gb = ygain[:, branch * MW:(branch + 1) * MW].unsqueeze(1).to_broadcast([P, T, MW])
                if act_gate is not None:
                    link(tt(y[:], y[:], gb, ALU.mult))
                    tt(y[:], y[:], act_gate, ALU.mult).then_inc(y_ready, 1)
                else:
                    tt(y[:], y[:], gb, ALU.mult).then_inc(y_ready, 1)
                v.wait_ge(y_ready, 4 * L + b + 1)

            def take_y(L, b):
                v.wait_ge(pv_mm, 4 * L + b + 1)
                if b:
                    v.wait_ge(filled, BK[L].filled(("yturn", b - 1)))

            def merge(L, b):
                B = BK[L]
                for h in range(2):
                    for i in range(T):
                        job = ("merge", b, h, i)
                        bank = pb[B.index[job] % 4]
                        g = gates[:, b % 2, i, h * 512:(h + 1) * 512]
                        m = merged[:, i, h * 512:(h + 1) * 512]
                        acted(B, ("gate", b, h, i))
                        v.wait_ge(filled, B.filled(job))
                        if b == 0:
                            tt(m, bank[:], g, ALU.mult).then_inc(dve_emptied, 1)
                        else:
                            tt(g, bank[:], g, ALU.mult).then_inc(dve_emptied, 1)
                        v.wait_ge(dve_emptied, B.emptied(job)[1])
                        if b:
                            ins = tt(m, m, g, ALU.add)
                            if (b, h, i) == (3, 1, 1):
                                ins.then_inc(merged_ready, 1)
                            else:
                                link(ins)

            def gla_levels(L, half):
                if half:
                    v.wait_ge(gla_mm, 5 * L + 2)
                for n in range(4):
                    b = 1 << (4 * half + n)
                    g = gT[:].rearrange("p (m s b) -> p m s b", s=2, b=b)
                    e = gla_e[:, n].rearrange("p (m s b) -> p m s b", s=2, b=b)
                    ref = g[:, :, 0, b - 1:b].to_broadcast([P, S // (2 * b), b])
                    tt(e[:, :, 0], ref, g[:, :, 0], ALU.subtract)
                    ins = tt(e[:, :, 1], g[:, :, 1], ref, ALU.subtract)
                ins.then_inc(gla_arg, 1)
                v.wait_ge(gla_exp, 2 * L + half + 1)
                tt(gla_k, gla_e, ch_in[:, 11:12].to_broadcast([P, 4, S]), ALU.mult)
                tt(gla_q, gla_e, ch_in[:, 10:11].to_broadcast([P, 4, S]), ALU.mult).then_inc(gla_kq, 1)

            def gla_put_levels(L, rnd):
                v.wait_ge(gla_mm, 5 * L + rnd + 1)
                for h in range(NH):
                    if rnd == 4:
                        ins = cp(probs[:, h, P:S], mb[h][:, 0:P])
                        continue
                    dst = probs[:, h, :].rearrange("p (a i) -> p a i", i=P)[:, 0:3:2, :]
                    for s_ in range(2):
                        src = mb[h][:, s_ * S:(s_ + 1) * S].rearrange("p (a i) -> p a i", i=P)
                        msk = levmask[:, 2 * rnd + s_].bitcast(U32).unsqueeze(1).to_broadcast([P, T, P])
                        ins = nc.vector.copy_predicated(dst, msk, src)
                        if not (h == NH - 1 and s_ == 1):
                            link(ins)
                ins.then_inc(gla_put, 1)
                v.wait_ge(gla_put, 5 * L + rnd + 1)

            def mixers(L):
                B = BK[L]
                acted(B, ("proj", 0, 0))
                acted(B, ("proj", 1, 1))
                if L:
                    v.wait_ge(pv_mm, 4 * L)
                convolve(L, 0, 6, 0, 24)
                acted(B, ("proj", 3, 0))
                convolve(L, 6, 4, 30, 46)
                acted(B, ("proj", 5, 1))
                v.wait_ge(alpha_mm, L + 1)
                softplus(L)
                v.wait_ge(ea_ready, 2)
                link(stt(out=dA.rearrange("p (t h) -> p t h", t=T), in0=soft[:, :, 0:4], scalar=-1.0,
                         in1=ea[:, L].unsqueeze(1).to_broadcast([P, T, 4]), op0=ALU.mult, op1=ALU.mult))
                dAh = dA.rearrange("p (t h) -> p h t", t=T)
                for t_ in range(T):
                    tt(w_seg[:, :, t_], after.unsqueeze(1).to_broadcast([P, NH, P]),
                       dAh[:, :, t_:t_ + 1].to_broadcast([P, NH, P]), ALU.mult)
                tt(w_one, ones.unsqueeze(1).to_broadcast([P, NH, P]), dAh[:, :, 1:2].to_broadcast([P, NH, P]),
                   ALU.mult).then_inc(wseg_ready, 1)
                acted(B, ("proj", 6, 1))
                for i in range(T):
                    u = u_ret[:, i, 0:512].rearrange("p (g h c) -> p g h c", g=8, h=2)
                    pc = rot_c[:, i].rearrange("p g (h c) -> p g h c", h=2)
                    ps_ = rot_s[:, i].rearrange("p g (h c) -> p g h c", h=2)
                    for h in range(2):
                        tt(pc[:, :, h], u[:, :, h], cosT[:, i].unsqueeze(1).to_broadcast([P, 8, 32]), ALU.mult)
                        link(tt(ps_[:, :, h], u[:, :, h], sinT[:, i].unsqueeze(1).to_broadcast([P, 8, 32]), ALU.mult))
                    tt(u[:, :, 0], pc[:, :, 0], ps_[:, :, 1], ALU.subtract)
                    ins = tt(u[:, :, 1], ps_[:, :, 0], pc[:, :, 1], ALU.add)
                ins.then_inc(rot_ready, 1)
                v.wait_ge(g_ready, L + 1)
                nb3, e3 = nb_tok.rearrange("p (t h) -> p t h", t=T), e_tok.rearrange("p (t h) -> p t h", t=T)
                link(cp(nb_tok, mb[0][:, S:S + 8]))
                link(tt(e3, u_ml[:, :, 2 * MW:2 * MW + 4], bc[:, L, 12:16].unsqueeze(1).to_broadcast([P, T, 4]), ALU.add))
                tt(e3, e3, nb3, ALU.add).then_inc(e_ready, 1)
                v.wait_ge(e_ready, L + 1)
                v.wait_ge(xs_mm, L + 1)
                link(cp(xs[:].rearrange("p t n -> p (t n)"), mb[1][:]))
                for i in range(T):
                    ins = tt(xdt[:, i].rearrange("p (h w) -> p h w", h=NH), xs[:, i].rearrange("p (h w) -> p h w", h=NH),
                             soft[:, i, 0:4].unsqueeze(2).to_broadcast([P, NH, 64]), ALU.mult)
                ins.then_inc(xdt_ready, 1)
                v.wait_ge(et_mm, L + 1)
                link(cp(mrow[:, 0], mb[3][0:NH, 0:S]))
                nc.vector.tensor_tensor_scan(mrow[:, 1], mrow[:, 0], mrow[:, 0], 0.0, ALU.max, ALU.max).then_inc(mt_ready, 1)
                v.wait_ge(scores_mm, 3 * L + 1)
                for h in range(NH):
                    v.wait_ge(seg_exp, 4 * L + h + 1)
                    ins = tt(probs[:, h, :], probs[:, h, :], mb[h // 2][:, 0:384], ALU.mult)
                ins.then_inc(probs_ready, 1)
                take_y(L, 0)
                for i in range(T):
                    link(tt(y[:, i].rearrange("p (h w) -> p h w", h=NH), xs[:, i].rearrange("p (h w) -> p h w", h=NH),
                            bc[:, L, 8:12].unsqueeze(2).to_broadcast([P, NH, 64]), ALU.mult))
                    ins = tt(y[:, i], y[:, i], mb[2 + i][:, 0:MW], ALU.add)
                    if i == 0:
                        link(ins)
                ins.then_inc(o_read, 1)
                v.wait_ge(o_read, 4 * L + 1)
                link(tt(y[:], y[:], u_z[:], ALU.mult))
                head_norm(L, 0, 1, None, True)
                for h in range(NH):
                    v.wait_ge(mbc_mm, 4 * L + h + 1)
                    if h == 0:
                        tt(negm, nb_tok, mb[0][:, 384:392], ALU.subtract).then_inc(negm_ready, 1)
                    ts(probs[:, h, 0:S], mb[h][:, 0:S], e_tok[:, h:h + 1], 0.0, ALU.subtract, ALU.max)
                    ts(probs[:, h, S:384], mb[h][:, S:384], e_tok[:, 4 + h:5 + h], 0.0, ALU.subtract, ALU.max).then_inc(ml_arg, 1)
                v.wait_ge(scores_mm, 3 * L + 2)
                for h in range(NH):
                    v.wait_ge(ml_exp, 4 * L + h + 1)
                    ins = stt(out=probs[:, h, :], in0=probs[:, h, :], scalar=64 ** -0.5, in1=mb[h][:, 0:384], op0=ALU.mult, op1=ALU.mult)
                ins.then_inc(probs_ready, 1)
                take_y(L, 1)
                v.wait_ge(em_ready, L + 1)
                for i in range(T):
                    link(cp(den[:, 4 * i:4 * i + 4], mb[i][:, MW:MW + 4]))
                link(stt(out=den, in0=den, scalar=-1.0, in1=den, op0=ALU.mult, op1=ALU.max))
                link(tt(den, den, em, ALU.max))
                link(nc.vector.reciprocal(rden, den))
                for i in range(T):
                    ins = tt(y[:, i].rearrange("p (h w) -> p h w", h=NH), mb[i][:, 0:MW].rearrange("p (h w) -> p h w", h=NH),
                             rden[:, 4 * i:4 * i + 4].unsqueeze(2).to_broadcast([P, NH, 64]), ALU.mult)
                ins.then_inc(o_read, 1)
                v.wait_ge(o_read, 4 * L + 2)
                head_norm(L, 1, 3, u_ml[:, :, MW:2 * MW], False)
                merge(L, 0)
                v.wait_ge(scores_mm, 3 * L + 3)
                v.wait_ge(pv_mm, 4 * L + 2)
                for h in range(NH):
                    tt(probs[:, h, 0:S], mb[h][:, 0:S], retdecay[:, h, 0:S], ALU.mult)
                    ins = tt(probs[:, h, S:384], mb[h][:, S:384], retdecay[:, h, 0:P], ALU.mult)
                ins.then_inc(probs_ready, 1)
                gla_levels(L, 0)
                take_y(L, 2)
                for i in range(T):
                    ins = cp(y[:, i], mb[i][:, 0:MW])
                ins.then_inc(o_read, 1)
                v.wait_ge(o_read, 4 * L + 3)
                head_norm(L, 2, 0, u_ret[:, :, 768:1024], False)
                merge(L, 1)
                v.wait_ge(pv_mm, 4 * L + 3)
                link(nc.vector.memset(probs[:].rearrange("p h n -> p (h n)"), 0.0))
                gla_put_levels(L, 0)
                gla_put_levels(L, 1)
                gla_levels(L, 1)
                gla_put_levels(L, 2)
                gla_put_levels(L, 3)
                gla_put_levels(L, 4)
                merge(L, 2)
                take_y(L, 3)
                for i in range(T):
                    ins = cp(y[:, i], mb[i][:, 0:MW])
                ins.then_inc(o_read, 1)
                v.wait_ge(o_read, 4 * L + 4)
                head_norm(L, 3, 2, u_gla[:, :, 4 + MW:], False)
                merge(L, 3)

            def normed(src, n_g, cols, gcol, m, r, w):
                for i in range(T):
                    ins = stt(out=src[:, i, cols], in0=src[:, i, cols], scalar=r[:, i:i + 1], in1=ygain[:, gcol:gcol + w],
                              op0=ALU.mult, op1=ALU.mult)
                return ins

            def rope(dst, src, c_, s_, n):
                for i in range(T):
                    sv = src(i)
                    pc = c_[:, i, 0:n * ROPE].rearrange("p (g h c) -> p g h c", g=n, h=2)
                    ps_ = s_[:, i, 0:n * ROPE].rearrange("p (g h c) -> p g h c", g=n, h=2)
                    for h in range(2):
                        tt(pc[:, :, h], sv[:, :, h], cos2[:, i].unsqueeze(1).to_broadcast([P, n, ROPE // 2]), ALU.mult)
                        link(tt(ps_[:, :, h], sv[:, :, h], sin2[:, i].unsqueeze(1).to_broadcast([P, n, ROPE // 2]), ALU.mult))
                    d = dst(i)
                    tt(d[:, :, 0], pc[:, :, 0], ps_[:, :, 1], ALU.subtract)
                    ins = tt(d[:, :, 1], pc[:, :, 1], ps_[:, :, 0], ALU.add)
                return ins

            def scale_by_gain(n):
                if n:
                    v.wait_ge(xn_ready, T * n)
                g = gains_landed(n)
                for i in range(T):
                    tt(xn[:, i, :], x[:, i, :], g, ALU.mult).then_inc(xn_ready, 1)

            def row_factors(n, u):
                v.wait_ge(squares, T * (n + 1))
                link(ts(r_in, ssq, 1.0 / D, EPS, ALU.mult, ALU.add))
                rsqrt(rstd, r_in, (rstd_ready, u + 1))

            def post_norm(n, bank, B=None):
                v.wait_ge(squares, T * (n + 1))
                link(tt(ssq, ssq_half[:, 0:2], ssq_half[:, 2:4], ALU.add))
                link(ts(r_in, ssq, 1.0 / D, EPS, ALU.mult, ALU.add))
                rsqrt(rstd, r_in)
                g = gains_landed(n)
                for h in range(2):
                    for i in range(T):
                        cs = slice(h * 512, (h + 1) * 512)
                        ins = stt(out=xn[:, i, cs], in0=bank(h, i)[:], scalar=rstd[:, i:i + 1], in1=g[:, cs], op0=ALU.mult,
                                  op1=ALU.mult)
                        if B is None:
                            link(ins)
                        else:
                            ins.then_inc(dve_emptied, 1)
                        if h:
                            if B is not None:
                                v.wait_ge(dve_emptied, B.emptied(("wout", 1, i))[1])
                            tt(x[:, i], x[:, i], xn[:, i], ALU.add).then_inc(xn_ready, 1)

            def merge2(L, b):
                B = BK[L]
                for h in range(2):
                    for i in range(T):
                        job = ("merge", b, h, i)
                        bank = pb[B.index[job] % 4]
                        g = gates[:, b % 2, i, h * 512:(h + 1) * 512]
                        m = merged[:, i, h * 512:(h + 1) * 512]
                        acted(B, ("gate", b, h, i))
                        v.wait_ge(filled, B.filled(job))
                        tt(m if b == 0 else g, bank[:], g, ALU.mult).then_inc(dve_emptied, 1)
                        v.wait_ge(dve_emptied, B.emptied(job)[1])
                        if b:
                            ins = tt(m, m, g, ALU.add)
                            if (b, h, i) == (3, 1, 1):
                                ins.then_inc(merged_ready, 1)
                            else:
                                link(ins)

            def att_maxima(l, g):
                for hh in range(4):
                    v.wait_ge(att_mm, 4 * (2 * l + g) + hh + 1)
                    if g or l:
                        v.wait_ge(att_exp, 8 * (2 * l + g))
                    for i, (lo, hi) in enumerate(((0, P), (P, 384))):
                        c = 2 * hh + i
                        link(nc.vector.tensor_reduce(mx[:, c:c + 1], mb[hh][:, lo:hi], AX.X, ALU.max))
                    ts(nmx[:, 2 * hh:2 * hh + 2], mx[:, 2 * hh:2 * hh + 2], -(NOPE + ROPE) ** -0.5, None, ALU.mult).then_inc(att_max, 1)

            def take_probsT(l, g):
                for hh in range(4):
                    v.wait_ge(probsT_mm, 4 * (2 * l + g) + hh + 1)
                    ins = cp(probsT[:, hh, :], mb[hh][:, 0:384])
                ins.then_inc(probsT_ready, 1)
                link(nc.vector.reciprocal(rsum, sums))

            def take_att(l, g):
                v.wait_ge(av_mm, 2 * l + g + 1)
                r3 = rsum.rearrange("p (h t) -> p t h", t=T)
                for i in range(T):
                    ins = tt(y_att[:, i, g * MW:(g + 1) * MW].rearrange("p (h w) -> p h w", h=4),
                             mb[i][:, 0:MW].rearrange("p (h w) -> p h w", h=4), r3[:, i].unsqueeze(2).to_broadcast([P, 4, VH]), ALU.mult)
                ins.then_inc(y_att_ready, 1)

            def mixers2(l):
                L = 2 + l
                B = BK[L]
                acted(B, ("proj", 0, 1))
                if l == 0:
                    v.wait_ge(cst2_in, 16)
                for i in range(T):
                    sq = u_z[:].rearrange("p t n -> p (t n)")[:, 0:384]
                    link(tt(sq, lat[:, i, 0:384], lat[:, i, 0:384], ALU.mult))
                    link(nc.vector.tensor_reduce(lat_s[:, 3 * i:3 * i + 3], sq.rearrange("p (g n) -> p g n", g=3), AX.X, ALU.add))
                s3 = lat_s.rearrange("p (t g) -> p t g", g=3)
                link(tt(lat_m[:, 0:2], s3[:, :, 0], s3[:, :, 1], ALU.add))
                link(ts(lat_m[:, 0:2], lat_m[:, 0:2], 1.0 / MW, EPS, ALU.mult, ALU.add))
                link(ts(lat_m[:, 2:4], s3[:, :, 2], 1.0 / P, EPS, ALU.mult, ALU.add))
                rsqrt(lat_r, lat_m)
                v.wait_ge(ygain_in, 16 * 8 + 48 * (l + 1))
                normed(lat, 2, slice(0, MW), 0, None, lat_r[:, 0:2], MW)
                normed(lat, 2, slice(MW, MW + P), MW, None, lat_r[:, 2:4], P)
                ins = (rope(lambda i: k_rot[:, i].rearrange("p (n h c) -> p n h c", n=1, h=2),
                          lambda i: lat[:, i, KR:KR + ROPE].rearrange("p (n h c) -> p n h c", n=1, h=2), rope_c, xs, 1))
                ins.then_inc(lat_ready, 1)
                v.wait_ge(lat_ready, l + 1)
                acted(B, ("proj", 2, 1))
                sq = u_z[:]
                link(tt(sq, sgu_v, sgu_v, ALU.mult))
                link(nc.vector.tensor_reduce(lat_m[:, 0:2], sq, AX.X, ALU.add))
                link(ts(lat_m[:, 0:2], lat_m[:, 0:2], 1.0 / MW, EPS, ALU.mult, ALU.add))
                rsqrt(lat_r[:, 0:2], lat_m[:, 0:2])
                normed(sgu_v, 2, slice(0, MW), MW + P, None, lat_r[:, 0:2], MW).then_inc(vn_ready, 1)
                v.wait_ge(sgu_turned, l + 1)
                link(cp(scratch[:], mb[3][:]))
                nc.vector.memset(sgu_wT[BLOCKED:P, :, 0:BLOCKED], 0.0).then_inc(sgu_wT_ready, 1)
                acted(B, ("proj", 3, 1))
                link(tt(conv_c, conv_c, conv_x, ALU.mult))
                for b in range(2):
                    o = 100 + 12 * l
                    w = lambda k: perch[:, o + 2 * k + b:o + 2 * k + b + 1]
                    link(ts(convT[:, b], conv_c[:, b], w(2), None, ALU.mult))
                    for s_ in (1, 2):
                        link(stt(out=convT[:, b, s_:S], in0=conv_c[:, b, 0:S - s_], scalar=w(2 - s_), in1=convT[:, b, s_:S],
                                 op0=ALU.mult, op1=ALU.add))
                tt(convT, convT, conv_b, ALU.mult).then_inc(convT_ready, 1)
                v.wait_ge(qrv_ready, l + 1)
                v.wait_ge(poolT_mm, l + 1)
                rope(lambda i: q_rot[:, i].rearrange("p (g h c) -> p g h c", g=AH, h=2),
                     lambda i: q_rope[:, i].rearrange("p (g h c) -> p g h c", g=AH, h=2), rope_c, rope_s, AH).then_inc(q_rot_ready, 1)
                v.wait_ge(sgu_mm, l + 1)
                for i in range(T):
                    for g in range(4):
                        o = 100 + 12 * l + 8 + g
                        cs = slice(g * 64, (g + 1) * 64)
                        ins = stt(out=y_sgu[:, i, cs], in0=mb[3][:, i * MW + g * 64:i * MW + (g + 1) * 64], scalar=perch[:, o:o + 1],
                                  in1=sgu_u[:, i, cs], op0=ALU.add, op1=ALU.mult)
                ins.then_inc(y_sgu_ready, 1)
                merge2(L, 0)
                att_maxima(l, 0)
                merge2(L, 1)
                take_probsT(l, 0)
                take_att(l, 0)
                att_maxima(l, 1)
                take_probsT(l, 1)
                merge2(L, 2)
                take_att(l, 1)
                merge2(L, 3)

            def add_out(L):
                B = BK[L]
                for h in range(2):
                    for i in range(T):
                        job = ("wout", h, i)
                        v.wait_ge(filled, B.filled(job))
                        xv = x[:, i, h * 512:(h + 1) * 512]
                        ins = tt(xv, xv, pb[B.index[job] % 4][:], ALU.add)
                        ins.then_inc(dve_emptied, 1)
                v.wait_ge(dve_emptied, B.emptied(("wout", 1, 1))[1])

            def low(dst, src, hi):
                return tt(dst, src, hi.bitcast(F32), ALU.subtract)

            def low_parts(u, lo, hi):
                for n in range(lo, hi):
                    c, q = PIECE_LIST[n]
                    m = u * ALL_PIECES + n
                    v.wait_ge(w_hi_ready, m + 1)
                    low(w_lo[:, m % NPIECE], ring[:, find[(u_key[u], c)][0], q * PIECE:(q + 1) * PIECE], w_hi[:, m % NPIECE]).then_inc(w_split, 1)

            def ffn(u):
                B = BK[(0, 2, 3)[u]]
                for k in range(4):
                    job = ("turn", 8 + k)
                    acted(B, job)
                    low(hT_lo[:, 2 * k:2 * k + 2].rearrange("p k s -> p (k s)"), pb[B.index[job] % 4][:],
                        hT_hi[:, 2 * k:2 * k + 2].rearrange("p k s -> p (k s)")).then_inc(hT_split, 1)
                row_factors((1, 7, 11)[u], u)
                at = NPIECE
                for c in range(NF + 1):
                    g = u * NF + c
                    if c:
                        low_parts(u, at, min(pieces(c) + 3, ALL_PIECES))
                        at = min(pieces(c) + 3, ALL_PIECES)
                        v.wait_ge(ht_hi, g)
                        low(fhT_lo[:].rearrange("p k s -> p (k s)"), mb[2][:], fhT_hi[:].rearrange("p k s -> p (k s)")).then_inc(ht_ready, 1)
                    if c < NF:
                        low_parts(u, at, pieces(c + 1) + 1)
                        at = pieces(c + 1) + 1
                        for i in range(T):
                            v.wait_ge(silu_done, T * g + i + 1)
                            if g:
                                v.wait_ge(ht_mm, g)
                            stt(out=fh[:, i, :], in0=mb[i][:, FC:2 * FC], scalar=rstd[:, i:i + 1], in1=fsg[:, i, :], op0=ALU.mult,
                                op1=ALU.mult).then_inc(h_ready, 1)
                v.wait_ge(w_used, (u + 1) * ALL_PIECES)
                if u == 0:
                    add_banks()

            def add_banks():
                for i in range(T):
                    for h in range(2):
                        xv = x[:, i, h * 512:(h + 1) * 512]
                        ins = tt(xv, xv, pb[2 * i + h][:], ALU.add)
                        if h == 0:
                            link(ins)
                    ins.then_inc(x_ready, 1)

            def route():
                v.wait_ge(logits_mm, 1)
                link(cp(logit.rearrange("p t e -> p (t e)"), mb[0][:, 0:2 * NE]))
                cp(slot_no, const("iotap")).then_inc(e_split, ALL_PIECES)
                v.wait_ge(e_split, ALL_PIECES)
                rk = const("rank8").unsqueeze(1).to_broadcast([P, T, NE])
                wide = lambda col: col.unsqueeze(2).to_broadcast([P, T, NE])
                for src, top, one in ((logit, m1, one1), (tmp16, m2, one2)):
                    link(nc.vector.tensor_reduce(top, src, AX.X, ALU.max))
                    link(tt(eq, src, wide(top), ALU.is_equal))
                    link(tt(eq, eq, rk, ALU.mult))
                    link(nc.vector.tensor_reduce(kx, eq, AX.X, ALU.max))
                    link(tt(one, rk, wide(kx), ALU.is_equal))
                    if src is logit:
                        link(stt(out=tmp16, in0=one1, scalar=NEG, in1=logit, op0=ALU.mult, op1=ALU.add))
                tt(ex, m2, m1, ALU.subtract).then_inc(ex_arg, 1)
                tt(both, one1, one2, ALU.add).then_inc(both_ready, 1)
                v.wait_ge(ex_ready, 1)
                w1, w2 = quad[:, 2], quad[:, 3]
                link(ts(w2, ex, 1.0, None, ALU.add))
                link(nc.vector.reciprocal(w1, w2))
                link(tt(w2, ex, w1, ALU.mult))
                v.wait_ge(rank_mm, 1)
                cnt = mb[1][:, 2 * NE:3 * NE]
                link(ts(zero8, cnt, 0.5, None, ALU.is_gt))
                link(stt(out=n_tiles, in0=cnt, scalar=P + 0.5, in1=zero8, op0=ALU.is_gt, op1=ALU.add))
                link(nc.vector.memset(zero8, 0.0))
                link(nc.vector.tensor_tensor_scan(p_end, n_tiles, zero8, 0.0, ALU.add, ALU.add))
                link(tt(e_cmp, p_end.unsqueeze(1).to_broadcast([P, MAXPASS, NE]),
                        const("passno").unsqueeze(2).to_broadcast([P, MAXPASS, NE]), ALU.is_le))
                link(nc.vector.tensor_reduce(e_tab[:, 0:MAXPASS], e_cmp, AX.X, ALU.add))
                link(ts(e_tab[:, 0:MAXPASS], e_tab[:, 0:MAXPASS], float(NE - 1), None, ALU.min))
                link(cp(e_tab[:, MAXPASS:], p_end[:, NE - 1:NE]))
                cp(table[:], e_tab[0:1, :]).then_inc(table_ready, 1)
                link(tt(p_start, p_end, n_tiles, ALU.subtract))
                link(ts(p_start, p_start, float(P), -1.0, ALU.mult, ALU.add))
                link(tt(at_, mb[1][:, 0:2 * NE].rearrange("p (t e) -> p t e", t=T), p_start.unsqueeze(1).to_broadcast([P, T, NE]), ALU.add))
                for q, one in enumerate((one1, one2)):
                    link(tt(eq, at_, one, ALU.mult))
                    link(nc.vector.tensor_reduce(quad[:, q], eq, AX.X, ALU.add))
                for q in range(4):
                    for i in range(T):
                        ins = ts(diag[:, q, i], ident, quad[:, q, i:i + 1], None, ALU.mult)
                ins.then_inc(diag_ready, 1)
                nc.vector.memset(scratch[:], 0.0).then_inc(zero_ready, 1)
                v.wait_ge(quad_mm, 1)
                for n in range(2):
                    link(cp(quad_b[:, 2 * n:2 * n + 2].rearrange("p q s -> p (q s)"), mb[2 + n][:]))

            def select_places(step):
                for i in range(T):
                    step(ts(sel[:, i], const("iota"), quad[:, 0, i:i + 1], None, ALU.is_equal))
                    ins = stt(out=sel[:, i], in0=const("iota"), scalar=quad[:, 1, i:i + 1], in1=sel[:, i], op0=ALU.is_equal, op1=ALU.add)
                    if i == 0:
                        step(ins)
                ins.then_inc(sel_ready, 1)

            def experts():
                route()
                select_places(link)
                n_pass = passes(v)
                with v.Fori(0, n_pass) as t:
                    n = [0]
                    STEPS = 7

                    def step(ins):
                        n[0] += 1
                        ins.then_inc(sel_step, 1)
                        v.wait_ge(sel_step, t * STEPS + n[0])

                    def low_parts(lo, hi):
                        for m in range(lo, hi):
                            c, q = PIECE_LIST[m]
                            v.wait_ge(e_hi_ready, t * ALL_PIECES + m + 1)
                            low(w_lo[:, m % NPIECE], ring[:, c % NSLOT, q * PIECE:(q + 1) * PIECE], w_hi[:, m % NPIECE]).then_inc(e_split, 1)

                    low_parts(0, 3)
                    at = 3
                    v.wait_ge(xg_hi_ready, t + 1)
                    for half in range(2):
                        ins = low(xg_lo[:, 4 * half:4 * half + 4], mb[3 - half][:].rearrange("p (k s) -> p k s", k=4),
                                  xg_hi[:, 4 * half:4 * half + 4])
                    ins.then_inc(xg_ready, 1)
                    v.wait_ge(scatter_mm, t + 1)
                    step(stt(out=selT, in0=quad_b[:, 0], scalar=slot_no, in1=quad_b[:, 2], op0=ALU.is_equal, op1=ALU.mult))
                    step(stt(out=sel_tmp, in0=quad_b[:, 1], scalar=slot_no, in1=quad_b[:, 3], op0=ALU.is_equal, op1=ALU.mult))
                    tt(selT, selT, sel_tmp, ALU.add).then_inc(selT_ready, 1)
                    v.wait_ge(selT_ready, t + 1)
                    step(ts(slot_no, slot_no, float(P), None, ALU.add))
                    for c in range(NF + 1):
                        if c:
                            low_parts(at, min(pieces(c) + 3, ALL_PIECES))
                            at = min(pieces(c) + 3, ALL_PIECES)
                            v.wait_ge(e_ht_hi, t * NF + c)
                            low(fhT_lo[:, :, 0:P], mb[3][:, 0:2 * P].rearrange("p (k s) -> p k s", k=2), fhT_hi[:, :, 0:P]).then_inc(e_ht, 1)
                        if c < NF:
                            low_parts(at, pieces(c + 1) + 1)
                            at = pieces(c + 1) + 1
                            v.wait_ge(e_silu, t * NF + c + 1)
                            tt(fh[:, 0, :], fsg[:, 0, :], mb[2][:, FC:2 * FC], ALU.mult).then_inc(e_h, 1)
                        if c == 0:
                            v.wait_ge(sel_ready, t + 1)
                            qv = quad[:, 0:2].rearrange("p q t -> p (q t)")
                            step(ts(qv, qv, -float(P), None, ALU.add))
                            select_places(step)
                    v.wait_ge(e_used, t * ALL_PIECES + ALL_PIECES + NPIECE)
                    cp(ys[:, 512:1024], mb[1][:]).then_inc(ys_ready, 1)
                assert n[0] == 7, n[0]
                v.wait_ge(moe_mm, 1)
                add_banks()

            for L in range(2):
                norm(2 * L)
                if L == 0:
                    v.wait_ge(rows_turned, 1)
                    cp(perch[:], mb[0][:, 0:P]).then_inc(perch_ready, 1)
                    v.wait_ge(perch_ready, 1)
                mixers(L)
                if L == 0:
                    low_parts(0, 0, NPIECE)
                add_out(L)
                if L == 0:
                    scale_by_gain(1)
                    ffn(0)
                else:
                    norm(3)
                    experts()
            norm(4, x)
            v.wait_ge(xn_ready, T * 5)
            for l in range(2):
                L, n = 2 + l, 5 + 4 * l
                norm(n)
                mixers2(l)
                low_parts(1 + l, 0, NPIECE)
                post_norm(n + 1, lambda h, i: pb[BK[L].index[("wout", h, i)] % 4], BK[L])
                scale_by_gain(n + 2)
                ffn(1 + l)
                post_norm(n + 3, lambda h, i: pb[2 * i + h])


INPUTS = ["x", "mix_norm_g", "w_in", "ret_norm_g", "ssd_conv_w", "ssd_conv_b", "ssd_dt_bias", "ssd_a_log", "ssd_d", "ssd_norm_g",
          "gla_w_alpha", "gla_b_alpha", "gla_norm_g", "ml_conv_w", "ml_conv_b", "ml_b_i", "ml_b_f", "ml_norm_g", "w_branch", "w_out",
          "ffn_norm_g", "ffn_w1", "ffn_w3", "ffn_w2", "router_w", "moe_w1", "moe_w3", "moe_w2", "final_norm_g",
          "w_in_2", "g_pre_mix_2", "g_cq_2", "g_ckv_2", "w_uq_2", "w_ukv_2", "pool_w_2", "pool_scale_2", "g_sgu_v_2", "sgu_w_2",
          "sgu_b_2", "conv_w_2", "w_br_a_2", "w_br_b_2", "w_br_c_2", "w_br_d_2", "w_out_2", "g_post_mix_2", "g_pre_ffn_2",
          "w_ffn_gate_2", "w_ffn_up_2", "w_ffn_down_2", "g_post_ffn_2"]


def kernel(**inputs):
    import numpy as _np
    import concourse.bacc as _bacc
    from concourse.bass_utils import run_bass_kernel_spmd as _run

    nc = _bacc.Bacc("TRN2", target_bir_lowering=False, num_devices=1)
    arrays, args = {}, {}
    for name in INPUTS:
        arr = _np.ascontiguousarray(inputs[name])
        arrays["in_" + name] = arr
        args[name] = nc.dram_tensor("in_" + name, arr.shape, mybir.dt.from_np(arr.dtype), kind="ExternalInput").ap()
    out = nc.dram_tensor("out", (1, S, D), F32, kind="ExternalOutput").ap()
    build(nc, args, out)
    return _run(nc, [arrays], core_ids=[0]).results[0]["out"]
```
